# Optimizing a Trainium2 kernel written in Bass

```python
import jax, jax.numpy as jnp
from jax import lax
import numpy as np

D_MODEL = 1024
BATCH = 1
SEQ = 256
DEPTH = 2
DEC_BATCH = 8
DEC_SEQ = 16
PAST_LEN = 128

CHUNK = 64
H_A = 4
DH_A = 64
H_B = 4
DK_B = 64
DV_B = 128
GATE_RANK = 16
GATE_TAU = 16.0
GLA_BLOCK = 64
H_C = 4
DH_C = 64
H_IDX = 4
D_IDX = 64
TOPK_MAX = 256
D_FF = 2816
SB_BLOCK = 128
DSA_BLOCK = 64
MACARON_W = 0.5
EPS = 1e-6
MIX_WIDTH = H_A * DH_A + H_B * DV_B + H_C * DH_C
IN_COLS = (H_A * DH_A, H_A * DH_A, H_A * DH_A,
           H_B * DK_B, H_B * DK_B, H_B * DV_B, H_B * DV_B, GATE_RANK,
           H_C * DH_C, DH_C, DH_C, H_IDX * D_IDX, D_IDX, H_IDX)
D_IN = sum(IN_COLS)
SPLIT_POINTS = tuple(int(v) for v in np.cumsum(IN_COLS)[:-1])

kernel_name = 'hybrid_stream_encoder_step'

def rms_norm(x, g):
    xf = x.astype(jnp.float32)
    y = xf * lax.rsqrt(jnp.mean(xf * xf, axis=-1, keepdims=True) + EPS)
    return (y * g.astype(jnp.float32)).astype(x.dtype)

def swiglu(h, w_up, w_down):
    gate, up = jnp.split(h @ w_up, 2, axis=-1)
    return (jax.nn.silu(gate) * up) @ w_down

def sweep_query_blocks(fn, qs, qpos, blk):
    B, T = qs[0].shape[:2]
    if T <= blk or T % blk:
        return fn(qs, qpos)
    nb = T // blk
    split = lambda a: jnp.moveaxis(a.reshape(B, nb, blk, *a.shape[2:]), 1, 0)
    out = lax.map(lambda args: fn(args[0], args[1]), (tuple(split(a) for a in qs), qpos.reshape(nb, blk)))
    return jnp.moveaxis(out, 0, 1).reshape(B, T, *out.shape[3:])

def stick_breaking_block(q, qpos, k, v, kpos):
    z = jnp.einsum('bqhd,blhd->bhql', q, k).astype(jnp.float32) * (DH_A ** -0.5)
    mask = kpos[None, :] < qpos[:, None]
    log_beta = jax.nn.log_sigmoid(z)
    log_keep = jnp.where(mask, jax.nn.log_sigmoid(-z), 0.0)
    cum = jnp.cumsum(log_keep, axis=-1)
    log_w = log_beta + cum[..., -1:] - cum
    w = jnp.where(mask, jnp.exp(log_w), 0.0)
    return jnp.einsum('bhql,blhd->bqhd', w.astype(v.dtype), v)

def dsa_block(qs, qpos, k, v, k_idx, kpos, n_sel):
    q, q_idx, w_idx = qs
    admissible = (kpos[None, :] // CHUNK) <= (qpos[:, None] // CHUNK)
    s = jnp.einsum('bqhd,bld->bqhl', q_idx, k_idx).astype(jnp.float32) * (D_IDX ** -0.5)
    score = jnp.einsum('bqh,bqhl->bql', w_idx.astype(jnp.float32), jax.nn.relu(s))
    score = jnp.where(admissible[None], score, -jnp.inf)
    _, idx = lax.top_k(score, n_sel)
    gather = jax.vmap(lambda rows, ids: rows[ids])
    k_sel = gather(k, idx)
    v_sel = gather(v, idx)
    valid = (kpos[idx] // CHUNK) <= (qpos[None, :, None] // CHUNK)
    logits = jnp.einsum('bqhd,bqnd->bqhn', q, k_sel).astype(jnp.float32) * (DH_C ** -0.5)
    logits = jnp.where(valid[:, :, None, :], logits, -jnp.inf)
    p = jax.nn.softmax(logits, axis=-1)
    return jnp.einsum('bqhn,bqnd->bqhd', p.astype(v.dtype), v_sel)

def gla_recurrence(q, k, v, log_a, s0, blk):
    B, T, H, _ = q.shape
    DV = v.shape[-1]
    if T % blk:
        blk = T
    nb = T // blk
    f32 = jnp.float32
    rs = lambda a: jnp.moveaxis(a.astype(f32).reshape(B, nb, blk, *a.shape[2:]), 1, 0)
    tri = jnp.tril(jnp.ones((blk, blk), bool))[None, :, :, None, None]

    def step(S, xs):
        qb, kb, vb, ab = xs
        b = jnp.cumsum(ab, axis=1)
        decay = jnp.exp(jnp.where(tri, b[:, :, None] - b[:, None, :], -jnp.inf))
        att = jnp.einsum('bthd,bshd,btshd->bhts', qb, kb, decay)
        o = jnp.einsum('bhts,bshv->bthv', att, vb) + jnp.einsum('bthd,bhdv->bthv', qb * jnp.exp(b), S)
        b_last = b[:, -1]
        S_new = jnp.exp(b_last)[..., None] * S + jnp.einsum('bshd,bshv->bhdv', kb * jnp.exp(b_last[:, None] - b), vb)
        return S_new, o

    s_fin, o = lax.scan(step, s0.astype(f32), (rs(q), rs(k), rs(v), rs(log_a)))
    return jnp.moveaxis(o, 0, 1).reshape(B, T, H, DV), s_fin.astype(s0.dtype)

def token_mixing(h, past_k_sb, past_v_sb, past_k_dsa, past_v_dsa, past_k_idx, gla_state,
                 w_in, w_gate, b_gate, g_gla, w_out):
    B, T, _ = h.shape
    P = past_k_sb.shape[1]
    (qa, ka, va, qb, kb, vb, rb, gb, qc, kc, vc, qi, ki, wi) = jnp.split(h @ w_in, SPLIT_POINTS, axis=-1)
    heads = lambda a, n: a.reshape(B, T, n, -1)
    kpos = jnp.arange(P + T, dtype=jnp.int32)
    qpos = P + jnp.arange(T, dtype=jnp.int32)
    ka, va = heads(ka, H_A), heads(va, H_A)
    k_all = jnp.concatenate([past_k_sb, ka], axis=1)
    v_all = jnp.concatenate([past_v_sb, va], axis=1)
    o_a = sweep_query_blocks(lambda qs, pos: stick_breaking_block(qs[0], pos, k_all, v_all, kpos),
                             (heads(qa, H_A),), qpos, SB_BLOCK)
    log_a = jax.nn.log_sigmoid((gb @ w_gate + b_gate).astype(jnp.float32)) / GATE_TAU
    o_b, s_new = gla_recurrence(heads(qb, H_B) * (DK_B ** -0.5), heads(kb, H_B), heads(vb, H_B),
                                heads(log_a, H_B), gla_state, GLA_BLOCK)
    o_b = rms_norm(o_b, g_gla.reshape(H_B, DV_B)).reshape(B, T, -1).astype(h.dtype) * jax.nn.silu(rb)
    kc_all = jnp.concatenate([past_k_dsa, kc], axis=1)
    vc_all = jnp.concatenate([past_v_dsa, vc], axis=1)
    ki_all = jnp.concatenate([past_k_idx, ki], axis=1)
    n_sel = min(TOPK_MAX, (P + T) // 4)
    o_c = sweep_query_blocks(lambda qs, pos: dsa_block(qs, pos, kc_all, vc_all, ki_all, kpos, n_sel),
                             (heads(qc, H_C), heads(qi, H_IDX), wi * (H_IDX ** -0.5)), qpos, DSA_BLOCK)
    o = jnp.concatenate([o_a.reshape(B, T, -1), o_b, o_c.reshape(B, T, -1)], axis=-1)
    return o @ w_out, (ka, va, kc, vc, ki, s_new)

def encoder_layer(x, c, past_k_sb, past_v_sb, past_k_dsa, past_v_dsa, past_k_idx, gla_state,
                  w_ada, b_ada, gains, w_f1_in, w_f1_out, w_f2_in, w_f2_out, w_in, w_gate, b_gate, g_gla, w_out):
    mod = jax.nn.silu(c) @ w_ada + b_ada
    sh1, sc1, ga1, sh2, sc2, ga2, sh3, sc3, ga3 = [m[:, None, :] for m in jnp.split(mod, 9, axis=-1)]
    h = rms_norm(x, gains[0]) * (1 + sc1) + sh1
    x = x + MACARON_W * ga1 * rms_norm(swiglu(h, w_f1_in, w_f1_out), gains[1])
    h = rms_norm(x, gains[2]) * (1 + sc2) + sh2
    y, rows = token_mixing(h, past_k_sb, past_v_sb, past_k_dsa, past_v_dsa, past_k_idx, gla_state,
                           w_in, w_gate, b_gate, g_gla, w_out)
    x = x + ga2 * rms_norm(y, gains[3])
    h = rms_norm(x, gains[4]) * (1 + sc3) + sh3
    x = x + MACARON_W * ga3 * rms_norm(swiglu(h, w_f2_in, w_f2_out), gains[5])
    return x, rows

def setup_inputs(seed: int = 0) -> dict:
    key = jax.random.key(seed)
    ks = jax.random.split(key, 24)
    nrm = lambda k, shape, s: jax.random.normal(k, shape, jnp.float32) * s
    return {
        'x_prompt': nrm(ks[0], (BATCH, SEQ, D_MODEL), 1.0),
        'x_sample': nrm(ks[1], (DEC_BATCH, DEC_SEQ, D_MODEL), 1.0),
        'cache_k_sb': nrm(ks[2], (DEPTH, DEC_BATCH, PAST_LEN, H_A, DH_A), 1.0),
        'cache_v_sb': nrm(ks[3], (DEPTH, DEC_BATCH, PAST_LEN, H_A, DH_A), 1.0),
        'cache_k_dsa': nrm(ks[4], (DEPTH, DEC_BATCH, PAST_LEN, DH_C), 1.0),
        'cache_v_dsa': nrm(ks[5], (DEPTH, DEC_BATCH, PAST_LEN, DH_C), 1.0),
        'cache_k_idx': nrm(ks[6], (DEPTH, DEC_BATCH, PAST_LEN, D_IDX), 1.0),
        'state_gla': nrm(ks[7], (DEPTH, DEC_BATCH, H_B, DK_B, DV_B), 0.5),
        'c_prompt': nrm(ks[8], (BATCH, D_MODEL), 1.0),
        'c_sample': nrm(ks[9], (DEC_BATCH, D_MODEL), 1.0),
        'w_ada': nrm(ks[10], (DEPTH, D_MODEL, 9 * D_MODEL), 0.5 * D_MODEL ** -0.5),
        'b_ada': nrm(ks[11], (DEPTH, 9 * D_MODEL), 0.01),
        'norm_gains': 1.0 + nrm(ks[12], (DEPTH, 6, D_MODEL), 0.05),
        'w_ffn1_in': nrm(ks[13], (DEPTH, D_MODEL, 2 * D_FF), D_MODEL ** -0.5),
        'w_ffn1_out': nrm(ks[14], (DEPTH, D_FF, D_MODEL), D_FF ** -0.5),
        'w_ffn2_in': nrm(ks[15], (DEPTH, D_MODEL, 2 * D_FF), D_MODEL ** -0.5),
        'w_ffn2_out': nrm(ks[16], (DEPTH, D_FF, D_MODEL), D_FF ** -0.5),
        'w_in': nrm(ks[17], (DEPTH, D_MODEL, D_IN), D_MODEL ** -0.5),
        'w_gla_gate': nrm(ks[18], (DEPTH, GATE_RANK, H_B * DK_B), GATE_RANK ** -0.5),
        'b_gla_gate': nrm(ks[19], (DEPTH, H_B * DK_B), 0.1),
        'gla_norm': 1.0 + nrm(ks[20], (DEPTH, H_B * DV_B), 0.05),
        'w_out': nrm(ks[21], (DEPTH, MIX_WIDTH, D_MODEL), MIX_WIDTH ** -0.5),
    }

def reference(x_prompt, x_sample, cache_k_sb, cache_v_sb, cache_k_dsa, cache_v_dsa, cache_k_idx, state_gla,
              c_prompt, c_sample, w_ada, b_ada, norm_gains, w_ffn1_in, w_ffn1_out, w_ffn2_in, w_ffn2_out,
              w_in, w_gla_gate, b_gla_gate, gla_norm, w_out):
    bp = x_prompt.shape[0]
    dt = x_prompt.dtype
    empty_past = (jnp.zeros((bp, 0, H_A, DH_A), dt), jnp.zeros((bp, 0, H_A, DH_A), dt),
                  jnp.zeros((bp, 0, DH_C), dt), jnp.zeros((bp, 0, DH_C), dt),
                  jnp.zeros((bp, 0, D_IDX), dt), jnp.zeros((bp, H_B, DK_B, DV_B), state_gla.dtype))
    xp, xs = x_prompt, x_sample
    acc_p, acc_s = [], []
    for l in range(DEPTH):
        w_l = (w_ada[l], b_ada[l], norm_gains[l], w_ffn1_in[l], w_ffn1_out[l], w_ffn2_in[l], w_ffn2_out[l],
               w_in[l], w_gla_gate[l], b_gla_gate[l], gla_norm[l], w_out[l])
        xp, rows_p = encoder_layer(xp, c_prompt, *empty_past, *w_l)
        xs, rows_s = encoder_layer(xs, c_sample, cache_k_sb[l], cache_v_sb[l], cache_k_dsa[l], cache_v_dsa[l],
                                   cache_k_idx[l], state_gla[l], *w_l)
        acc_p.append(rows_p)
        acc_s.append(rows_s)
    field = lambda acc, i: jnp.stack([r[i] for r in acc], axis=0)
    new_k_sb_p, new_v_sb_p = field(acc_p, 0), field(acc_p, 1)
    new_k_dsa_p, new_v_dsa_p, new_k_idx_p = field(acc_p, 2), field(acc_p, 3), field(acc_p, 4)
    new_gla_p = field(acc_p, 5)
    new_k_sb_s, new_v_sb_s = field(acc_s, 0), field(acc_s, 1)
    new_k_dsa_s, new_v_dsa_s, new_k_idx_s = field(acc_s, 2), field(acc_s, 3), field(acc_s, 4)
    new_gla_s = field(acc_s, 5)
    return (xp, xs, new_k_sb_p, new_v_sb_p, new_k_dsa_p, new_v_dsa_p, new_k_idx_p, new_gla_p,
            new_k_sb_s, new_v_sb_s, new_k_dsa_s, new_v_dsa_s, new_k_idx_s, new_gla_s)


_drawn_inputs = setup_inputs


def setup_inputs(seed=0):
    import zlib

    import numpy as np

    out = dict(_drawn_inputs(seed))
    spreads = {}
    factors = {}
    for name, (base, spread) in spreads.items():
        noise = np.random.default_rng([zlib.crc32(name.encode()), seed]).standard_normal(out[name].shape)
        drawn = base * np.exp(spread * noise) if base else spread * noise
        out[name] = __import__('jax').numpy.asarray(drawn.astype(out[name].dtype))
    for name, factor in factors.items():
        out[name] = (out[name] * factor).astype(out[name].dtype)
    return out
```

```python
from contextlib import ExitStack

import concourse.bass as bass
from concourse import mybir

ALU = mybir.AluOpType
ACT = mybir.ActivationFunctionType
F32 = mybir.dt.float32
F32R = mybir.dt.float32r
AX = mybir.AxisListType.X

P = 128
EPS = 1e-6
MACARON_W = 0.5
GATE_TAU = 16.0
NEG_MASKED = -3.0e38
NEG_TAKEN = -3.4e38
TAKEN_BELOW = -3.3e38
LOGIT_OFF = -1.0e30


class Signal:

    def __init__(self, ctx, nc, name, per_layer, step=1, start=0):
        self.sem = ctx.enter_context(nc.semaphore(name))
        self.per_layer, self.step, self.start = per_layer, step, start

    def credit(self, engine):
        engine.sem_inc(self.sem, self.start)

    def at(self, layer, n):
        return layer * (self.per_layer * self.step) + (self.start + n * self.step)


def encoder_program(nc, T):
    x_prompt, x_sample = T["x_prompt"], T["x_sample"]
    _, SEQ, D = x_prompt.shape
    B, S, _ = x_sample.shape
    DEPTH, _, PAST, HA, DH = T["cache_k_sb"].shape
    HB, DK, DV = T["state_gla"].shape[2:]
    FF = T["w_ffn1_out"].shape[1]
    RANK = T["w_gla_gate"].shape[1]
    NSEQ = 1 + B
    DIN = T["w_in"].shape[2]
    N_SEL_P = SEQ // 4
    N_SEL_S = (PAST + S) // 4
    QSCALE = float(DH) ** -0.5

    NP, NS = SEQ, B * S
    N = NP + NS
    TT = N // P
    KD = D // P
    KF = FF // P
    CH = 64
    LP = 32
    NBP = NP // LP
    NK = PAST + 2 * S
    PAIRS = B // 2
    assert (D, N, NP, NS, PAST, S, B, DH, DV, DK, HA, HB) == (1024, 384, 256, 128, 128, 16, 8, 64, 128, 64, 4, 4)

    C_RB_END = 2304
    C_GB, C_QC, C_KV, C_QI, C_KI = C_RB_END, C_RB_END + RANK, C_RB_END + RANK + 256, C_RB_END + RANK + 384, C_RB_END + RANK + 640
    assert C_KI + 68 == DIN
    QA, KA, VA, QB, KB, VB, RB, QC, QI, KV, KI = 0, 2, 4, 6, 8, 10, 14, 18, 20, 22, 23
    NU = 24
    GB_ROW = 96
    WI_ROW = 64
    TM_TILES = [KA, KA + 1, VA, VA + 1, VB, VB + 1, VB + 2, VB + 3, KV, KI]
    TM_KA, TM_VA, TM_VB, TM_KV, TM_KI = 0, 256, 512, 1024, 1152
    TM_W = 128 * len(TM_TILES)

    U_F1IN, U_F1OUT = 0, KF
    U_WIN = U_F1OUT + KF // 2
    U_WOUT = U_WIN + NU // 2
    U_F2IN = U_WOUT + KD // 2
    U_F2OUT = U_F2IN + KF
    UNITS = U_F2OUT + KF // 2
    assert UNITS % 2 == 0
    ADA = 9 * 4

    with ExitStack() as ctx:
        base = (nc.sbuf_base + 63) // 64 * 64
        cursor = [base]

        def place(name, shape, dt=F32, at=None):
            size = 4
            for n in shape[1:]:
                size *= n
            size = (size + 31) // 32 * 32
            if at is None:
                at = cursor[0]
                cursor[0] += size
            return nc.alloc_sbuf_tensor_at(name, shape, dt, offset=at)

        x = place("x", [P, KD, N])
        act_hi = place("act_hi", [P, KD, N], F32R)
        act_lo = place("act_lo", [P, KD, N], F32R)
        w_raw = [place(f"w_raw{i}", [P, 2048]) for i in range(2)]
        w_hi = [place(f"w_hi{i}", [P, 2048], F32R) for i in range(2)]
        w_lo = [place(f"w_lo{i}", [P, 2048], F32R) for i in range(2)]
        stage_at = cursor[0]
        w_ada_sb = [place(f"w_ada_sb{i}", [P, 2, 1024]) for i in range(2)]
        stage_end = cursor[0]
        mod = place("mod", [P, 3, 3, KD, NSEQ])
        silu_cT = place("silu_cT", [P, KD, 32])
        params = place("params", [P, P])
        params_t = place("params_t", [P, P])
        w_gate_sb = place("w_gate_sb", [P, 256])
        ident = place("ident", [P, P])
        ones_d = place("ones_d", [P, P])
        ones_v = place("ones_v", [P, P])
        causal = place("causal", [P, P])
        gla_mask = place("gla_mask", [P, 2, P])
        restart = place("restart", [P, N])
        dup_eye = place("dup_eye", [P, P])
        spread = place("spread", [P, P])
        sb_mask_c = place("sb_mask_c", [32, 32])
        sb_mask = place("sb_mask", [P, 32])
        own_step = place("own_step", [P, 32])
        head_rows = place("head_rows", [P, P])
        other_seq = place("other_seq", [P, 32])
        parity = place("parity", [P, 2])
        ones_row = place("ones_row", [P, 256])
        rstd = place("rstd", [P, N])
        sq = place("sq", [P, 2, N])
        sumsq = place("sumsq", [P, N])
        scaled = place("scaled", [P, N])
        act_f32 = place("act_f32", [P, 2, N])
        ada_rows = place("ada_rows", [P, 256])
        small = place("small", [P, 64])
        snT = sq[:].rearrange("p a n -> p (a n)")[:, 0:PAIRS * P].rearrange("p (i r) -> p i r", r=P)
        arena = cursor[0]
        room = nc.sbuf_usable_end - arena

        def overlay(offset):
            at = [arena + offset]

            def put(name, shape, dt=F32):
                size = 4
                for n in shape[1:]:
                    size *= n
                t = nc.alloc_sbuf_tensor_at(name, shape, dt, offset=at[0])
                at[0] += (size + 31) // 32 * 32
                assert at[0] <= nc.sbuf_usable_end, (name, at[0] - nc.sbuf_usable_end)
                return t
            return put

        put = overlay(0)
        hid_hi = put("hid_hi", [P, KF, N], F32R)
        hid_lo = put("hid_lo", [P, KF, N], F32R)
        y = put("y", [P, KD, N])
        silu_g = put("silu_g", [P, 2, N])
        hid_f32 = put("hid_f32", [P, N])
        put = overlay(0)
        tok_in = put("tok_in", [P, TT, D])
        c_rows = put("c_rows", [32, D])
        put = overlay(0)
        tok_out = put("tok_out", [P, TT, D])
        put = overlay(0)
        U = put("U", [P, NU, N])
        TM = put("TM", [P, TT, TM_W])
        kc_dup = put("kc_dup", [P, N])
        ki_dup = put("ki_dup", [P, N])
        phase = NU * N * 4 + TT * TM_W * 4 + 2 * N * 4
        tile_at = lambda u: u * N * 4
        k_sb_raw = nc.alloc_sbuf_tensor_at("k_sb_raw", [P, B, 2 * P], F32, offset=stage_at)
        kc_raw = nc.alloc_sbuf_tensor_at("kc_raw", [P, B, 2, DH], F32, offset=stage_at + 8192)
        ki_raw = nc.alloc_sbuf_tensor_at("ki_raw", [P, B, 2, DH], F32, offset=stage_at + 12288)
        assert stage_end - stage_at == 16384
        put = overlay(phase)
        kcT = put("kcT", [P, B, P])
        kiT = put("kiT", [P, B, P])
        vc_past = put("vc_past", [P, B, 2, DH])
        qc_bd = put("qc_bd", [P, 2, B, 32])
        qi_bd = put("qi_bd", [P, 2, B, 32])
        vc_new = put("vc_new", [P, 2, DH])
        score_at = [phase + 4096 * 3 + 2048 * 2 + 512]
        score = put("score", [P, N + NK])
        left = put("left", [P, N + NK])
        off = put("off", [P, N + NK])
        dsa_w = put("dsa_w", [P, HA, N])
        w_sel = scaled[:, 0:P]
        put = overlay(score_at[0])
        dsa_swT = put("dsa_swT", [P, PAIRS, P])
        put = overlay(tile_at(VA))
        relu_s = put("relu_s", [P, PAIRS, NK])
        put = overlay(tile_at(VA))
        dsa_sw = put("dsa_sw", [P, PAIRS, NK])
        put = overlay(tile_at(VB))
        relu_p = put("relu_p", [P, 2, N])
        put = overlay(tile_at(VB))
        dsa_wT = put("dsa_wT", [P, HA, N])
        put = overlay(phase)
        kaT = put("kaT", [P, 2, B, P])
        va_past = put("va_past", [P, B, 2 * P])
        qa_bd = put("qa_bd", [P, 2, B, 32])
        rest = put("rest", [P, HA, N + 2])
        put_wT = overlay(phase + 8192 * 2 + 2048)
        sb_wT = put_wT("sb_wT", [P, HA, N])
        rest_s = put("rest_s", [P, PAIRS, NK + 1])
        sb_swT = put("sb_swT", [P, PAIRS, P])
        put = overlay(tile_at(VA))
        keep_s = put("keep_s", [P, PAIRS, NK])
        put = overlay(tile_at(VB))
        keep = put("keep", [P, HA, N])
        put = overlay(phase)
        gstate = put("gstate", [P, B, 2, DV])
        logdecay = put("logdecay", [P, 2, N])
        q_in = put("q_in", [P, 2, N])
        k_in = put("k_in", [P, 2, N])
        k_out = put("k_out", [P, 2, N])
        k_rows = put("k_rows", [P, 4, 256])
        put = overlay(tile_at(QA))
        att = put("att", [P, TT, HB * P])
        put = overlay(tile_at(VA))
        tmp_a = put("tmp_a", [P, 2, N])
        put = overlay(tile_at(VB))
        tmp_b = put("tmp_b", [P, 2, N])
        q_dec = put("q_dec", [P, 2, N])
        put = overlay(tile_at(QC))
        states = put("states", [P, NBP, 2, DV])

        ps = ctx.enter_context(nc.psum_tensor("ps", [P, 8, 512], F32))

        def sig(name, per_layer, step=1, start=0):
            return Signal(ctx, nc, name, per_layer, step, start)

        sem = lambda name: ctx.enter_context(nc.semaphore(name))
        inputs_landed = sem("inputs_landed")
        consts_ready = sem("consts_ready")
        silu_c_ready = sem("silu_c_ready")
        cT_mm = sem("cT_mm")
        cT_ready = sem("cT_ready")
        const_mm = sem("const_mm")
        masks_ready = sem("masks_ready")
        xT_mm = sem("xT_mm")
        raw_landed = [sig(f"raw_landed{i}", UNITS // 2, 32) for i in range(2)]
        gate_cols_landed = sig("gate_cols_landed", 1, 16)
        params_landed = sig("params_landed", 1, 5 * 16)
        hi_ready = sig("hi_ready", UNITS)
        lo_ready = sig("lo_ready", UNITS, start=2)
        unit_used = sig("unit_used", UNITS, start=2)
        ada_landed = [sig(f"ada_landed{i}", ADA // 2, 16) for i in range(2)]
        ada_used = sig("ada_used", ADA, start=2)
        ada_rows_ready = sig("ada_rows_ready", 9, start=1)
        ada_tr = sig("ada_tr", 9, start=1)
        mod_ready = sig("mod_ready", 9, start=1)
        params_tr = sig("params_tr", 1, start=1)
        params_ready = sig("params_ready", 1)
        silu_ready = sig("silu_ready", 2 * KF)
        hidden_ready = sig("hidden_ready", 2 * KF, start=2)
        proj_done = sig("proj_done", 3 * (KD - 1))
        sq_ready = sig("sq_ready", 6 * KD)
        sq_summed = sig("sq_summed", 6 * KD, start=2)
        mean_mm = sig("mean_mm", 6)
        std_ready = sig("std_ready", 6)
        x_ready = sig("x_ready", 3 * KD)
        act_f32_ready = sig("act_f32_ready", 3 * KD)
        act_hi_ready = sig("act_hi_ready", 3 * KD)
        act_ready = sig("act_ready", 3 * KD)
        u_even = sig("u_even", NU // 2, start=2)
        u_odd = sig("u_odd", NU // 2, start=2)
        tm_tr = sig("tm_tr", 9)
        tm_act = sig("tm_act", 5)
        tm_dve = sig("tm_dve", 4)
        dup_mm = sig("dup_mm", 2)
        dup_ready = sig("dup_ready", 2)
        k_cache_landed = sig("k_cache_landed", 5, 16)
        v_cache_landed = [sig(f"v_cache_landed{i}", n, 16) for i, n in enumerate((2, 1))]
        gstate_landed = sig("gstate_landed", 2, 16)
        kt_tr = sig("kt_tr", 8, start=1)
        kt_ready = sig("kt_ready", 8)
        bd_ready = sig("bd_ready", 2)
        idx_mm = sig("idx_mm", HA)
        idx_relu = sig("idx_relu", HA)
        idx_summed = sig("idx_summed", HA, start=2)
        idx_s_mm = sig("idx_s_mm", 1)
        idx_s_relu = sig("idx_s_relu", 1)
        wsel_mm = sig("wsel_mm", 1)
        wsel_ready = sig("wsel_ready", 1)
        score_s_mm = sig("score_s_mm", 1)
        off_ready = sig("off_ready", 1)
        z_mm = sig("z_mm", 10)
        neg_max_ready = sig("neg_max_ready", 2)
        exp_ready = sig("exp_ready", 2)
        keep_ready = sig("keep_ready", 5)
        weights_ready = sig("weights_ready", 10)
        wt_tr = sig("wt_tr", 12)
        wt_ready = sig("wt_ready", 12)
        pv_mm = sig("pv_mm", 6)
        mix_hi = sig("mix_hi", 6)
        mix_lo = sig("mix_lo", 6)
        gate_mm = sig("gate_mm", 1, start=1)
        gate_split = sig("gate_split", 1)
        softplus_ready = sig("softplus_ready", 1)
        decay_ready = sig("decay_ready", 1)
        decay_exp = sig("decay_exp", 1)
        silu_r_ready = sig("silu_r_ready", 1)
        qk_ready = sig("qk_ready", 1)
        krow_tr = sig("krow_tr", 1)
        krow_ready = sig("krow_ready", 1)
        att_mm = sig("att_mm", 2)
        att_ready = sig("att_ready", 1)
        kv_mm = sig("kv_mm", 2)
        states_ready = sig("states_ready", NBP + 1)
        gla_mm = sig("gla_mm", HB)
        gla_sq = sig("gla_sq", HB)
        gla_mean_mm = sig("gla_mean_mm", HB)
        gla_std = sig("gla_std", HB)
        gla_f32 = sig("gla_f32", HB)
        gla_hi = sig("gla_hi", HB)
        gla_lo = sig("gla_lo", HB)
        rows_stored = sig("rows_stored", 10, 16)
        states_stored = sig("states_stored", 4, 16)
        pool_gates = sem("pool_gates")
        yT_mm = sem("yT_mm")
        y_left, y_right = sem("y_left"), sem("y_right")
        y_stored = sem("y_stored")

        def sample_view(rows, h):
            return ps[rows, 4, :].rearrange("p (b c h t) -> p c h b t", c=2, h=2, t=S)[:, :, h, :, :]

        def sample_logits(i):
            return ps[:, i, 0:NK]

        def wait_chunk(engine, l, nth, f):
            if f < KD - 1:
                engine.wait_ge(proj_done.sem, proj_done.at(l, nth * (KD - 1) + f + 1))
            else:
                engine.wait_ge(unit_used.sem, unit_used.at(l, (U_WIN, U_F2IN, UNITS)[nth]))

        block = ctx.enter_context(nc.Block())

        @block.sync
        def _(sp):
            with sp.Fori(0, DEPTH) as l:
                def ada_component(i):
                    for q in range(4):
                        if q == 0:
                            sp.wait_ge(kt_tr.sem, kt_tr.at(l, 0))
                        sp.wait_ge(ada_used.sem, ada_used.at(l, i * 4 + (q - 1)))
                        sp.dma_start(w_ada_sb[q % 2][:],
                                     T["w_ada"][l, q * 256:(q + 1) * 256, bass.ts(i, 1024)]
                                     .rearrange("(k p) n -> p k n", p=P)).then_inc(ada_landed[q % 2].sem, 16)

                with sp.Fori(0, 9) as i:
                    ada_component(i)

                def slot_free(u):
                    sp.wait_ge(lo_ready.sem, lo_ready.at(l, u - 1))

                def ffn_in(w, u0):
                    with sp.Fori(0, KF // 2) as i:
                        for s in range(2):
                            slot = (u0 + s) % 2
                            slot_free(i * 2 + (u0 + s))
                            for half in range(2):
                                src = w[l, :, bass.ds(i * 256 + (half * FF + s * P), P)]
                                sp.dma_start(w_raw[slot][:, half * 1024:(half + 1) * 1024]
                                             .rearrange("p (k n) -> p k n", n=P),
                                             src.rearrange("(k p) n -> p k n", p=P)
                                             ).then_inc(raw_landed[slot].sem, 16)

                def proj_out(w, u0, chunks):
                    def pair(i, s):
                        slot = (u0 + s) % 2
                        slot_free(i * 2 + (u0 + s))
                        for half in range(2):
                            sp.dma_start(w_raw[slot][:, half * 1024:(half + 1) * 1024],
                                         w[l, bass.ds(i * 512 + (s * 256 + half * P), P), :]
                                         ).then_inc(raw_landed[slot].sem, 16)
                    with sp.Fori(0, chunks // 4) as i:
                        pair(i, 0)
                        pair(i, 1)
                    if chunks % 4:
                        pair(chunks // 4, 0)

                def w_in_regular(i, u, s, col):
                    slot = (U_WIN + s) % 2
                    slot_free(u)
                    for half in range(2):
                        src = T["w_in"][l, half * 512:(half + 1) * 512, bass.ds(col, 256)]
                        sp.dma_start(w_raw[slot][:, half * 1024:(half + 1) * 1024]
                                     .rearrange("p (k n) -> p k n", n=256),
                                     src.rearrange("(k p) n -> p k n", p=P)).then_inc(raw_landed[slot].sem, 16)

                ffn_in(T["w_ffn1_in"], U_F1IN)
                proj_out(T["w_ffn1_out"], U_F1OUT, KF)
                with sp.Fori(0, 4) as i:
                    for s in range(2):
                        w_in_regular(i, i * 2 + (U_WIN + s), s, i * 512 + s * 256)
                w_in_regular(0, U_WIN + 8, 0, 8 * 256)
                w_in_regular(0, U_WIN + 9, 1, C_QC)
                w_in_regular(0, U_WIN + 10, 0, C_QI)
                slot = (U_WIN + 11) % 2
                slot_free(U_WIN + 11)
                last = w_raw[slot][:].rearrange("p (k n) -> p k n", n=256)
                rows = lambda a, b: T["w_in"][l, :, a:b].rearrange("(k p) n -> p k n", p=P)
                sp.dma_start(last[:, :, 0:128], rows(C_KV, C_KV + 128)).then_inc(raw_landed[slot].sem, 16)
                sp.dma_start(last[:, :, 128:196], rows(C_KI, C_KI + 68)).then_inc(raw_landed[slot].sem, 16)
                sp.dma_start(last[:, :, 196:256], rows(C_GB - 28, C_GB + 32)).then_inc(gate_cols_landed.sem, 16)
                proj_out(T["w_out"], U_WOUT, KD)
                ffn_in(T["w_ffn2_in"], U_F2IN)
                proj_out(T["w_ffn2_out"], U_F2OUT, KF)

            for t in range(TT):
                sp.wait_ge(y_left, t + 1)
                sp.wait_ge(y_right, t + 1)
                dst = T["y_prompt"][0, t * P:(t + 1) * P, :] if t < 2 else T["y_sample"].rearrange("b s d -> (b s) d")
                sp.dma_start(dst, tok_out[:, t, :]).then_inc(y_stored, 16)
            sp.wait_ge(y_stored, 16 * TT)

        @block.gpsimd
        def _(pool):
            def keep_where(t, pattern, base, channel, compare, fill):
                pool.affine_select(out=t, in_=t, compare_op=compare, fill=fill, base=base,
                                   pattern=pattern, channel_multiplier=channel)
                pool.drain()

            pool.dma_start(tok_in[:, 0:2, :], x_prompt[0].rearrange("(t p) d -> p t d", p=P)).then_inc(inputs_landed, 16)
            pool.dma_start(tok_in[:, 2, :], x_sample.rearrange("b s d -> (b s) d")).then_inc(inputs_landed, 16)
            pool.memset(c_rows[:], 0.0)
            pool.drain()
            pool.dma_start(c_rows[0:1, :], T["c_prompt"]).then_inc(inputs_landed, 16)
            pool.dma_start(c_rows[1:NSEQ, :], T["c_sample"]).then_inc(inputs_landed, 16)
            pool.memset(params[:], 0.0)
            for t, v in ((ident, 0.0), (ones_d, 1.0 / D), (ones_v, 1.0 / DV), (causal, 0.0), (gla_mask, 1.0),
                         (restart, 1.0), (dup_eye, 0.0), (spread, 0.0), (sb_mask_c, 0.0), (head_rows, 0.0),
                         (other_seq, 0.0), (parity, 1.0), (ones_row, 1.0)):
                pool.memset(t[:], v)
            pool.drain()
            keep_where(ident[:], [[-1, P]], 0, 1, ALU.not_equal, 1.0)
            keep_where(causal[:], [[-1, P]], 0, 1, ALU.is_gt, 1.0)
            for kind, length in ((0, LP), (1, S)):
                m = gla_mask[:, kind, :]
                keep_where(m, [[1, P]], 0, -1, ALU.is_ge, 0.0)
            pool.memset(restart[:, 0:NP].rearrange("p (n l) -> p n l", l=LP)[:, :, 0:1], 0.0)
            pool.memset(restart[:, NP:N].rearrange("p (n l) -> p n l", l=S)[:, :, 0:1], 0.0)
            keep_where(dup_eye[0:64, :].rearrange("p (a n) -> p a n", a=2), [[0, 2], [-1, 64]], 0, 1, ALU.not_equal, 1.0)
            for i in range(PAIRS):
                rows = slice(32 * i, 32 * i + 32)
                for c in range(4):
                    keep_where(spread[rows, :].rearrange("p (b c t) -> p b c t", b=2, c=4)[:, :, c, :],
                               [[-16, 2], [-1, 16]], 0, 1, ALU.not_equal, 1.0)
                keep_where(other_seq[rows, 0:16], [[0, 16]], 15, -1, ALU.is_ge, NEG_MASKED)
                keep_where(other_seq[rows, 16:32], [[0, 16]], -16, 1, ALU.is_ge, NEG_MASKED)
                keep_where(parity[rows, 0:1], [[0, 1]], 15, -1, ALU.is_ge, 0.0)
                keep_where(parity[rows, 1:2], [[0, 1]], -16, 1, ALU.is_ge, 0.0)
            keep_where(sb_mask_c[:], [[-1, 32]], 0, 1, ALU.is_gt, 1.0)
            keep_where(head_rows[WI_ROW:WI_ROW + 4, :].rearrange("p (b h t) -> p b h t", b=2, h=4),
                       [[0, 2], [-1, 4], [0, 16]], 0, 1, ALU.not_equal, 1.0)
            pool.drain()
            for kind, length in ((0, LP), (1, S)):
                m = gla_mask[:, kind, :].rearrange("p (n l) -> p n l", l=length)
                keep_where(m, [[-length, P // length], [0, length]], 0, 1, ALU.is_ge, 0.0)
            pool.affine_select(out=sb_mask_c[:, 0:16], in_=sb_mask_c[:, 0:16], compare_op=ALU.is_ge, fill=1.0,
                               base=15, pattern=[[0, 16]], channel_multiplier=-1)
            pool.drain()
            pool.sem_inc(consts_ready, 1)

            with pool.Fori(0, DEPTH) as l:
                def pass_gate():
                    pool.sem_inc(pool_gates, 1)

                pool.wait_ge(params_tr.sem, params_tr.at(l, 0))
                pool.wait_ge(gate_mm.sem, gate_mm.at(l, 0))
                pass_gate()
                for dst, src in (
                    (params[0:72, :], T["b_ada"][l].rearrange("(r p) -> r p", p=P)),
                    (params[72:120, :], T["norm_gains"][l].rearrange("g (r p) -> (g r) p", p=P)),
                    (params[120:124, :], T["gla_norm"][l].rearrange("(r p) -> r p", p=P)),
                    (params[124:126, :], T["b_gla_gate"][l].rearrange("(r p) -> r p", p=P)),
                    (w_gate_sb[GB_ROW:GB_ROW + RANK, :], T["w_gla_gate"][l]),
                ):
                    pool.dma_start(dst, src).then_inc(params_landed.sem, 16)

                pool.wait_ge(ada_used.sem, ada_used.at(l, ADA))
                pass_gate()
                pool.dma_start(k_sb_raw[:].rearrange("p b n -> p b n"),
                               T["cache_k_sb"][l].rearrange("b p h d -> p b (h d)")).then_inc(k_cache_landed.sem, 16)
                for half in range(2):
                    pool.dma_start(kc_raw[:, :, half, :],
                                   T["cache_k_dsa"][l].rearrange("b p d -> p b d")).then_inc(k_cache_landed.sem, 16)
                    pool.dma_start(ki_raw[:, :, half, :],
                                   T["cache_k_idx"][l].rearrange("b p d -> p b d")).then_inc(k_cache_landed.sem, 16)
                pool.wait_ge(x_ready.sem, x_ready.at(l, 2 * KD))
                pass_gate()
                for half in range(2):
                    pool.dma_start(vc_past[:, :, half, :],
                                   T["cache_v_dsa"][l].rearrange("b p d -> p b d")).then_inc(v_cache_landed[0].sem, 16)

                pool.wait_ge(tm_act.sem, tm_act.at(l, 5))
                pool.wait_ge(tm_dve.sem, tm_dve.at(l, 4))
                pass_gate()
                for name, col, width in (("k_sb", TM_KA, 256), ("v_sb", TM_VA, 256), ("k_dsa", TM_KV, 64),
                                         ("v_dsa", TM_KV + 64, 64), ("k_idx", TM_KI, 64)):
                    dst = T[f"new_{name}_p"][l, 0]
                    dst = dst.rearrange("(t p) h d -> p t (h d)", p=P) if width == 256 else dst.rearrange("(t p) d -> p t d", p=P)
                    pool.dma_start(dst, TM[:, 0:2, col:col + width]).then_inc(rows_stored.sem, 16)
                    dst = T[f"new_{name}_s"][l]
                    dst = dst.rearrange("b s h d -> (b s) (h d)") if width == 256 else dst.rearrange("b s d -> (b s) d")
                    pool.dma_start(dst, TM[:, 2, col:col + width]).then_inc(rows_stored.sem, 16)

                pool.wait_ge(mix_lo.sem, mix_lo.at(l, 3))
                pass_gate()
                pool.dma_start(va_past[:], T["cache_v_sb"][l].rearrange("b p h d -> p b (h d)")).then_inc(v_cache_landed[1].sem, 16)
                pool.wait_ge(mix_lo.sem, mix_lo.at(l, 6))
                pass_gate()
                for c in range(2):
                    pool.dma_start(gstate[:, :, c, :],
                                   T["state_gla"][l, :, 2 * c:2 * c + 2].rearrange("b h k v -> (h k) b v")
                                   ).then_inc(gstate_landed.sem, 16)
                pool.wait_ge(states_ready.sem, states_ready.at(l, NBP + 1))
                pass_gate()
                for c in range(2):
                    pool.dma_start(T["new_gla_p"][l, 0, 2 * c:2 * c + 2].rearrange("h k v -> (h k) v"),
                                   states[:, NBP - 1, c, :]).then_inc(states_stored.sem, 16)
                    pool.dma_start(T["new_gla_s"][l, :, 2 * c:2 * c + 2].rearrange("b h k v -> (h k) b v"),
                                   gstate[:, :, c, :]).then_inc(states_stored.sem, 16)
            pool.wait_ge(rows_stored.sem, rows_stored.at(DEPTH, 0))
            pool.wait_ge(states_stored.sem, states_stored.at(DEPTH, 0))

        @block.scalar
        def _(act):
            u_even.credit(act)
            ada_rows_ready.credit(act)
            act.wait_ge(inputs_landed, 64)
            act.activation(c_rows[:], c_rows[:], ACT.Silu).then_inc(silu_c_ready, 1)
            for f in range(4, KD):
                act.wait_ge(xT_mm, f + 1)
                act.activation(x[:, f, :], ps[:, f, 0:N], ACT.Copy).then_inc(x_ready.sem, 1)

            with act.Fori(0, DEPTH) as l:
                def split_hi(u, slot):
                    act.wait_ge(raw_landed[slot].sem, raw_landed[slot].at(l, 0) + (u // 2 + 1) * 32)
                    act.wait_ge(unit_used.sem, unit_used.at(l, 0) + (u - 1))
                    act.activation(w_hi[slot][:], w_raw[slot][:], ACT.Copy).then_inc(hi_ready.sem, 1)

                def split_hi_in_loop(i, u):
                    slot = u % 2
                    act.wait_ge(raw_landed[slot].sem, raw_landed[slot].at(l, 0) + (i * 32 + (u // 2 + 1) * 32))
                    act.wait_ge(unit_used.sem, unit_used.at(l, 0) + (i * 2 + (u - 1)))
                    act.activation(w_hi[slot][:], w_raw[slot][:], ACT.Copy).then_inc(hi_ready.sem, 1)

                def ada(i):
                    act.wait_ge(ada_used.sem, ada_used.at(l, 4) + i * 4)
                    act.wait_ge(ada_tr.sem, ada_tr.at(l, 0) + i)
                    act.activation(ada_rows[:], ps[:, 4, 0:256], ACT.Copy).then_inc(ada_rows_ready.sem, 1)

                def squares_of_x(norm, nth):
                    for f in range(KD):
                        act.wait_ge(x_ready.sem, x_ready.at(l, nth * KD + f + 1))
                        act.wait_ge(sq_summed.sem, sq_summed.at(l, norm * KD + f - 1))
                        act.activation(sq[:, f % 2, :], x[:, f, :], ACT.Square).then_inc(sq_ready.sem, 1)

                def std(norm):
                    act.wait_ge(mean_mm.sem, mean_mm.at(l, norm + 1))
                    act.activation(rstd[:], ps[:, 0, 0:N], ACT.Sqrt, bias=eps_col).then_inc(std_ready.sem, 1)

                def pre_norm(nth):
                    squares_of_x(2 * nth, nth)
                    std(2 * nth)
                    for f in range(KD):
                        act.wait_ge(act_f32_ready.sem, act_f32_ready.at(l, nth * KD + f + 1))
                        act.activation(act_hi[:, f, :], act_f32[:, f % 2, :], ACT.Copy).then_inc(act_hi_ready.sem, 1)

                def post_norm(nth):
                    for f in range(KD):
                        wait_chunk(act, l, nth, f)
                        act.wait_ge(sq_summed.sem, sq_summed.at(l, (2 * nth + 1) * KD + f - 1))
                        act.activation(sq[:, f % 2, :], ps[:, f, 0:N], ACT.Square).then_inc(sq_ready.sem, 1)
                    std(2 * nth + 1)

                def ffn_in(u0, h0):
                    with act.Fori(0, KF // 2) as i:
                        for s in range(2):
                            split_hi_in_loop(i, u0 + s + 1)
                            act.wait_ge(unit_used.sem, unit_used.at(l, u0 + s + 1) + i * 2)
                            act.wait_ge(hidden_ready.sem, hidden_ready.at(l, h0 + s - 1) + i * 2)
                            act.activation(silu_g[:, s, :], ps[:, 2 * s, 0:N], ACT.Silu).then_inc(silu_ready.sem, 1)

                def proj_out(u0, units, ahead=True):
                    with act.Fori(0, (units - 1) // 2) as i:
                        for s in range(2):
                            split_hi_in_loop(i, u0 + s + 1)
                    for u in range(u0 + (units - 1) // 2 * 2, u0 + units):
                        if ahead or u < u0 + units - 1:
                            split_hi(u + 1, (u + 1) % 2)

                eps_col = small[:, 0:1]
                with act.Fori(0, 9) as i:
                    ada(i)
                pre_norm(0)
                split_hi(0, 0)
                ffn_in(U_F1IN, 0)
                proj_out(U_F1OUT, KF // 2)
                post_norm(0)
                pre_norm(1)
                def w_in_pair(i, ends):
                    for s in range(2):
                        if ends and s == 0:
                            act.wait_ge(gate_cols_landed.sem, gate_cols_landed.at(l, 1))
                        split_hi_in_loop(i, U_WIN + s + 1)
                        act.wait_ge(unit_used.sem, unit_used.at(l, U_WIN + s + 1) + i * 2)
                        act.activation(U[:, bass.ds(i * 4 + 2 * s, 1), :], ps[:, 2 * s, 0:N].rearrange("p (a n) -> p a n", a=1),
                                       ACT.Copy).then_inc(u_even.sem, 1)

                with act.Fori(0, NU // 4 - 1) as i:
                    w_in_pair(i, False)
                w_in_pair(NU // 4 - 1, True)

                for n in range(0, 9, 2):
                    act.wait_ge(tm_tr.sem, tm_tr.at(l, n + 1))
                    t, g = n // 3, n % 3
                    width = 512 if g < 2 else 256
                    act.activation(TM[:, t, g * 512:g * 512 + width], ps[:, 4 + n % 4, 0:width], ACT.Copy).then_inc(tm_act.sem, 1)
                for n, dst in enumerate((kc_dup, ki_dup)):
                    act.wait_ge(dup_mm.sem, dup_mm.at(l, n + 1))
                    act.activation(dst[:], ps[:, n, 0:N], ACT.Copy).then_inc(dup_ready.sem, 1)

                def keys_T(phase_no):
                    for g in range(4):
                        act.wait_ge(kt_tr.sem, kt_tr.at(l, 4 * phase_no + g + 1))
                        if phase_no == 0:
                            dst = (kcT, kiT)[g // 2][:, 4 * (g % 2):4 * (g % 2) + 4, :]
                            bank = (2, 3, 0, 1)[g]
                        else:
                            dst = kaT[:, g // 2, 4 * (g % 2):4 * (g % 2) + 4, :]
                            bank = g
                        act.activation(dst, ps[:, bank, :].rearrange("p (b k) -> p b k", k=P), ACT.Copy).then_inc(kt_ready.sem, 1)

                def attend_tail(phase_no, chunk, wT, swT):
                    for h in range(HA):
                        act.wait_ge(wt_tr.sem, wt_tr.at(l, 6 * phase_no + h + 1))
                        act.activation(wT[:, h, :], ps[:, 4 + h, 0:N], ACT.Copy).then_inc(wt_ready.sem, 1)
                    act.wait_ge(wt_tr.sem, wt_tr.at(l, 6 * phase_no + 5))
                    act.activation(swT[:], ps[:, 2, :].rearrange("p (i r) -> p i r", r=P), ACT.Copy).then_inc(wt_ready.sem, 1)
                    act.wait_ge(wt_tr.sem, wt_tr.at(l, 6 * phase_no + 6))
                    for i in range(PAIRS):
                        rows = slice(32 * i, 32 * i + 32)
                        ins = act.activation(snT[rows, i, :], ps[rows, 3, 0:P], ACT.Copy)
                    ins.then_inc(wt_ready.sem, 1)
                    for c in range(2):
                        act.wait_ge(pv_mm.sem, pv_mm.at(l, 3 * phase_no + c + 1))
                        act.activation(act_hi[:, chunk + c, 0:NP], ps[:, c, 0:NP], ACT.Copy).then_inc(mix_hi.sem, 1)
                    act.wait_ge(pv_mm.sem, pv_mm.at(l, 3 * phase_no + 3))
                    for h in range(2):
                        rows = slice(64 * h, 64 * h + 64)
                        ins = act.activation(act_hi[rows, chunk:chunk + 2, NP:N].rearrange("p c (b t) -> p c b t", t=S),
                                             sample_view(rows, h), ACT.Copy)
                    ins.then_inc(mix_hi.sem, 1)

                keys_T(0)
                for h in range(HA):
                    act.wait_ge(idx_mm.sem, idx_mm.at(l, h + 1))
                    act.wait_ge(idx_summed.sem, idx_summed.at(l, h - 1))
                    act.activation(relu_p[:, h % 2, :], ps[:, 4 + h, 0:N], ACT.Relu).then_inc(idx_relu.sem, 1)
                act.wait_ge(idx_s_mm.sem, idx_s_mm.at(l, 1))
                act.activation(relu_s[:, 0:3, :], ps[:, 0, 0:3 * NK].rearrange("p (i k) -> p i k", k=NK), ACT.Relu)
                act.activation(relu_s[:, 3, :], ps[:, 1, 0:NK], ACT.Relu).then_inc(idx_s_relu.sem, 1)
                act.wait_ge(neg_max_ready.sem, neg_max_ready.at(l, 1))
                for h in range(HA):
                    for t, cols in enumerate((slice(0, P), slice(P, N))):
                        ins = act.activation(dsa_w[:, h, cols], dsa_w[:, h, cols], ACT.Exp, scale=QSCALE,
                                             bias=small[:, 8 + 4 * t + h:9 + 4 * t + h],
                                             accum_out=small[:, 24 + 4 * t + h:25 + 4 * t + h])
                ins.then_inc(exp_ready.sem, 1)
                act.wait_ge(neg_max_ready.sem, neg_max_ready.at(l, 2))
                for i in range(PAIRS):
                    ins = act.activation(dsa_sw[:, i, :], sample_logits(i), ACT.Exp, scale=QSCALE,
                                         bias=small[:, 16 + i:17 + i], accum_out=small[:, 32 + i:33 + i])
                ins.then_inc(exp_ready.sem, 1)
                attend_tail(0, 6, dsa_wT, dsa_swT)

                keys_T(1)
                for h in range(HA):
                    act.wait_ge(z_mm.sem, z_mm.at(l, 5 + h + 1))
                    act.activation(keep[:, h, :], ps[:, 4 + h, 0:N], ACT.Sigmoid, scale=-QSCALE).then_inc(keep_ready.sem, 1)
                act.wait_ge(z_mm.sem, z_mm.at(l, 10))
                act.activation(keep_s[:, 0:3, :], ps[:, 0, 0:3 * NK].rearrange("p (i k) -> p i k", k=NK), ACT.Sigmoid, scale=-QSCALE)
                act.activation(keep_s[:, 3, :], ps[:, 1, 0:NK], ACT.Sigmoid, scale=-QSCALE).then_inc(keep_ready.sem, 1)
                act.wait_ge(weights_ready.sem, weights_ready.at(l, 10))
                attend_tail(1, 0, sb_wT, sb_swT)

                act.wait_ge(gate_mm.sem, gate_mm.at(l, 1))
                act.wait_ge(gate_split.sem, gate_split.at(l, 1))
                for c in range(2):
                    act.activation(tmp_a[:, c, :], ps[:, c, 0:N], ACT.Abs, bias=params_t[:, 124 + c:125 + c])
                act.drain()
                act.activation(tmp_a[:], tmp_a[:], ACT.Exp, scale=-1.0)
                act.drain()
                act.activation(tmp_a[:], tmp_a[:], ACT.Ln, bias=1.0).then_inc(softplus_ready.sem, 1)
                act.wait_ge(decay_ready.sem, decay_ready.at(l, 1))
                act.activation(q_in[:], tmp_a[:], ACT.Exp, scale=1.0 / GATE_TAU)
                act.activation(k_in[:], tmp_a[:], ACT.Exp, scale=-1.0 / GATE_TAU)
                act.activation(k_out[:], tmp_b[:], ACT.Exp, scale=1.0 / GATE_TAU)
                act.activation(logdecay[:], logdecay[:], ACT.Exp, scale=1.0 / GATE_TAU).then_inc(decay_exp.sem, 1)
                act.activation(U[:, RB:RB + 4, :], U[:, RB:RB + 4, :], ACT.Silu).then_inc(silu_r_ready.sem, 1)
                act.wait_ge(krow_tr.sem, krow_tr.at(l, 1))
                act.activation(k_rows[:, 0:2, :], ps[:, 2, :].rearrange("p (t n) -> p t n", n=256), ACT.Copy)
                act.activation(k_rows[:, 2, :], ps[:, 3, 0:256], ACT.Identity, scale=parity[:, 0:1])
                act.activation(k_rows[:, 3, :], ps[:, 3, 0:256], ACT.Identity, scale=parity[:, 1:2]).then_inc(krow_ready.sem, 1)
                for h in range(HB):
                    act.wait_ge(gla_mm.sem, gla_mm.at(l, h + 1))
                    if h >= 2:
                        act.wait_ge(gla_mean_mm.sem, gla_mean_mm.at(l, h - 1))
                    act.activation(sq[:, h % 2, :], ps[:, 4 + h, 0:N], ACT.Square).then_inc(gla_sq.sem, 1)
                    act.wait_ge(gla_mean_mm.sem, gla_mean_mm.at(l, h + 1))
                    if h >= 1:
                        act.wait_ge(gla_f32.sem, gla_f32.at(l, h))
                    act.activation(rstd[:], ps[:, h, 0:N], ACT.Sqrt, bias=eps_col).then_inc(gla_std.sem, 1)
                    act.wait_ge(gla_f32.sem, gla_f32.at(l, h + 1))
                    act.activation(act_hi[:, 2 + h, :], act_f32[:, h % 2, :], ACT.Copy).then_inc(gla_hi.sem, 1)

                proj_out(U_WOUT, KD // 2)
                post_norm(1)
                pre_norm(2)
                ffn_in(U_F2IN, KF)
                proj_out(U_F2OUT, KF // 2, ahead=False)
                post_norm(2)

            for t in range(TT):
                act.wait_ge(yT_mm, 2 * t + 1)
                act.activation(tok_out[:, t, 0:512], ps[:, 2 * t, :], ACT.Copy).then_inc(y_left, 1)

        @block.vector
        def _(dve):
            for free_slots in (lo_ready, hidden_ready, sq_summed, u_odd, idx_summed, mod_ready):
                free_slots.credit(dve)
            dve.memset(small[:], EPS)
            dve.wait_ge(cT_mm, 1)
            dve.tensor_copy(silu_cT[:], ps[:, 4, 0:KD * 32].rearrange("p (f n) -> p f n", n=32)).then_inc(cT_ready, 1)
            dve.wait_ge(const_mm, 1)
            dve.tensor_copy(sb_mask[:], ps[:, 5, 0:32])
            dve.tensor_copy(own_step[:], ps[:, 5, 32:64]).then_inc(masks_ready, 1)
            for f in range(4):
                dve.wait_ge(xT_mm, f + 1)
                dve.tensor_copy(x[:, f, :], ps[:, f, 0:N]).then_inc(x_ready.sem, 1)
            dve.drain()

            with dve.Fori(0, DEPTH) as l:
                def split_lo(g, slot):
                    dve.wait_ge(hi_ready.sem, hi_ready.at(l, 1) + g)
                    dve.tensor_tensor(w_lo[slot][:], w_raw[slot][:], w_hi[slot][:].bitcast(F32), ALU.subtract).then_inc(lo_ready.sem, 1)

                def gains(row):
                    return params_t[:, 72 + KD * row:72 + KD * (row + 1)].unsqueeze(2).broadcast_to([P, KD, NSEQ])

                def ada(i, role):
                    dve.wait_ge(ada_tr.sem, ada_tr.at(l, 1 + role) + i * 3)
                    dst = mod[:, bass.ds(i, 1), role, :, :].rearrange("p a (q j) s -> p (a q) j s", j=2)
                    bias = params_t[:, bass.ds(i * 24 + 8 * role, 8)].rearrange("p (q j) -> p q j", j=2)
                    for j in range(2):
                        ins = dve.tensor_tensor(dst[:, :, j, :],
                                                ps[:, 5, j * P:(j + 1) * P].rearrange("p (q s) -> p q s", q=4)[:, :, 0:NSEQ],
                                                bias[:, :, j].unsqueeze(2).broadcast_to([P, 4, NSEQ]), ALU.add)
                    ins.then_inc(mod_ready.sem, 1)

                def fold_gains():
                    for n in range(3):
                        dve.scalar_tensor_tensor(out=mod[:, n, 1, :, :], in0=mod[:, n, 1, :, :], scalar=1.0,
                                                 in1=gains(2 * n), op0=ALU.add, op1=ALU.mult)
                        dve.scalar_tensor_tensor(out=mod[:, n, 2, :, :], in0=mod[:, n, 2, :, :],
                                                 scalar=1.0 if n == 1 else MACARON_W,
                                                 in1=gains(2 * n + 1), op0=ALU.mult, op1=ALU.mult)
                    dve.drain()

                def per_seq(n, role, f):
                    return mod[:, n, role, f, 1:NSEQ].unsqueeze(2).broadcast_to([P, B, S])

                def samples(t):
                    return t[:, NP:N].rearrange("p (b s) -> p b s", s=S)

                def sum_squares(norm):
                    for f in range(KD):
                        dve.drain()
                        dve.wait_ge(sq_ready.sem, sq_ready.at(l, norm * KD + f + 1))
                        if f == 0:
                            ins = dve.tensor_copy(sumsq[:], sq[:, 0, :])
                        else:
                            ins = dve.tensor_tensor(sumsq[:], sumsq[:], sq[:, f % 2, :], ALU.add)
                        ins.then_inc(sq_summed.sem, 1)

                def inverse_std(norm):
                    dve.wait_ge(std_ready.sem, std_ready.at(l, norm + 1))
                    dve.reciprocal(rstd[:], rstd[:])
                    dve.drain()

                def pre_norm(nth):
                    sum_squares(2 * nth)
                    inverse_std(2 * nth)

                    def low(f):
                        dve.wait_ge(act_hi_ready.sem, act_hi_ready.at(l, nth * KD + f + 1))
                        dve.tensor_tensor(act_lo[:, f, :], act_f32[:, f % 2, :], act_hi[:, f, :].bitcast(F32),
                                          ALU.subtract).then_inc(act_ready.sem, 1)

                    for f in range(KD):
                        dst = act_f32[:, f % 2, :]
                        dve.tensor_tensor(scaled[:], x[:, f, :], rstd[:], ALU.mult)
                        dve.drain()
                        dve.tensor_scalar(dst[:, 0:NP], scaled[:, 0:NP], mod[:, nth, 1, f, 0:1], mod[:, nth, 0, f, 0:1], ALU.mult, ALU.add)
                        dve.tensor_tensor(samples(dst), samples(scaled), per_seq(nth, 1, f), ALU.mult)
                        dve.drain()
                        dve.tensor_tensor(samples(dst), samples(dst), per_seq(nth, 0, f), ALU.add).then_inc(act_f32_ready.sem, 1)
                        if f >= 1:
                            low(f - 1)
                    low(KD - 1)

                def post_norm(nth):
                    for f in range(KD):
                        wait_chunk(dve, l, nth, f)
                        dve.wait_ge(sq_ready.sem, sq_ready.at(l, (2 * nth + 1) * KD + f + 1))
                        dve.tensor_copy(y[:, f, :], ps[:, f, 0:N])
                        if f == 0:
                            ins = dve.tensor_copy(sumsq[:], sq[:, 0, :])
                        else:
                            ins = dve.tensor_tensor(sumsq[:], sumsq[:], sq[:, f % 2, :], ALU.add)
                        ins.then_inc(sq_summed.sem, 1)
                        dve.drain()
                    inverse_std(2 * nth + 1)
                    for f in range(KD):
                        dve.tensor_tensor(y[:, f, :], y[:, f, :], rstd[:], ALU.mult)
                        dve.drain()
                        dve.tensor_tensor(samples(scaled), samples(y[:, f, :]), per_seq(nth, 2, f), ALU.mult)
                        dve.scalar_tensor_tensor(out=x[:, f, 0:NP], in0=y[:, f, 0:NP], scalar=mod[:, nth, 2, f, 0:1],
                                                 in1=x[:, f, 0:NP], op0=ALU.mult, op1=ALU.add)
                        dve.drain()
                        dve.tensor_tensor(x[:, f, NP:N], x[:, f, NP:N], scaled[:, NP:N], ALU.add).then_inc(x_ready.sem, 1)

                def ffn_in(u0, h0):
                    with dve.Fori(0, KF // 2) as i:
                        for s in range(2):
                            split_lo(i * 2 + (u0 + s + 1), (u0 + s + 1) % 2)
                            dve.wait_ge(silu_ready.sem, silu_ready.at(l, h0 + s + 1) + i * 2)
                            dve.tensor_tensor(hid_f32[:], silu_g[:, s, :], ps[:, 2 * s + 1, 0:N], ALU.mult)
                            dve.drain()
                            chunk = bass.ds(i * 2 + s, 1)
                            one = hid_f32[:].rearrange("p (a n) -> p a n", a=1)
                            dve.tensor_copy(hid_hi[:, chunk, :], one)
                            dve.drain()
                            dve.tensor_tensor(hid_lo[:, chunk, :], one, hid_hi[:, chunk, :].bitcast(F32), ALU.subtract).then_inc(hidden_ready.sem, 1)
                            dve.drain()

                def proj_out(u0, units, ahead=True):
                    with dve.Fori(0, (units - 1) // 2) as i:
                        for s in range(2):
                            split_lo(i * 2 + (u0 + s + 1), (u0 + s + 1) % 2)
                    for u in range(u0 + (units - 1) // 2 * 2, u0 + units):
                        if ahead or u < u0 + units - 1:
                            split_lo(u + 1, (u + 1) % 2)

                dve.wait_ge(params_tr.sem, params_tr.at(l, 1))
                dve.tensor_copy(params_t[:], ps[:, 6, 0:P]).then_inc(params_ready.sem, 1)
                dve.drain()
                with dve.Fori(0, 3) as i:
                    for role in range(3):
                        ada(i, role)
                dve.drain()
                fold_gains()
                pre_norm(0)
                split_lo(0, 0)
                ffn_in(U_F1IN, 0)
                proj_out(U_F1OUT, KF // 2)
                post_norm(0)
                pre_norm(1)
                with dve.Fori(0, NU // 4) as i:
                    for s in range(2):
                        split_lo(i * 2 + (U_WIN + s + 1), (U_WIN + s + 1) % 2)
                        dve.wait_ge(unit_used.sem, unit_used.at(l, U_WIN + s + 1) + i * 2)
                        dve.tensor_copy(U[:, bass.ds(i * 4 + 2 * s + 1, 1), :],
                                        ps[:, 2 * s + 1, 0:N].rearrange("p (a n) -> p a n", a=1)).then_inc(u_odd.sem, 1)
                for n in range(1, 9, 2):
                    dve.wait_ge(tm_tr.sem, tm_tr.at(l, n + 1))
                    t, g = n // 3, n % 3
                    width = 512 if g < 2 else 256
                    dve.tensor_copy(TM[:, t, g * 512:g * 512 + width], ps[:, 4 + n % 4, 0:width]).then_inc(tm_dve.sem, 1)

                def block_diagonal(dst, tile):
                    for c in range(2):
                        for h in range(2):
                            rows = slice(64 * h, 64 * h + 64)
                            ins = dve.tensor_copy(dst[rows, c, :, 16 * h:16 * h + 16],
                                                  U[rows, tile + c, NP:N].rearrange("p (b t) -> p b t", t=S))
                    return ins

                def mix_low(phase_no, chunk):
                    for c in range(2):
                        dve.wait_ge(mix_hi.sem, mix_hi.at(l, 3 * phase_no + c + 1))
                        dve.tensor_tensor(act_lo[:, chunk + c, 0:NP], ps[:, c, 0:NP], act_hi[:, chunk + c, 0:NP].bitcast(F32),
                                          ALU.subtract).then_inc(mix_lo.sem, 1)
                    dve.wait_ge(mix_hi.sem, mix_hi.at(l, 3 * phase_no + 3))
                    for h in range(2):
                        rows = slice(64 * h, 64 * h + 64)
                        v = lambda t: t[rows, chunk:chunk + 2, NP:N].rearrange("p c (b t) -> p c b t", t=S)
                        ins = dve.tensor_tensor(v(act_lo), sample_view(rows, h), v(act_hi).bitcast(F32), ALU.subtract)
                    ins.then_inc(mix_lo.sem, 1)

                dve.wait_ge(u_even.sem, u_even.at(l, NU // 2))
                dve.memset(snT, 0.0)
                dve.memset(qc_bd[:], 0.0)
                dve.memset(qi_bd[:], 0.0)
                dve.drain()
                block_diagonal(qc_bd, QC)
                block_diagonal(qi_bd, QI)
                dve.wait_ge(tm_act.sem, tm_act.at(l, 5))
                for half in range(2):
                    ins = dve.tensor_copy(vc_new[:, half, :], TM[:, 2, TM_KV + 64:TM_KV + 128])
                ins.then_inc(bd_ready.sem, 1)
                regions = ((0, P), (P, N))
                for h in range(HA):
                    dve.wait_ge(idx_relu.sem, idx_relu.at(l, h + 1))
                    for t, (a, b) in enumerate(regions):
                        w = TM[:, t, TM_KI + WI_ROW + h:TM_KI + WI_ROW + h + 1]
                        if h == 0:
                            ins = dve.tensor_scalar(score[:, a:b], relu_p[:, 0, a:b], w, None, ALU.mult)
                        else:
                            ins = dve.scalar_tensor_tensor(out=score[:, a:b], in0=relu_p[:, h % 2, a:b], scalar=w,
                                                           in1=score[:, a:b], op0=ALU.mult, op1=ALU.add)
                    ins.then_inc(idx_summed.sem, 1)
                    dve.drain()
                dve.memset(score[0:CH, CH:P], NEG_MASKED)
                dve.memset(score[0:CH, P + 3 * CH:N], NEG_MASKED)
                dve.wait_ge(wsel_mm.sem, wsel_mm.at(l, 1))
                dve.tensor_tensor(w_sel[:].rearrange("p (i k) -> p i k", k=32), ps[:, 2, 0:P].rearrange("p (i k) -> p i k", k=32),
                                  own_step[:].unsqueeze(1).broadcast_to([P, PAIRS, 32]), ALU.mult).then_inc(wsel_ready.sem, 1)
                dve.wait_ge(score_s_mm.sem, score_s_mm.at(l, 1))
                dve.tensor_copy(score[:, N:N + PAST], ps[:, 3, 0:PAST])
                dve.tensor_tensor(score[:, N + PAST:N + NK], ps[:, 3, PAST:NK], other_seq[:], ALU.add)
                dve.drain()
                regions = ((0, P, N_SEL_P), (P, N, N_SEL_P), (N, N + NK, N_SEL_S))
                for r in range((N_SEL_P + 7) // 8):
                    src = score if r == 0 else left
                    live = [(n, a, b, k) for n, (a, b, k) in enumerate(regions) if 8 * r < k]
                    for n, a, b, k in live:
                        dve.max(small[:, 40 + 8 * n:48 + 8 * n], src[:, a:b])
                    dve.drain()
                    for n, a, b, k in live:
                        if k - 8 * r < 8:
                            dve.memset(small[:, 40 + 8 * n + k - 8 * r:48 + 8 * n], NEG_TAKEN)
                            dve.drain()
                    for n, a, b, k in live:
                        dve.match_replace(left[:, a:b], small[:, 40 + 8 * n:48 + 8 * n], src[:, a:b], NEG_TAKEN)
                    dve.drain()
                dve.tensor_scalar(off[:], left[:], TAKEN_BELOW, LOGIT_OFF, ALU.is_gt, ALU.mult).then_inc(off_ready.sem, 1)
                dve.drain()
                for h in range(HA):
                    dve.wait_ge(z_mm.sem, z_mm.at(l, h + 1))
                    dve.tensor_tensor(dsa_w[:, h, :], ps[:, 4 + h, 0:N], off[:, 0:N], ALU.add)
                dve.drain()
                dve.tensor_reduce(small[:, 8:12], dsa_w[:, :, 0:P], AX, ALU.max)
                dve.tensor_reduce(small[:, 12:16], dsa_w[:, :, P:N], AX, ALU.max)
                dve.drain()
                dve.tensor_scalar(small[:, 8:16], small[:, 8:16], -QSCALE, None, ALU.mult).then_inc(neg_max_ready.sem, 1)
                dve.wait_ge(z_mm.sem, z_mm.at(l, 5))
                dve.tensor_reduce(small[:, 16:20], ps[:, 0:PAIRS, 0:NK], AX, ALU.max)
                dve.drain()
                dve.tensor_scalar(small[:, 16:20], small[:, 16:20], -QSCALE, None, ALU.mult).then_inc(neg_max_ready.sem, 1)
                dve.wait_ge(exp_ready.sem, exp_ready.at(l, 1))
                dve.reciprocal(small[:, 24:32], small[:, 24:32])
                dve.drain()
                for t, (a, b) in enumerate(((0, P), (P, N))):
                    ins = dve.tensor_tensor(dsa_w[:, :, a:b], dsa_w[:, :, a:b],
                                            small[:, 24 + 4 * t:28 + 4 * t].unsqueeze(2).broadcast_to([P, HA, b - a]), ALU.mult)
                ins.then_inc(weights_ready.sem, 4)
                dve.wait_ge(exp_ready.sem, exp_ready.at(l, 2))
                dve.reciprocal(small[:, 32:36], small[:, 32:36])
                dve.drain()
                dve.tensor_tensor(dsa_sw[:], dsa_sw[:], small[:, 32:36].unsqueeze(2).broadcast_to([P, PAIRS, NK]),
                                  ALU.mult).then_inc(weights_ready.sem, 1)
                mix_low(0, 6)
                dve.drain()

                dve.memset(qa_bd[:], 0.0)
                dve.memset(rest[:, :, P:P + 1], 1.0)
                dve.memset(rest[:, :, N + 1:N + 2], 1.0)
                dve.memset(rest_s[:, :, NK:NK + 1], 1.0)
                dve.drain()
                block_diagonal(qa_bd, QA).then_inc(bd_ready.sem, 1)
                for h in range(HA):
                    dve.wait_ge(keep_ready.sem, keep_ready.at(l, h + 1))
                    for a in (0, 2 * P):
                        dve.tensor_tensor(keep[:, h, a:a + P], keep[:, h, a:a + P], causal[:], ALU.max)
                    dve.drain()
                    for a, b, at in ((0, P, 0), (P, N, P + 1)):
                        dve.tensor_tensor_scan(rest[:, h, at:at + b - a][:, ::-1], keep[:, h, a:b][:, ::-1], ones_row[:, 0:b - a],
                                               1.0, ALU.mult, ALU.mult)
                    dve.drain()
                    for a, b, at in ((0, P, 0), (P, N, P + 1)):
                        ins = dve.tensor_tensor(keep[:, h, a:b], rest[:, h, at + 1:at + 1 + b - a], rest[:, h, at:at + b - a], ALU.subtract)
                    ins.then_inc(weights_ready.sem, 1)
                dve.wait_ge(keep_ready.sem, keep_ready.at(l, 5))
                dve.tensor_tensor(keep_s[:, :, PAST:NK], keep_s[:, :, PAST:NK], sb_mask[:].unsqueeze(1).broadcast_to([P, PAIRS, 32]), ALU.max)
                dve.drain()
                for i in range(PAIRS):
                    dve.tensor_tensor_scan(rest_s[:, i, 0:NK][:, ::-1], keep_s[:, i, :][:, ::-1], ones_row[:, 0:NK], 1.0, ALU.mult, ALU.mult)
                dve.drain()
                dve.tensor_tensor(keep_s[:], rest_s[:, :, 1:NK + 1], rest_s[:, :, 0:NK], ALU.subtract).then_inc(weights_ready.sem, 1)
                mix_low(1, 0)

                dve.wait_ge(gate_mm.sem, gate_mm.at(l, 1))
                for c in range(2):
                    ins = dve.tensor_scalar(logdecay[:, c, :], ps[:, c, 0:N], params_t[:, 124 + c:125 + c], 0.0, ALU.add, ALU.min)
                ins.then_inc(gate_split.sem, 1)
                dve.wait_ge(softplus_ready.sem, softplus_ready.at(l, 1))
                dve.tensor_tensor(tmp_b[:], logdecay[:], tmp_a[:], ALU.subtract)
                dve.drain()
                for c in range(2):
                    dve.tensor_tensor_scan(logdecay[:, c, :], restart[:], tmp_b[:, c, :], 0.0, ALU.mult, ALU.add)
                dve.drain()
                for a, b, length in ((0, NP, LP), (NP, N, S)):
                    view = lambda t: t[:, :, a:b].rearrange("p c (n l) -> p c n l", l=length)
                    n = (b - a) // length
                    cum = view(logdecay)
                    mid = cum[:, :, :, length // 2 - 1:length // 2].broadcast_to([P, 2, n, length])
                    end = cum[:, :, :, length - 1:length].broadcast_to([P, 2, n, length])
                    dve.tensor_tensor(view(tmp_a), cum, mid, ALU.subtract)
                    ins = dve.tensor_tensor(view(tmp_b), end, cum, ALU.subtract)
                ins.then_inc(decay_ready.sem, 1)
                dve.wait_ge(decay_exp.sem, decay_exp.at(l, 1))
                q, k = U[:, QB:QB + 2, :], U[:, KB:KB + 2, :]
                dve.tensor_tensor(k_out[:], k_out[:], k, ALU.mult)
                dve.tensor_tensor(k_in[:], k_in[:], k, ALU.mult)
                dve.scalar_tensor_tensor(out=q_in[:], in0=q, scalar=QSCALE, in1=q_in[:], op0=ALU.mult, op1=ALU.mult)
                dve.scalar_tensor_tensor(out=q_dec[:], in0=q, scalar=QSCALE, in1=logdecay[:], op0=ALU.mult, op1=ALU.mult).then_inc(qk_ready.sem, 1)
                att_v = att[:].rearrange("p t (c e n) -> p t c e n", c=2, e=2)
                for kind in range(2):
                    dve.wait_ge(att_mm.sem, att_mm.at(l, kind + 1))
                    for e in range(2):
                        if kind == 0:
                            for t in range(2):
                                dve.tensor_tensor(att_v[:, t, :, e, :], ps[:, 4 + e, 256 * t:256 * t + 256].rearrange("p (c n) -> p c n", n=P),
                                                  gla_mask[:, 0, :].unsqueeze(1).broadcast_to([P, 2, P]), ALU.mult)
                        else:
                            ins = dve.tensor_tensor(att_v[:, 2, :, e, :], ps[:, 6 + e, 0:256].rearrange("p (c n) -> p c n", n=P),
                                                    gla_mask[:, 1, :].unsqueeze(1).broadcast_to([P, 2, P]), ALU.mult)
                    if kind == 1:
                        ins.then_inc(att_ready.sem, 1)
                dve.wait_ge(kv_mm.sem, kv_mm.at(l, 1))
                for n in range(NBP):
                    for c in range(2):
                        kv = ps[:, n % 4, (n // 4 * 2 + c) * P:(n // 4 * 2 + c + 1) * P]
                        if n == 0:
                            ins = dve.tensor_copy(states[:, 0, c, :], kv)
                        else:
                            end = LP * n + LP - 1
                            ins = dve.scalar_tensor_tensor(out=states[:, n, c, :], in0=states[:, n - 1, c, :],
                                                           scalar=logdecay[:, c, end:end + 1], in1=kv, op0=ALU.mult, op1=ALU.add)
                    ins.then_inc(states_ready.sem, 1)
                    dve.drain()
                dve.wait_ge(kv_mm.sem, kv_mm.at(l, 2))
                dve.wait_ge(gla_mm.sem, gla_mm.at(l, HB))
                for b in range(B):
                    for c in range(2):
                        end = NP + S * b + S - 1
                        ins = dve.scalar_tensor_tensor(out=gstate[:, b, c, :], in0=gstate[:, b, c, :],
                                                       scalar=logdecay[:, c, end:end + 1],
                                                       in1=ps[:, b // 2, (b % 2 * 2 + c) * P:(b % 2 * 2 + c + 1) * P],
                                                       op0=ALU.mult, op1=ALU.add)
                ins.then_inc(states_ready.sem, 1)
                dve.wait_ge(silu_r_ready.sem, silu_r_ready.at(l, 1))
                for h in range(HB):
                    dve.wait_ge(gla_std.sem, gla_std.at(l, h + 1))
                    dve.reciprocal(sumsq[:], rstd[:])
                    dve.drain()
                    dve.scalar_tensor_tensor(out=scaled[:], in0=ps[:, 4 + h, 0:N], scalar=params_t[:, 120 + h:121 + h], in1=sumsq[:],
                                             op0=ALU.mult, op1=ALU.mult)
                    dve.drain()
                    dve.tensor_tensor(act_f32[:, h % 2, :], scaled[:], U[:, RB + h, :], ALU.mult).then_inc(gla_f32.sem, 1)
                    dve.wait_ge(gla_hi.sem, gla_hi.at(l, h + 1))
                    dve.tensor_tensor(act_lo[:, 2 + h, :], act_f32[:, h % 2, :], act_hi[:, 2 + h, :].bitcast(F32), ALU.subtract).then_inc(gla_lo.sem, 1)

                proj_out(U_WOUT, KD // 2)
                dve.wait_ge(rows_stored.sem, rows_stored.at(l, 10))
                dve.wait_ge(states_stored.sem, states_stored.at(l, 4))
                post_norm(1)
                pre_norm(2)
                ffn_in(U_F2IN, KF)
                proj_out(U_F2OUT, KF // 2, ahead=False)
                post_norm(2)

            for t in range(TT):
                dve.wait_ge(yT_mm, 2 * t + 2)
                dve.tensor_copy(tok_out[:, t, 512:1024], ps[:, 2 * t + 1, :]).then_inc(y_right, 1)

        @block.tensor
        def _(pe):
            for never_zero in (unit_used, ada_used, ada_tr, params_tr, kt_tr, gate_mm):
                never_zero.credit(pe)
            pe.wait_ge(consts_ready, 1)
            pe.wait_ge(inputs_landed, 64)
            pe.wait_ge(silu_c_ready, 1)
            for f in range(KD):
                m = pe.transpose(ps[:, 4, 32 * f:32 * f + 32], c_rows[:, f * P:(f + 1) * P], ident[0:32, 0:32])
            m.then_inc(cT_mm, 1)
            pe.matmul(ps[:, 5, 0:32], spread[0:32, :], sb_mask_c[:], start=True, stop=True)
            pe.matmul(ps[:, 5, 32:64], spread[0:32, :], ident[0:32, 0:32], start=True, stop=True).then_inc(const_mm, 1)
            for f in range(KD):
                if f == 4:
                    pe.wait_ge(cT_ready, 1)
                if f == 5:
                    pe.wait_ge(masks_ready, 1)
                for t in range(TT):
                    m = pe.transpose(ps[:, f, t * P:(t + 1) * P], tok_in[:, t, f * P:(f + 1) * P], ident[:])
                m.then_inc(xT_mm, 1)

            with pe.Fori(0, DEPTH) as l:
                def split_ready(g):
                    pe.wait_ge(lo_ready.sem, lo_ready.at(l, 1) + g)

                def three_products(out, w, wl, a, al, first, last):
                    pe.matmul(out, w, a, start=first, stop=False)
                    pe.matmul(out, w, al, start=False, stop=False)
                    return pe.matmul(out, wl, a, start=False, stop=last)

                def ada_component(i):
                    for q in range(4):
                        pe.wait_ge(ada_landed[q % 2].sem, ada_landed[q % 2].at(l, q // 2 + 1) + i * 32)
                        if q == 0:
                            pe.wait_ge(ada_rows_ready.sem, ada_rows_ready.at(l, 0) + i)
                        for k in range(2):
                            for g in range(4):
                                m = pe.matmul(ps[32 * g:32 * g + 32, 4, 0:256], silu_cT[:, 2 * q + k, :],
                                              w_ada_sb[q % 2][:, k, 256 * g:256 * g + 256],
                                              start=(q + k == 0), stop=(q == 3 and k == 1))
                        m.then_inc(ada_used.sem, 1)
                    pe.wait_ge(ada_rows_ready.sem, ada_rows_ready.at(l, 1) + i)
                    pe.wait_ge(mod_ready.sem, mod_ready.at(l, 0) + i)
                    for j in range(2):
                        m = pe.transpose(ps[:, 5, j * P:(j + 1) * P], ada_rows[:, j * P:(j + 1) * P], ident[:])
                    m.then_inc(ada_tr.sem, 1)

                def mean(norm):
                    pe.wait_ge(sq_summed.sem, sq_summed.at(l, (norm + 1) * KD))
                    pe.matmul(ps[:, 0, 0:N], ones_d[:], sumsq[:], start=True, stop=True).then_inc(mean_mm.sem, 1)

                def column_tile(bank, slot, at, stride, nth=None):
                    for f in range(KD):
                        if nth is not None:
                            pe.wait_ge(act_ready.sem, act_ready.at(l, nth * KD + f + 1))
                        cols = slice(at + f * stride, at + f * stride + P)
                        m = three_products(ps[:, bank, 0:N], w_hi[slot][:, cols], w_lo[slot][:, cols],
                                           act_hi[:, f, :], act_lo[:, f, :], f == 0, f == KD - 1)
                    return m

                def ffn_in(u0, h0, nth):
                    with pe.Fori(0, KF // 2) as i:
                        for s in range(2):
                            slot = (u0 + s) % 2
                            split_ready(i * 2 + (u0 + s))
                            pe.wait_ge(hidden_ready.sem, hidden_ready.at(l, h0 + s - 1) + i * 2)
                            column_tile(2 * s, slot, 0, P, nth)
                            column_tile(2 * s + 1, slot, 1024, P).then_inc(unit_used.sem, 1)

                def proj_out(u0, units, src_hi, src_lo, h0=None):
                    def products(slot, chunk, kc, o, first, last):
                        cols = slice(kc * 1024 + o * P, kc * 1024 + o * P + P)
                        return three_products(ps[:, o:o + 1, 0:N], w_hi[slot][:, cols], w_lo[slot][:, cols],
                                              src_hi[:, bass.ds(chunk, 1), :], src_lo[:, bass.ds(chunk, 1), :], first, last)

                    split_ready(u0)
                    order = (4, 5, 6, 7, 0, 1, 2, 3) if h0 is not None else range(KD)
                    for kc in range(2):
                        for n, o in enumerate(order):
                            if kc == 0 and h0 is not None and n in (0, 4):
                                pe.wait_ge(hidden_ready.sem, hidden_ready.at(l, h0 + (KF - 2 if n == 0 else KF)))
                            m = products(u0 % 2, kc, kc, o, kc == 0, False)
                    m.then_inc(unit_used.sem, 1)
                    pairs = (units - 2) // 2
                    with pe.Fori(0, pairs) as i:
                        for s in range(2):
                            split_ready(i * 2 + (u0 + 1 + s))
                            for kc in range(2):
                                for o in range(KD):
                                    m = products((u0 + 1 + s) % 2, i * 4 + (2 + 2 * s + kc), kc, o, False, False)
                            m.then_inc(unit_used.sem, 1)
                    for u in range(1 + 2 * pairs, units - 1):
                        split_ready(u0 + u)
                        for kc in range(2):
                            for o in range(KD):
                                m = products((u0 + u) % 2, 2 * u + kc, kc, o, False, False)
                        m.then_inc(unit_used.sem, 1)
                    u = units - 1
                    split_ready(u0 + u)
                    for o in range(KD):
                        for kc in range(2):
                            m = products((u0 + u) % 2, 2 * u + kc, kc, o, False, kc == 1)
                        if o < KD - 1:
                            m.then_inc(proj_done.sem, 1)
                    m.then_inc(unit_used.sem, 1)

                pe.wait_ge(x_ready.sem, x_ready.at(l, KD))
                pe.wait_ge(params_landed.sem, params_landed.at(l, 1))
                pe.transpose(ps[:, 6, 0:P], params[:], ident[:]).then_inc(params_tr.sem, 1)
                with pe.Fori(0, 9) as i:
                    ada_component(i)
                mean(0)
                ffn_in(U_F1IN, 0, 0)
                proj_out(U_F1OUT, KF // 2, hid_hi, hid_lo, 0)
                mean(1)
                mean(2)
                with pe.Fori(0, NU // 4) as i:
                    for s in range(2):
                        slot = (U_WIN + s) % 2
                        split_ready(i * 2 + (U_WIN + s))
                        pe.wait_ge(u_even.sem, u_even.at(l, s - 1) + i * 2)
                        pe.wait_ge(u_odd.sem, u_odd.at(l, s - 1) + i * 2)
                        column_tile(2 * s, slot, 0, 256, 1)
                        column_tile(2 * s + 1, slot, P, 256).then_inc(unit_used.sem, 1)

                pe.wait_ge(u_even.sem, u_even.at(l, NU // 2))
                pe.wait_ge(u_odd.sem, u_odd.at(l, NU // 2))
                for n in range(9):
                    t, g = n // 3, n % 3
                    if n >= 4:
                        if n % 2 == 0:
                            pe.wait_ge(tm_act.sem, tm_act.at(l, (n - 4) // 2 + 1))
                        else:
                            pe.wait_ge(tm_dve.sem, tm_dve.at(l, (n - 4) // 2 + 1))
                    for j, tile in enumerate(TM_TILES[4 * g:4 * g + 4]):
                        m = pe.transpose(ps[:, 4 + n % 4, j * P:(j + 1) * P], U[:, tile, t * P:(t + 1) * P], ident[:])
                    m.then_inc(tm_tr.sem, 1)
                for n, tile in enumerate((KV, KI)):
                    pe.matmul(ps[:, n, 0:N], dup_eye[0:64, :], U[0:64, tile, :], start=True, stop=True).then_inc(dup_mm.sem, 1)

                def keys_T(phase_no):
                    pe.wait_ge(k_cache_landed.sem, k_cache_landed.at(l, 5))
                    for g in range(4):
                        if phase_no == 0:
                            bank = (2, 3, 0, 1)[g]
                            if g >= 2:
                                pe.wait_ge(dup_ready.sem, dup_ready.at(l, g - 1))
                        else:
                            bank = g
                        for j in range(4):
                            b = 4 * (g % 2) + j
                            if phase_no == 0:
                                src = (kc_raw, ki_raw)[g // 2][:, b, :, :].rearrange("p a d -> p (a d)")
                            else:
                                src = k_sb_raw[:, b, P * (g // 2):P * (g // 2) + P]
                            m = pe.transpose(ps[:, bank, j * P:(j + 1) * P], src, ident[:])
                        m.then_inc(kt_tr.sem, 1)
                    pe.wait_ge(kt_ready.sem, kt_ready.at(l, 4 * phase_no + 4))

                def scores_prompt(h, q_tile, key, done):
                    rows = slice(64 * (h % 2), 64 * (h % 2) + 64)
                    c = h // 2
                    pe.matmul(ps[:, 4 + h, 0:P], U[rows, q_tile + c, 0:P], key(c)[rows, 0:P], start=True, stop=True)
                    pe.matmul(ps[:, 4 + h, P:N], U[rows, q_tile + c, P:NP], key(c)[rows, 0:NP], start=True, stop=True).then_inc(done.sem, 1)

                def scores_samples(q_bd, past, new, mask=None):
                    for i in range(PAIRS):
                        bank, at = (i, 0) if mask is not None else ((0, NK * i) if i < 3 else (1, 0))
                        if mask is not None:
                            pe.matmul(ps[:, bank, at:at + NK], spread[32 * i:32 * i + 32, :], mask[32 * i:32 * i + 32, N:N + NK],
                                      start=True, stop=False, skip_group_check=True)
                        first = mask is None
                        for b2 in range(2):
                            b = 2 * i + b2
                            for c in range(2):
                                out = ps[64 * b2 + 32 * c:64 * b2 + 32 * c + 32, bank, at:at + NK]
                                pe.matmul(out[:, 0:PAST], q_bd[:, c, b, :], past(c, b), start=first, stop=True, skip_group_check=True)
                                m = pe.matmul(out[:, PAST:NK], q_bd[:, c, b, :], new(c, i), start=first, stop=True, skip_group_check=True)
                    return m

                def attend_tail(phase_no, w, sw, wT, swT, v_prompt, v_past, v_new, per_pair):
                    for h in range(HA):
                        pe.wait_ge(weights_ready.sem, weights_ready.at(l, 5 * phase_no + h + 1))
                        for j in range(3):
                            m = pe.transpose(ps[:, 4 + h, j * P:(j + 1) * P], w[:, h, j * P:(j + 1) * P], ident[:])
                        m.then_inc(wt_tr.sem, 1)
                    pe.wait_ge(weights_ready.sem, weights_ready.at(l, 5 * phase_no + 5))
                    for i in range(PAIRS):
                        m = pe.transpose(ps[:, 2, i * P:(i + 1) * P], sw[:, i, 0:PAST], ident[:])
                    m.then_inc(wt_tr.sem, 1)
                    for i in range(PAIRS):
                        m = pe.matmul(ps[32 * i:32 * i + 32, 3, 0:P], sw[:, i, PAST:NK], ident[:], start=True, stop=True)
                    m.then_inc(wt_tr.sem, 1)
                    for c in range(2):
                        for h2 in range(2):
                            h = 2 * c + h2
                            pe.wait_ge(wt_ready.sem, wt_ready.at(l, 6 * phase_no + h + 1))
                            out = ps[64 * h2:64 * h2 + 64, c, :]
                            pe.matmul(out[:, 0:P], v_prompt(0, h), wT[:, h, 0:P], start=True, stop=True)
                            pe.matmul(out[:, P:NP], v_prompt(0, h), wT[:, h, P:2 * P], start=True, stop=False)
                            m = pe.matmul(out[:, P:NP], v_prompt(1, h), wT[:, h, 2 * P:N], start=False, stop=True)
                        m.then_inc(pv_mm.sem, 1)
                    pe.wait_ge(wt_ready.sem, wt_ready.at(l, 6 * phase_no + 6))
                    for b in range(B):
                        i, b2 = b // 2, b % 2
                        for c in range(2 if per_pair else 1):
                            width = 32 if per_pair else 64
                            cols = slice(64 * b2 + 32 * c, 64 * b2 + 32 * c + width)
                            out = ps[:, 4, 64 * b + 32 * c:64 * b + 32 * c + width]
                            pe.matmul(out, v_past(c, b), swT[:, i, cols], start=True, stop=False)
                            m = pe.matmul(out, v_new(c), snT[:, i, cols], start=False, stop=True)
                    m.then_inc(pv_mm.sem, 1)

                keys_T(0)
                pe.wait_ge(tm_act.sem, tm_act.at(l, 5))
                pe.wait_ge(tm_dve.sem, tm_dve.at(l, 4))
                for h in range(HA):
                    scores_prompt(h, QI, lambda c: ki_dup, idx_mm)
                pe.wait_ge(bd_ready.sem, bd_ready.at(l, 1))
                scores_samples(qi_bd, lambda c, b: kiT[:, b, :], lambda c, i: ki_dup[:, NP + 32 * i:NP + 32 * i + 32]).then_inc(idx_s_mm.sem, 1)
                pe.matmul(ps[:, 2, 0:P], head_rows[WI_ROW:WI_ROW + 4, :], U[WI_ROW:WI_ROW + 4, KI, NP:N], start=True, stop=True).then_inc(wsel_mm.sem, 1)
                pe.wait_ge(wsel_ready.sem, wsel_ready.at(l, 1))
                pe.wait_ge(idx_s_relu.sem, idx_s_relu.at(l, 1))
                for i in range(PAIRS):
                    m = pe.matmul(ps[32 * i:32 * i + 32, 3, 0:NK], w_sel[:, 32 * i:32 * i + 32], relu_s[:, i, :], start=True, stop=True)
                m.then_inc(score_s_mm.sem, 1)
                pe.wait_ge(idx_relu.sem, idx_relu.at(l, HA))
                for h in range(HA):
                    scores_prompt(h, QC, lambda c: kc_dup, z_mm)
                pe.wait_ge(off_ready.sem, off_ready.at(l, 1))
                scores_samples(qc_bd, lambda c, b: kcT[:, b, :], lambda c, i: kc_dup[:, NP + 32 * i:NP + 32 * i + 32], off).then_inc(z_mm.sem, 1)
                pe.wait_ge(v_cache_landed[0].sem, v_cache_landed[0].at(l, 2))
                attend_tail(0, dsa_w, dsa_sw, dsa_wT, dsa_swT,
                            lambda t, h: TM[:, t, TM_KV + 64:TM_KV + 128],
                            lambda c, b: vc_past[:, b, :, :].rearrange("p a d -> p (a d)"),
                            lambda c: vc_new[:].rearrange("p a d -> p (a d)"), False)

                pe.wait_ge(mix_lo.sem, mix_lo.at(l, 3))
                keys_T(1)
                for h in range(HA):
                    scores_prompt(h, QA, lambda c: U[:, KA + c, :], z_mm)
                pe.wait_ge(bd_ready.sem, bd_ready.at(l, 2))
                scores_samples(qa_bd, lambda c, b: kaT[:, c, b, :], lambda c, i: U[:, KA + c, NP + 32 * i:NP + 32 * i + 32]).then_inc(z_mm.sem, 1)
                pe.wait_ge(v_cache_landed[1].sem, v_cache_landed[1].at(l, 1))
                attend_tail(1, keep, keep_s, sb_wT, sb_swT,
                            lambda t, h: TM[:, t, TM_VA + 64 * h:TM_VA + 64 * h + 64],
                            lambda c, b: va_past[:, b, P * c:P * c + P],
                            lambda c: TM[:, 2, TM_VA + P * c:TM_VA + P * c + P], True)

                pe.wait_ge(mix_lo.sem, mix_lo.at(l, 6))
                for c in range(2):
                    m = pe.matmul(ps[:, c, 0:N], w_gate_sb[GB_ROW:GB_ROW + RANK, c * P:(c + 1) * P], U[GB_ROW:GB_ROW + RANK, KI, :],
                                  start=True, stop=True)
                m.then_inc(gate_mm.sem, 1)
                pe.wait_ge(qk_ready.sem, qk_ready.at(l, 1))
                for t in range(TT):
                    for c in range(2):
                        m = pe.transpose(ps[:, 2 + t // 2, (t % 2 * 2 + c) * P:(t % 2 * 2 + c + 1) * P], k_out[:, c, t * P:(t + 1) * P], ident[:])
                m.then_inc(krow_tr.sem, 1)
                for kind, tiles in enumerate(((0, 1), (2,))):
                    for t in tiles:
                        for h in range(HB):
                            e, c = h % 2, h // 2
                            rows = slice(64 * e, 64 * e + 64)
                            at = (t % 2 * 2 + c) * P
                            m = pe.matmul(ps[:, 4 + 2 * kind + e, at:at + P], k_in[rows, c, t * P:(t + 1) * P], q_in[rows, c, t * P:(t + 1) * P],
                                          start=True, stop=True)
                    m.then_inc(att_mm.sem, 1)
                pe.wait_ge(krow_ready.sem, krow_ready.at(l, 1))
                for n in range(NBP):
                    rows = slice(LP * (n % 4), LP * (n % 4) + LP)
                    for c in range(2):
                        for e in range(2):
                            at = (n // 4 * 2 + c) * P
                            m = pe.matmul(ps[64 * e:64 * e + 64, n % 4, at:at + P], k_rows[rows, n // 4, P * c + 64 * e:P * c + 64 * e + 64],
                                          TM[rows, n // 4, TM_VB + (2 * c + e) * P:TM_VB + (2 * c + e + 1) * P], start=True, stop=True)
                m.then_inc(kv_mm.sem, 1)
                pe.wait_ge(att_ready.sem, att_ready.at(l, 1))
                pe.wait_ge(gstate_landed.sem, gstate_landed.at(l, 2))
                for h in range(HB):
                    e, c = h % 2, h // 2
                    rows = slice(64 * e, 64 * e + 64)
                    bank = 4 + h
                    for t in range(TT):
                        pe.matmul(ps[:, bank, t * P:(t + 1) * P], TM[:, t, TM_VB + h * P:TM_VB + (h + 1) * P], att[:, t, h * P:(h + 1) * P],
                                  start=(t == 0), stop=False, skip_group_check=True)
                    for b in range(B):
                        cols = slice(NP + S * b, NP + S * b + S)
                        m = pe.matmul(ps[:, bank, cols], gstate[rows, b, c, :], q_dec[rows, c, cols], start=False, stop=False, skip_group_check=True)
                    for n in range(1, NBP):
                        cols = slice(LP * n, LP * n + LP)
                        if h == 0:
                            pe.wait_ge(states_ready.sem, states_ready.at(l, n))
                        m = pe.matmul(ps[:, bank, cols], states[rows, n - 1, c, :], q_dec[rows, c, cols],
                                      start=False, stop=(n == NBP - 1), skip_group_check=True)
                    m.then_inc(gla_mm.sem, 1)
                pe.wait_ge(states_ready.sem, states_ready.at(l, NBP))
                for b in range(B):
                    rows = slice(32 * (b // 2), 32 * (b // 2) + 32)
                    for c in range(2):
                        for e in range(2):
                            at = (b % 2 * 2 + c) * P
                            m = pe.matmul(ps[64 * e:64 * e + 64, b // 2, at:at + P], k_rows[rows, 2 + b % 2, P * c + 64 * e:P * c + 64 * e + 64],
                                          TM[rows, 2, TM_VB + (2 * c + e) * P:TM_VB + (2 * c + e + 1) * P], start=True, stop=True)
                m.then_inc(kv_mm.sem, 1)
                pe.wait_ge(states_ready.sem, states_ready.at(l, NBP + 1))
                for h in range(HB):
                    pe.wait_ge(gla_sq.sem, gla_sq.at(l, h + 1))
                    pe.matmul(ps[:, h, 0:N], ones_v[:], sq[:, h % 2, :], start=True, stop=True).then_inc(gla_mean_mm.sem, 1)

                pe.wait_ge(gla_lo.sem, gla_lo.at(l, HB))
                proj_out(U_WOUT, KD // 2, act_hi, act_lo)
                mean(3)
                mean(4)
                ffn_in(U_F2IN, KF, 2)
                proj_out(U_F2OUT, KF // 2, hid_hi, hid_lo, KF)
                mean(5)

            for t in range(TT):
                if t == 0:
                    pe.wait_ge(x_ready.sem, x_ready.at(DEPTH, KD))
                for f in range(KD):
                    m = pe.transpose(ps[:, 2 * t + f // 4, (f % 4) * P:(f % 4 + 1) * P], x[:, f, t * P:(t + 1) * P], ident[:])
                    if f % 4 == 3:
                        m.then_inc(yT_mm, 1)


_INS = ['x_prompt', 'x_sample', 'cache_k_sb', 'cache_v_sb', 'cache_k_dsa', 'cache_v_dsa', 'cache_k_idx', 'state_gla',
        'c_prompt', 'c_sample', 'w_ada', 'b_ada', 'norm_gains', 'w_ffn1_in', 'w_ffn1_out', 'w_ffn2_in', 'w_ffn2_out',
        'w_in', 'w_gla_gate', 'b_gla_gate', 'gla_norm', 'w_out']
_OUTS = [('y_prompt', (1, 256, 1024)), ('y_sample', (8, 16, 1024)),
         ('new_k_sb_p', (2, 1, 256, 4, 64)), ('new_v_sb_p', (2, 1, 256, 4, 64)),
         ('new_k_dsa_p', (2, 1, 256, 64)), ('new_v_dsa_p', (2, 1, 256, 64)), ('new_k_idx_p', (2, 1, 256, 64)),
         ('new_gla_p', (2, 1, 4, 64, 128)),
         ('new_k_sb_s', (2, 8, 16, 4, 64)), ('new_v_sb_s', (2, 8, 16, 4, 64)),
         ('new_k_dsa_s', (2, 8, 16, 64)), ('new_v_dsa_s', (2, 8, 16, 64)), ('new_k_idx_s', (2, 8, 16, 64)),
         ('new_gla_s', (2, 8, 4, 64, 128))]


def kernel(**inputs):
    import numpy as _np
    import concourse.bacc as _bacc
    from concourse import mybir as _mybir
    from concourse.bass_utils import run_bass_kernel_spmd as _run

    nc = _bacc.Bacc("TRN2", target_bir_lowering=False, num_devices=1)
    arrays, tensors = {}, {}
    for name in _INS:
        a = _np.ascontiguousarray(inputs[name])
        arrays[f"in_{name}_dram"] = a
        tensors[name] = nc.dram_tensor(f"in_{name}_dram", a.shape, _mybir.dt.from_np(a.dtype), kind="ExternalInput").ap()
    for name, shape in _OUTS:
        tensors[name] = nc.dram_tensor(f"out_{name}_dram", shape, _mybir.dt.float32, kind="ExternalOutput").ap()
    encoder_program(nc, tensors)
    r = _run(nc, [arrays], core_ids=[0])
    return tuple(r.results[0][f"out_{name}_dram"] for name, _ in _OUTS)
```

```python
from contextlib import ExitStack

import concourse.bass as bass
from concourse import mybir

ALU = mybir.AluOpType
ACT = mybir.ActivationFunctionType
F32 = mybir.dt.float32
F32R = mybir.dt.float32r
AX = mybir.AxisListType.X

P = 128
EPS = 1e-6
MACARON_W = 0.5
GATE_TAU = 16.0
NEG_MASKED = -3.0e38
NEG_TAKEN = -3.4e38
TAKEN_BELOW = -3.3e38
LOGIT_OFF = -1.0e30


class Signal:

    def __init__(self, ctx, nc, name, per_layer, step=1, start=0, before=0):
        self.sem = ctx.enter_context(nc.semaphore(name))
        self.per_layer, self.step, self.start, self.before = per_layer, step, start, before

    def credit(self, engine):
        engine.sem_inc(self.sem, self.start)

    def at(self, layer, n):
        return layer * (self.per_layer * self.step) + (n * self.step + (self.start + self.before * self.step))


def encoder_program(nc, T):
    x_prompt, x_sample = T["x_prompt"], T["x_sample"]
    _, SEQ, D = x_prompt.shape
    B, S, _ = x_sample.shape
    DEPTH, _, PAST, HA, DH = T["cache_k_sb"].shape
    HB, DK, DV = T["state_gla"].shape[2:]
    FF = T["w_ffn1_out"].shape[1]
    RANK = T["w_gla_gate"].shape[1]
    NSEQ = 1 + B
    DIN = T["w_in"].shape[2]
    N_SEL_P = SEQ // 4
    N_SEL_S = (PAST + S) // 4
    QSCALE = float(DH) ** -0.5

    NP, NS = SEQ, B * S
    N = NP + NS
    TT = N // P
    KD = D // P
    KF = FF // P
    CH = 64
    LP = 32
    NBP = NP // LP
    NK = PAST + 2 * S
    PAIRS = B // 2
    assert (D, N, NP, NS, PAST, S, B, DH, DV, DK, HA, HB) == (1024, 384, 256, 128, 128, 16, 8, 64, 128, 64, 4, 4)

    C_RB_END = 2304
    C_GB, C_QC, C_KV, C_QI, C_KI = C_RB_END, C_RB_END + RANK, C_RB_END + RANK + 256, C_RB_END + RANK + 384, C_RB_END + RANK + 640
    assert C_KI + 68 == DIN
    QA, KA, VA, QB, KB, VB, RB, QC, QI, KV, KI = 0, 2, 4, 6, 8, 10, 14, 18, 20, 22, 23
    NU = 24
    GB_ROW = 96
    WI_ROW = 64
    TM_TILES = [KA, KA + 1, VA, VA + 1, VB, VB + 1, VB + 2, VB + 3, KV, KI]
    TM_KA, TM_VA, TM_VB, TM_KV, TM_KI = 0, 256, 512, 1024, 1152
    TM_W = 128 * len(TM_TILES)

    U_F1IN, U_F1OUT = 0, KF
    U_WIN = U_F1OUT + KF // 2
    U_WOUT = U_WIN + NU // 2
    U_F2IN = U_WOUT + KD // 2
    U_F2OUT = U_F2IN + KF
    UNITS = U_F2OUT + KF // 2
    assert UNITS % 2 == 0
    WOUT_CHUNKS = (0, 6, 2, 4)
    N_ADA = 9
    ADA_F1, ADA_WIN, ADA_F2 = 0, 5, 6
    assert DEPTH == 2
    NEXT = DEPTH - 1

    with ExitStack() as ctx:
        base = (nc.sbuf_base + 63) // 64 * 64
        cursor = [base]

        def place(name, shape, dt=F32, at=None):
            size = 4
            for n in shape[1:]:
                size *= n
            size = (size + 31) // 32 * 32
            if at is None:
                at = cursor[0]
                cursor[0] += size
            return nc.alloc_sbuf_tensor_at(name, shape, dt, offset=at)

        x = place("x", [P, KD, N])
        act_hi = place("act_hi", [P, KD, N], F32R)
        act_lo = place("act_lo", [P, KD, N], F32R)
        w_raw = [place(f"w_raw{i}", [P, 2048]) for i in range(2)]
        w_hi = [place(f"w_hi{i}", [P, 2048], F32R) for i in range(2)]
        w_lo = [place(f"w_lo{i}", [P, 2048], F32R) for i in range(2)]
        stage_at = cursor[0]
        w_ada_sb = [place(f"w_ada_sb{i}", [P, 2, 1024]) for i in range(2)]
        stage_end = cursor[0]
        mod = place("mod", [P, 9, KD, NSEQ])
        silu_cT = place("silu_cT", [P, KD, 32])
        params = place("params", [P, P])
        w_gate_sb = place("w_gate_sb", [P, 256])
        head = w_gate_sb[0:24, 0:P]
        params_t = place("params_t", [P, P + 24])
        ident = place("ident", [P, P])
        ones_d = place("ones_d", [P, P])
        ones_v = place("ones_v", [P, P])
        causal = place("causal", [P, P])
        gla_mask = place("gla_mask", [P, 2, P])
        restart = place("restart", [P, N])
        dup_eye = place("dup_eye", [P, P])
        spread = place("spread", [P, P])
        sb_mask_c = place("sb_mask_c", [32, 32])
        sb_mask = place("sb_mask", [P, 32])
        own_step = place("own_step", [P, 32])
        head_rows = place("head_rows", [P, P])
        other_seq = place("other_seq", [P, 32])
        parity = place("parity", [P, 2])
        ones_row = place("ones_row", [P, 256])
        rstd = place("rstd", [P, N])
        sq = place("sq", [P, 2, N])
        sumsq = place("sumsq", [P, N])
        scaled = place("scaled", [P, N])
        act_f32 = place("act_f32", [P, 2, N])
        ada_rows = place("ada_rows", [P, 256])
        small = place("small", [P, 64])
        sumsq_pool = act_f32[:, 0, :]
        snT = sq[:].rearrange("p a n -> p (a n)")[:, 0:PAIRS * P].rearrange("p (i r) -> p i r", r=P)
        arena = cursor[0]
        room = nc.sbuf_usable_end - arena

        def overlay(offset):
            at = [arena + offset]

            def put(name, shape, dt=F32):
                size = 4
                for n in shape[1:]:
                    size *= n
                t = nc.alloc_sbuf_tensor_at(name, shape, dt, offset=at[0])
                at[0] += (size + 31) // 32 * 32
                assert at[0] <= nc.sbuf_usable_end, (name, at[0] - nc.sbuf_usable_end)
                return t
            return put

        put = overlay(0)
        hid_hi = put("hid_hi", [P, KF, N], F32R)
        hid_lo = put("hid_lo", [P, KF, N], F32R)
        y = put("y", [P, KD, N])
        silu_g = put("silu_g", [P, 2, N])
        hid_f32 = put("hid_f32", [P, N])
        put = overlay(0)
        tok_in = put("tok_in", [P, TT, D])
        c_rows = put("c_rows", [32, D])
        put = overlay(0)
        tok_out = put("tok_out", [P, TT, D])
        put = overlay(0)
        U = put("U", [P, NU, N])
        TM = put("TM", [P, TT, TM_W])
        kc_dup = put("kc_dup", [P, N])
        ki_dup = put("ki_dup", [P, N])
        phase = NU * N * 4 + TT * TM_W * 4 + 2 * N * 4
        tile_at = lambda u: u * N * 4
        k_sb_raw = nc.alloc_sbuf_tensor_at("k_sb_raw", [P, B, 2 * P], F32, offset=stage_at)
        kc_raw = nc.alloc_sbuf_tensor_at("kc_raw", [P, B, 2, DH], F32, offset=stage_at + 8192)
        ki_raw = nc.alloc_sbuf_tensor_at("ki_raw", [P, B, 2, DH], F32, offset=stage_at + 12288)
        assert stage_end - stage_at == 16384
        put = overlay(phase)
        kcT = put("kcT", [P, B, P])
        kiT = put("kiT", [P, B, P])
        vc_past = put("vc_past", [P, B, 2, DH])
        qc_bd = put("qc_bd", [P, 2, B, 32])
        qi_bd = put("qi_bd", [P, 2, B, 32])
        vc_new = put("vc_new", [P, 2, DH])
        score_at = [phase + 4096 * 3 + 2048 * 2 + 512]
        score = put("score", [P, N + NK])
        left = put("left", [P, N + NK])
        off = put("off", [P, N + NK])
        dsa_w = put("dsa_w", [P, HA, N])
        w_sel = scaled[:, 0:P]
        put = overlay(score_at[0])
        dsa_swT = put("dsa_swT", [P, PAIRS, P])
        put = overlay(tile_at(VA))
        relu_s = put("relu_s", [P, PAIRS, NK])
        put = overlay(tile_at(VA))
        dsa_sw = put("dsa_sw", [P, PAIRS, NK])
        put = overlay(tile_at(VB))
        relu_p = put("relu_p", [P, 2, N])
        put = overlay(tile_at(VB))
        dsa_wT = put("dsa_wT", [P, HA, N])
        put = overlay(phase)
        kaT = put("kaT", [P, 2, B, P])
        va_past = put("va_past", [P, B, 2 * P])
        qa_bd = put("qa_bd", [P, 2, B, 32])
        rest = put("rest", [P, HA, N + 2])
        put_wT = overlay(phase + 8192 * 2 + 2048)
        sb_wT = put_wT("sb_wT", [P, HA, N])
        rest_s = put("rest_s", [P, PAIRS, NK + 1])
        sb_swT = put("sb_swT", [P, PAIRS, P])
        put = overlay(tile_at(VA))
        keep_s = put("keep_s", [P, PAIRS, NK])
        put = overlay(tile_at(VB))
        keep = put("keep", [P, HA, N])
        put = overlay(phase)
        gstate = put("gstate", [P, B, 2, DV])
        gstate_new = put("gstate_new", [P, B, 2, DV])
        logdecay = put("logdecay", [P, 2, N])
        q_in = put("q_in", [P, 2, N])
        k_in = put("k_in", [P, 2, N])
        k_out = put("k_out", [P, 2, N])
        put = overlay(tile_at(QB))
        k_rows = put("k_rows", [P, 4, 256])
        put = overlay(phase + 2 * B * 2 * DV * 4 + 2 * 2 * N * 4)
        gla_out = put("gla_out", [P, HB, N])
        gla_sqs = [sq[:, 0, :], sq[:, 1, :], kc_dup[:], ki_dup[:]]
        gla_stds = [rstd[:], sumsq[:], scaled[:], act_f32[:, 1, :]]
        put = overlay(tile_at(QA))
        att = put("att", [P, TT, HB * P])
        put = overlay(tile_at(VA))
        tmp_a = put("tmp_a", [P, 2, N])
        put = overlay(tile_at(VB))
        tmp_b = put("tmp_b", [P, 2, N])
        q_dec = put("q_dec", [P, 2, N])
        put = overlay(tile_at(QC))
        states = put("states", [P, NBP, 2, DV])

        ps = ctx.enter_context(nc.psum_tensor("ps", [P, 8, 512], F32))

        def sig(name, per_layer, step=1, start=0, before=0):
            return Signal(ctx, nc, name, per_layer, step, start, before)

        sem = lambda name: ctx.enter_context(nc.semaphore(name))
        x_landed = sem("x_landed")
        c_zeroed = sem("c_zeroed")
        c_landed = sem("c_landed")
        ident_ready = sem("ident_ready")
        consts_ready = sem("consts_ready")
        silu_c_ready = sem("silu_c_ready")
        cT_mm = sem("cT_mm")
        cT_ready = sem("cT_ready")
        const_mm = sem("const_mm")
        masks_ready = sem("masks_ready")
        head_ready = sem("head_ready")
        xT_mm = sem("xT_mm")
        raw_landed = [sig(f"raw_landed{i}", UNITS // 2, 32) for i in range(2)]
        gate_cols_landed = sig("gate_cols_landed", 1, 16)
        params_landed = sig("params_landed", 1, 5 * 16)
        hi_ready = sig("hi_ready", UNITS)
        lo_ready = sig("lo_ready", UNITS, start=2)
        unit_used = sig("unit_used", UNITS, start=2)
        ada_landed = [sig(f"ada_landed{i}", N_ADA * 2, 16) for i in range(2)]
        first_ada_landed = [sem(f"first_ada_landed{i}") for i in range(2)]
        ada_used = sig("ada_used", N_ADA * 4, start=2, before=8)
        head_landed = sig("head_landed", 1, 32, before=1)
        head_tr = sig("head_tr", 1, before=1)
        ada_rows_ready = sig("ada_rows_ready", N_ADA, start=1, before=2)
        ada_tr = sig("ada_tr", N_ADA, start=1, before=2)
        mod_ready = sig("mod_ready", N_ADA, start=1, before=2)
        params_tr = sig("params_tr", 1, start=1)
        params_ready = sig("params_ready", 1)
        silu_ready = sig("silu_ready", 2 * KF)
        hidden_ready = sig("hidden_ready", 2 * KF, start=2)
        proj_done = sig("proj_done", 3 * (KD - 1))
        y_sq_ready = sig("y_sq_ready", 3 * KD)
        y_sq_summed = sig("y_sq_summed", 3 * (KD - 1))
        x_sq_ready = sig("x_sq_ready", 3 * KD)
        x_sq_summed = sig("x_sq_summed", 3 * (KD - 3))
        x_sq_last = sig("x_sq_last", 3)
        x_scaled = sig("x_scaled", 3 * KD)
        samples_ready = sig("samples_ready", 3 * KD)
        mean_mm = sig("mean_mm", 6)
        std_ready = sig("std_ready", 6)
        x_ready = sig("x_ready", 3 * KD)
        act_hi_ready = sig("act_hi_ready", 3 * KD)
        act_ready = sig("act_ready", 3 * KD)
        u_even = sig("u_even", NU // 2, start=2)
        u_odd = sig("u_odd", NU // 2, start=2)
        tm_tr = sig("tm_tr", 9)
        tm_act = sig("tm_act", 5)
        tm_dve = sig("tm_dve", 4)
        dup_mm = sig("dup_mm", 2)
        dup_ready = sig("dup_ready", 2)
        k_cache_landed = sig("k_cache_landed", 5, 16)
        v_cache_landed = [sig(f"v_cache_landed{i}", n, 16) for i, n in enumerate((2, 1))]
        gstate_landed = sig("gstate_landed", 2, 16)
        kt_tr = sig("kt_tr", 8, start=1)
        kt_ready = sig("kt_ready", 8)
        bd_ready = sig("bd_ready", 2)
        idx_mm = sig("idx_mm", HA)
        idx_relu = sig("idx_relu", HA)
        idx_summed = sig("idx_summed", HA, start=2)
        idx_s_mm = sig("idx_s_mm", 1)
        idx_s_relu = sig("idx_s_relu", 1)
        wsel_mm = sig("wsel_mm", 1)
        wsel_ready = sig("wsel_ready", 1)
        score_s_mm = sig("score_s_mm", 1)
        off_ready = sig("off_ready", 1)
        z_mm = sig("z_mm", 10)
        neg_max_ready = sig("neg_max_ready", 2)
        exp_ready = sig("exp_ready", 2)
        keep_ready = sig("keep_ready", 5)
        weights_ready = sig("weights_ready", 10)
        wt_tr = sig("wt_tr", 12)
        wt_ready = sig("wt_ready", 12)
        pv_mm = sig("pv_mm", 6)
        mix_hi = sig("mix_hi", 6)
        mix_lo = sig("mix_lo", 6)
        gate_mm = sig("gate_mm", 1, start=1)
        gate_split = sig("gate_split", 1)
        softplus_ready = sig("softplus_ready", 1)
        decay_ready = sig("decay_ready", 1)
        decay_exp = sig("decay_exp", 1)
        silu_r_ready = sig("silu_r_ready", 1)
        qk_ready = sig("qk_ready", 1)
        krow_tr = sig("krow_tr", 1)
        krow_ready = sig("krow_ready", 1)
        att_mm = sig("att_mm", 2)
        att_ready = sig("att_ready", 1)
        kv_mm = sig("kv_mm", 2)
        states_ready = sig("states_ready", NBP + 1)
        gla_mm = sig("gla_mm", HB)
        gla_sq = sig("gla_sq", HB)
        gla_mean_mm = sig("gla_mean_mm", HB)
        gla_std = sig("gla_std", HB)
        gla_copied = sig("gla_copied", HB)
        gla_gated = sig("gla_gated", HB)
        gla_f32 = sig("gla_f32", HB)
        gla_hi = sig("gla_hi", HB)
        gla_lo = sig("gla_lo", HB)
        rows_stored = sig("rows_stored", 10, 16)
        states_stored = sig("states_stored", 4, 16)
        pool_gates = sem("pool_gates")
        yT_mm = sem("yT_mm")
        y_left, y_right = sem("y_left"), sem("y_right")
        y_stored = sem("y_stored")

        def sample_view(rows, h):
            return ps[rows, 4, :].rearrange("p (b c h t) -> p c h b t", c=2, h=2, t=S)[:, :, h, :, :]

        def sample_logits(i):
            return ps[:, i, 0:NK]

        def per_seq(n, role, f):
            return mod[:, 3 * n + role, f, 1:NSEQ].unsqueeze(2).broadcast_to([P, B, S])

        def samples(t):
            return t[:, NP:N].rearrange("p (b s) -> p b s", s=S)

        def slot_sum(f):
            return max(1, f - 2)

        def wait_chunk(engine, l, nth, f):
            if f < KD - 1:
                engine.wait_ge(proj_done.sem, proj_done.at(l, nth * (KD - 1) + f + 1))
            else:
                engine.wait_ge(unit_used.sem, unit_used.at(l, (U_WIN, U_F2IN, UNITS)[nth]))

        block = ctx.enter_context(nc.Block())

        @block.sync
        def _(sp):
            sp.dma_start(tok_in[:, 0:2, :], x_prompt[0].rearrange("(t p) d -> p t d", p=P)).then_inc(x_landed, 16)
            sp.dma_start(tok_in[:, 2, :], x_sample.rearrange("b s d -> (b s) d")).then_inc(x_landed, 16)
            for nth in (-2, -1):
                for q in range(4):
                    sp.wait_ge(ada_used.sem, ada_used.at(0, 4 * nth + q - 1))
                    sp.dma_start(w_ada_sb[q % 2][:],
                                 T["w_ada"][0, q * 256:(q + 1) * 256, (nth + 2) * 1024:(nth + 3) * 1024]
                                 .rearrange("(k p) n -> p k n", p=P)).then_inc(first_ada_landed[q % 2], 16)

            with sp.Fori(0, DEPTH) as l:
                def slot_free(u):
                    sp.wait_ge(lo_ready.sem, lo_ready.at(l, u - 1))

                def ffn_in(w, u0):
                    with sp.Fori(0, KF // 2) as i:
                        for s in range(2):
                            slot = (u0 + s) % 2
                            slot_free(i * 2 + (u0 + s))
                            for half in range(2):
                                src = w[l, :, bass.ds(i * 256 + (half * FF + s * P), P)]
                                sp.dma_start(w_raw[slot][:, half * 1024:(half + 1) * 1024]
                                             .rearrange("p (k n) -> p k n", n=P),
                                             src.rearrange("(k p) n -> p k n", p=P)
                                             ).then_inc(raw_landed[slot].sem, 16)

                def proj_out(w, u0, chunks):
                    def pair(i, s):
                        slot = (u0 + s) % 2
                        slot_free(i * 2 + (u0 + s))
                        for half in range(2):
                            sp.dma_start(w_raw[slot][:, half * 1024:(half + 1) * 1024],
                                         w[l, bass.ds(i * 512 + (s * 256 + half * P), P), :]
                                         ).then_inc(raw_landed[slot].sem, 16)
                    with sp.Fori(0, chunks // 4) as i:
                        pair(i, 0)
                        pair(i, 1)
                    if chunks % 4:
                        pair(chunks // 4, 0)

                def w_in_regular(i, u, s, col):
                    slot = (U_WIN + s) % 2
                    slot_free(u)
                    for half in range(2):
                        src = T["w_in"][l, half * 512:(half + 1) * 512, bass.ds(col, 256)]
                        sp.dma_start(w_raw[slot][:, half * 1024:(half + 1) * 1024]
                                     .rearrange("p (k n) -> p k n", n=256),
                                     src.rearrange("(k p) n -> p k n", p=P)).then_inc(raw_landed[slot].sem, 16)

                ffn_in(T["w_ffn1_in"], U_F1IN)
                proj_out(T["w_ffn1_out"], U_F1OUT, KF)
                with sp.Fori(0, 4) as i:
                    for s in range(2):
                        w_in_regular(i, i * 2 + (U_WIN + s), s, i * 512 + s * 256)
                w_in_regular(0, U_WIN + 8, 0, 8 * 256)
                w_in_regular(0, U_WIN + 9, 1, C_QC)
                w_in_regular(0, U_WIN + 10, 0, C_QI)
                slot = (U_WIN + 11) % 2
                slot_free(U_WIN + 11)
                last = w_raw[slot][:].rearrange("p (k n) -> p k n", n=256)
                rows = lambda a, b: T["w_in"][l, :, a:b].rearrange("(k p) n -> p k n", p=P)
                sp.dma_start(last[:, :, 0:128], rows(C_KV, C_KV + 128)).then_inc(raw_landed[slot].sem, 16)
                sp.dma_start(last[:, :, 128:196], rows(C_KI, C_KI + 68)).then_inc(raw_landed[slot].sem, 16)
                sp.dma_start(last[:, :, 196:256], rows(C_GB - 28, C_GB + 32)).then_inc(gate_cols_landed.sem, 16)
                for u, chunk in enumerate(WOUT_CHUNKS):
                    slot = (U_WOUT + u) % 2
                    slot_free(U_WOUT + u)
                    for half in range(2):
                        row = (chunk + half) * P
                        sp.dma_start(w_raw[slot][:, half * 1024:(half + 1) * 1024],
                                     T["w_out"][l, row:row + P, :]).then_inc(raw_landed[slot].sem, 16)
                ffn_in(T["w_ffn2_in"], U_F2IN)
                proj_out(T["w_ffn2_out"], U_F2OUT, KF)

            for t in range(TT):
                sp.wait_ge(y_left, t + 1)
                sp.wait_ge(y_right, t + 1)
                dst = T["y_prompt"][0, t * P:(t + 1) * P, :] if t < 2 else T["y_sample"].rearrange("b s d -> (b s) d")
                sp.dma_start(dst, tok_out[:, t, :]).then_inc(y_stored, 16)
            sp.wait_ge(y_stored, 16 * TT)

        @block.gpsimd
        def _(pool):
            def keep_where(t, pattern, base, channel, compare, fill):
                pool.affine_select(out=t, in_=t, compare_op=compare, fill=fill, base=base,
                                   pattern=pattern, channel_multiplier=channel)
                pool.drain()

            def load_head(layer):
                pool.dma_start(head[0:16, :], T["b_ada"][layer, 0:2 * D].rearrange("(r p) -> r p", p=P)).then_inc(head_landed.sem, 16)
                pool.dma_start(head[16:24, :], T["norm_gains"][layer, 0].rearrange("(r p) -> r p", p=P)).then_inc(head_landed.sem, 16)

            load_head(0)
            pool.memset(ident[:], 0.0)
            pool.drain()
            keep_where(ident[:], [[-1, P]], 0, 1, ALU.not_equal, 1.0)
            pool.sem_inc(ident_ready, 1)
            pool.memset(params[:], 0.0)
            for t, v in ((ones_d, 1.0 / D), (ones_v, 1.0 / DV), (causal, 0.0), (gla_mask, 1.0),
                         (restart, 1.0), (dup_eye, 0.0), (spread, 0.0), (sb_mask_c, 0.0), (head_rows, 0.0),
                         (other_seq, 0.0), (parity, 1.0), (ones_row, 1.0)):
                pool.memset(t[:], v)
            pool.drain()
            keep_where(causal[:], [[-1, P]], 0, 1, ALU.is_gt, 1.0)
            for kind, length in ((0, LP), (1, S)):
                m = gla_mask[:, kind, :]
                keep_where(m, [[1, P]], 0, -1, ALU.is_ge, 0.0)
            pool.memset(restart[:, 0:NP].rearrange("p (n l) -> p n l", l=LP)[:, :, 0:1], 0.0)
            pool.memset(restart[:, NP:N].rearrange("p (n l) -> p n l", l=S)[:, :, 0:1], 0.0)
            keep_where(dup_eye[0:64, :].rearrange("p (a n) -> p a n", a=2), [[0, 2], [-1, 64]], 0, 1, ALU.not_equal, 1.0)
            for i in range(PAIRS):
                rows = slice(32 * i, 32 * i + 32)
                for c in range(4):
                    keep_where(spread[rows, :].rearrange("p (b c t) -> p b c t", b=2, c=4)[:, :, c, :],
                               [[-16, 2], [-1, 16]], 0, 1, ALU.not_equal, 1.0)
                keep_where(other_seq[rows, 0:16], [[0, 16]], 15, -1, ALU.is_ge, NEG_MASKED)
                keep_where(other_seq[rows, 16:32], [[0, 16]], -16, 1, ALU.is_ge, NEG_MASKED)
                keep_where(parity[rows, 0:1], [[0, 1]], 15, -1, ALU.is_ge, 0.0)
                keep_where(parity[rows, 1:2], [[0, 1]], -16, 1, ALU.is_ge, 0.0)
            keep_where(sb_mask_c[:], [[-1, 32]], 0, 1, ALU.is_gt, 1.0)
            keep_where(head_rows[WI_ROW:WI_ROW + 4, :].rearrange("p (b h t) -> p b h t", b=2, h=4),
                       [[0, 2], [-1, 4], [0, 16]], 0, 1, ALU.not_equal, 1.0)
            pool.drain()
            for kind, length in ((0, LP), (1, S)):
                m = gla_mask[:, kind, :].rearrange("p (n l) -> p n l", l=length)
                keep_where(m, [[-length, P // length], [0, length]], 0, 1, ALU.is_ge, 0.0)
            pool.affine_select(out=sb_mask_c[:, 0:16], in_=sb_mask_c[:, 0:16], compare_op=ALU.is_ge, fill=1.0,
                               base=15, pattern=[[0, 16]], channel_multiplier=-1)
            pool.drain()
            pool.sem_inc(consts_ready, 1)

            with pool.Fori(0, DEPTH) as l:
                def pass_gate():
                    pool.sem_inc(pool_gates, 1)

                pool.wait_ge(params_tr.sem, params_tr.at(l, 0))
                pool.wait_ge(gate_mm.sem, gate_mm.at(l, 0))
                pass_gate()
                for dst, src in (
                    (params[0:72, :], T["b_ada"][l].rearrange("(r p) -> r p", p=P)),
                    (params[72:120, :], T["norm_gains"][l].rearrange("g (r p) -> (g r) p", p=P)),
                    (params[120:124, :], T["gla_norm"][l].rearrange("(r p) -> r p", p=P)),
                    (params[124:126, :], T["b_gla_gate"][l].rearrange("(r p) -> r p", p=P)),
                    (w_gate_sb[GB_ROW:GB_ROW + RANK, :], T["w_gla_gate"][l]),
                ):
                    pool.dma_start(dst, src).then_inc(params_landed.sem, 16)

                pool.wait_ge(head_tr.sem, head_tr.at(l, 0))
                pass_gate()
                load_head(NEXT)

                def ada_component(nth, layer, component, quarters=range(4)):
                    for q in quarters:
                        pool.wait_ge(ada_used.sem, ada_used.at(l, nth * 4 + (q - 1)))
                        pass_gate()
                        pool.dma_start(w_ada_sb[q % 2][:],
                                       T["w_ada"][layer, q * 256:(q + 1) * 256, bass.ds(component * 1024, 1024)]
                                       .rearrange("(k p) n -> p k n", p=P)).then_inc(ada_landed[q % 2].sem, 16)

                def pre_norm(nth):
                    for f in range(1, KD - 2):
                        pool.wait_ge(x_sq_ready.sem, x_sq_ready.at(l, nth * KD + f + 1))
                        pool.tensor_tensor(sumsq_pool, sq[:, 0, :] if f == 1 else sumsq_pool, sq[:, f % 2, :],
                                           ALU.add).then_inc(x_sq_summed.sem, 1)
                        pool.drain()
                    for f in range(KD):
                        pool.wait_ge(x_scaled.sem, x_scaled.at(l, nth * KD + f + 1))
                        pool.tensor_tensor(samples(y[:, f, :]), samples(y[:, f, :]), per_seq(nth, 1, f), ALU.mult)
                        pool.drain()
                        pool.tensor_tensor(samples(y[:, f, :]), samples(y[:, f, :]), per_seq(nth, 0, f), ALU.add).then_inc(samples_ready.sem, 1)

                ada_component(0, l, 2, (0, 1))
                pre_norm(0)
                ada_component(0, l, 2, (2, 3))
                with pool.Fori(1, ADA_WIN) as i:
                    ada_component(i, l, i + 2)
                ada_component(ADA_WIN, l, 7, (0, 1))
                pre_norm(1)
                ada_component(ADA_WIN, l, 7, (2, 3))

                pool.wait_ge(ada_used.sem, ada_used.at(l, 4 * ADA_F2))
                pass_gate()
                pool.dma_start(k_sb_raw[:].rearrange("p b n -> p b n"),
                               T["cache_k_sb"][l].rearrange("b p h d -> p b (h d)")).then_inc(k_cache_landed.sem, 16)
                for half in range(2):
                    pool.dma_start(kc_raw[:, :, half, :],
                                   T["cache_k_dsa"][l].rearrange("b p d -> p b d")).then_inc(k_cache_landed.sem, 16)
                    pool.dma_start(ki_raw[:, :, half, :],
                                   T["cache_k_idx"][l].rearrange("b p d -> p b d")).then_inc(k_cache_landed.sem, 16)
                pool.wait_ge(act_ready.sem, act_ready.at(l, 2 * KD))
                pass_gate()
                for half in range(2):
                    pool.dma_start(vc_past[:, :, half, :],
                                   T["cache_v_dsa"][l].rearrange("b p d -> p b d")).then_inc(v_cache_landed[0].sem, 16)

                pool.wait_ge(tm_act.sem, tm_act.at(l, 5))
                pool.wait_ge(tm_dve.sem, tm_dve.at(l, 4))
                pass_gate()
                for name, col, width in (("k_sb", TM_KA, 256), ("v_sb", TM_VA, 256), ("k_dsa", TM_KV, 64),
                                         ("v_dsa", TM_KV + 64, 64), ("k_idx", TM_KI, 64)):
                    dst = T[f"new_{name}_p"][l, 0]
                    dst = dst.rearrange("(t p) h d -> p t (h d)", p=P) if width == 256 else dst.rearrange("(t p) d -> p t d", p=P)
                    pool.dma_start(dst, TM[:, 0:2, col:col + width]).then_inc(rows_stored.sem, 16)
                    dst = T[f"new_{name}_s"][l]
                    dst = dst.rearrange("b s h d -> (b s) (h d)") if width == 256 else dst.rearrange("b s d -> (b s) d")
                    pool.dma_start(dst, TM[:, 2, col:col + width]).then_inc(rows_stored.sem, 16)

                pool.wait_ge(mix_lo.sem, mix_lo.at(l, 3))
                pass_gate()
                pool.dma_start(va_past[:], T["cache_v_sb"][l].rearrange("b p h d -> p b (h d)")).then_inc(v_cache_landed[1].sem, 16)
                pool.wait_ge(mix_lo.sem, mix_lo.at(l, 6))
                pass_gate()
                for c in range(2):
                    pool.dma_start(gstate[:, :, c, :],
                                   T["state_gla"][l, :, 2 * c:2 * c + 2].rearrange("b h k v -> (h k) b v")
                                   ).then_inc(gstate_landed.sem, 16)
                pool.wait_ge(states_ready.sem, states_ready.at(l, NBP + 1))
                pass_gate()
                for c in range(2):
                    pool.dma_start(T["new_gla_p"][l, 0, 2 * c:2 * c + 2].rearrange("h k v -> (h k) v"),
                                   states[:, NBP - 1, c, :]).then_inc(states_stored.sem, 16)
                    pool.dma_start(T["new_gla_s"][l, :, 2 * c:2 * c + 2].rearrange("b h k v -> (h k) b v"),
                                   gstate_new[:, :, c, :]).then_inc(states_stored.sem, 16)
                for h in range(HB):
                    if h == 0:
                        pool.wait_ge(silu_r_ready.sem, silu_r_ready.at(l, 1))
                    pool.wait_ge(gla_copied.sem, gla_copied.at(l, h + 1))
                    pool.tensor_tensor(gla_out[:, h, :], gla_out[:, h, :], U[:, RB + h, :], ALU.mult).then_inc(gla_gated.sem, 1)

                pool.wait_ge(kt_tr.sem, kt_tr.at(l, 8))
                ada_component(ADA_F2, l, 8, (0, 1))
                pre_norm(2)
                ada_component(ADA_F2, l, 8, (2, 3))
                with pool.Fori(0, 2) as i:
                    ada_component(i + (ADA_F2 + 1), NEXT, i)
            pool.wait_ge(rows_stored.sem, rows_stored.at(DEPTH, 0))
            pool.wait_ge(states_stored.sem, states_stored.at(DEPTH, 0))

        @block.scalar
        def _(act):
            u_even.credit(act)
            ada_rows_ready.credit(act)
            act.wait_ge(c_zeroed, 1)
            act.dma_start(c_rows[0:1, :], T["c_prompt"]).then_inc(c_landed, 16)
            act.dma_start(c_rows[1:NSEQ, :], T["c_sample"]).then_inc(c_landed, 16)
            act.wait_ge(c_landed, 32)
            act.activation(c_rows[:], c_rows[:], ACT.Silu).then_inc(silu_c_ready, 1)
            for f in range(4, KD):
                act.wait_ge(xT_mm, f + 1)
                act.activation(x[:, f, :], ps[:, f, 0:N], ACT.Copy).then_inc(x_ready.sem, 1)

            def ada(l, nth):
                act.wait_ge(ada_used.sem, ada_used.at(l, nth * 4 + 4))
                act.wait_ge(ada_tr.sem, ada_tr.at(l, nth))
                act.activation(ada_rows[:], ps[:, 4, 0:256], ACT.Copy).then_inc(ada_rows_ready.sem, 1)

            ada(0, -2)
            ada(0, -1)

            with act.Fori(0, DEPTH) as l:
                def split_hi(u, slot):
                    act.wait_ge(raw_landed[slot].sem, raw_landed[slot].at(l, 0) + (u // 2 + 1) * 32)
                    act.wait_ge(unit_used.sem, unit_used.at(l, 0) + (u - 1))
                    act.activation(w_hi[slot][:], w_raw[slot][:], ACT.Copy).then_inc(hi_ready.sem, 1)

                def split_hi_in_loop(j, u):
                    slot = u % 2
                    act.wait_ge(raw_landed[slot].sem, raw_landed[slot].at(l, 0) + (j * 16 + (u // 2 + 1) * 32))
                    act.wait_ge(unit_used.sem, unit_used.at(l, 0) + (j + (u - 1)))
                    act.activation(w_hi[slot][:], w_raw[slot][:], ACT.Copy).then_inc(hi_ready.sem, 1)

                def std(norm):
                    act.wait_ge(mean_mm.sem, mean_mm.at(l, norm + 1))
                    act.activation(rstd[:], ps[:, 0, 0:N], ACT.Sqrt, bias=eps_col).then_inc(std_ready.sem, 1)

                def pre_norm(nth):
                    for f in range(KD):
                        act.wait_ge(x_ready.sem, x_ready.at(l, nth * KD + f + 1))
                        if f >= 2:
                            act.wait_ge(x_sq_summed.sem, x_sq_summed.at(l, nth * (KD - 3) + slot_sum(f)))
                        act.activation(sq[:, f % 2, :], x[:, f, :], ACT.Square).then_inc(x_sq_ready.sem, 1)
                    std(2 * nth)
                    for f in range(KD):
                        act.wait_ge(x_scaled.sem, x_scaled.at(l, nth * KD + f + 1))
                        scale, shift = mod[:, 3 * nth + 1, f, 0:1], mod[:, 3 * nth, f, 0:1]
                        act.activation(act_hi[:, f, 0:NP], y[:, f, 0:NP], ACT.Identity, scale=scale, bias=shift)
                        act.activation(y[:, f, 0:NP], y[:, f, 0:NP], ACT.Identity, scale=scale, bias=shift)
                        act.wait_ge(samples_ready.sem, samples_ready.at(l, nth * KD + f + 1))
                        act.activation(act_hi[:, f, NP:N], y[:, f, NP:N], ACT.Copy).then_inc(act_hi_ready.sem, 1)

                def post_norm(nth):
                    for f in range(KD):
                        wait_chunk(act, l, nth, f)
                        act.activation(y[:, f, 0:NP], ps[:, f, 0:NP], ACT.Identity, scale=mod[:, 3 * nth + 2, f, 0:1])
                        if f >= 2:
                            act.wait_ge(y_sq_summed.sem, y_sq_summed.at(l, nth * (KD - 1) + slot_sum(f)))
                        act.activation(sq[:, f % 2, :], ps[:, f, 0:N], ACT.Square).then_inc(y_sq_ready.sem, 1)
                    std(2 * nth + 1)

                def hidden(u0, h0, j, s):
                    split_hi_in_loop(j, u0 + s + 1)
                    if s == 3:
                        return
                    finish(u0, h0, j, s)

                def finish(u0, h0, j, s):
                    act.wait_ge(unit_used.sem, unit_used.at(l, u0 + s + 1) + j)
                    act.wait_ge(hidden_ready.sem, hidden_ready.at(l, h0 + s - 1) + j)
                    act.activation(silu_g[:, s % 2, :], ps[:, 2 * (s % 2), 0:N], ACT.Silu).then_inc(silu_ready.sem, 1)

                def four_hidden(u0, h0, j, nth):
                    for s in range(4):
                        hidden(u0, h0, j, s)
                    ada(l, nth)
                    finish(u0, h0, j, 3)

                def proj_out(u0, units, ahead=True):
                    with act.Fori(0, (units - 1) // 2) as i:
                        for s in range(2):
                            split_hi_in_loop(i * 2, u0 + s + 1)
                    for u in range(u0 + (units - 1) // 2 * 2, u0 + units):
                        if ahead or u < u0 + units - 1:
                            split_hi(u + 1, (u + 1) % 2)

                eps_col = small[:, 0:1]
                pre_norm(0)
                split_hi(0, 0)
                with act.Fori(0, ADA_WIN) as i:
                    four_hidden(U_F1IN, 0, i * 4, i)
                for s in range(2):
                    hidden(U_F1IN, 0, KF - 2, s)
                proj_out(U_F1OUT, KF // 2)
                post_norm(0)
                pre_norm(1)

                def w_in_unit(j, s):
                    split_hi_in_loop(j, U_WIN + s + 1)
                    act.wait_ge(unit_used.sem, unit_used.at(l, U_WIN + s + 1) + j)
                    act.activation(U[:, bass.ds(j * 2 + 2 * s, 1), :], ps[:, 2 * (s % 2), 0:N].rearrange("p (a n) -> p a n", a=1),
                                   ACT.Copy).then_inc(u_even.sem, 1)

                for s in range(4):
                    w_in_unit(0, s)
                ada(l, ADA_WIN)
                with act.Fori(0, 3) as i:
                    for s in range(2):
                        w_in_unit(i * 2 + 4, s)
                act.wait_ge(gate_cols_landed.sem, gate_cols_landed.at(l, 1))
                for s in range(2):
                    w_in_unit(10, s)

                for n in range(0, 9, 2):
                    act.wait_ge(tm_tr.sem, tm_tr.at(l, n + 1))
                    t, g = n // 3, n % 3
                    width = 512 if g < 2 else 256
                    act.activation(TM[:, t, g * 512:g * 512 + width], ps[:, 4 + n % 4, 0:width], ACT.Copy).then_inc(tm_act.sem, 1)
                for n, dst in enumerate((kc_dup, ki_dup)):
                    act.wait_ge(dup_mm.sem, dup_mm.at(l, n + 1))
                    act.activation(dst[:], ps[:, n, 0:N], ACT.Copy).then_inc(dup_ready.sem, 1)

                def keys_T(phase_no):
                    for g in range(4):
                        act.wait_ge(kt_tr.sem, kt_tr.at(l, 4 * phase_no + g + 1))
                        if phase_no == 0:
                            dst = (kcT, kiT)[g // 2][:, 4 * (g % 2):4 * (g % 2) + 4, :]
                            bank = (2, 3, 0, 1)[g]
                        else:
                            dst = kaT[:, g // 2, 4 * (g % 2):4 * (g % 2) + 4, :]
                            bank = g
                        act.activation(dst, ps[:, bank, :].rearrange("p (b k) -> p b k", k=P), ACT.Copy).then_inc(kt_ready.sem, 1)

                def attend_tail(phase_no, chunk, wT, swT):
                    for h in range(HA):
                        act.wait_ge(wt_tr.sem, wt_tr.at(l, 6 * phase_no + h + 1))
                        act.activation(wT[:, h, :], ps[:, 4 + h, 0:N], ACT.Copy).then_inc(wt_ready.sem, 1)
                    act.wait_ge(wt_tr.sem, wt_tr.at(l, 6 * phase_no + 5))
                    act.activation(swT[:], ps[:, 2, :].rearrange("p (i r) -> p i r", r=P), ACT.Copy).then_inc(wt_ready.sem, 1)
                    act.wait_ge(wt_tr.sem, wt_tr.at(l, 6 * phase_no + 6))
                    for i in range(PAIRS):
                        rows = slice(32 * i, 32 * i + 32)
                        ins = act.activation(snT[rows, i, :], ps[rows, 3, 0:P], ACT.Copy)
                    ins.then_inc(wt_ready.sem, 1)
                    for c in range(2):
                        act.wait_ge(pv_mm.sem, pv_mm.at(l, 3 * phase_no + c + 1))
                        act.activation(act_hi[:, chunk + c, 0:NP], ps[:, c, 0:NP], ACT.Copy).then_inc(mix_hi.sem, 1)
                    act.wait_ge(pv_mm.sem, pv_mm.at(l, 3 * phase_no + 3))
                    for h in range(2):
                        rows = slice(64 * h, 64 * h + 64)
                        ins = act.activation(act_hi[rows, chunk:chunk + 2, NP:N].rearrange("p c (b t) -> p c b t", t=S),
                                             sample_view(rows, h), ACT.Copy)
                    ins.then_inc(mix_hi.sem, 1)

                keys_T(0)
                for h in range(HA):
                    act.wait_ge(idx_mm.sem, idx_mm.at(l, h + 1))
                    act.wait_ge(idx_summed.sem, idx_summed.at(l, h - 1))
                    act.activation(relu_p[:, h % 2, :], ps[:, 4 + h, 0:N], ACT.Relu).then_inc(idx_relu.sem, 1)
                act.wait_ge(idx_s_mm.sem, idx_s_mm.at(l, 1))
                act.activation(relu_s[:, 0:3, :], ps[:, 0, 0:3 * NK].rearrange("p (i k) -> p i k", k=NK), ACT.Relu)
                act.activation(relu_s[:, 3, :], ps[:, 1, 0:NK], ACT.Relu).then_inc(idx_s_relu.sem, 1)
                act.wait_ge(neg_max_ready.sem, neg_max_ready.at(l, 1))
                for h in range(HA):
                    for t, cols in enumerate((slice(0, P), slice(P, N))):
                        ins = act.activation(dsa_w[:, h, cols], dsa_w[:, h, cols], ACT.Exp, scale=QSCALE,
                                             bias=small[:, 8 + 4 * t + h:9 + 4 * t + h],
                                             accum_out=small[:, 24 + 4 * t + h:25 + 4 * t + h])
                ins.then_inc(exp_ready.sem, 1)
                act.wait_ge(neg_max_ready.sem, neg_max_ready.at(l, 2))
                for i in range(PAIRS):
                    ins = act.activation(dsa_sw[:, i, :], sample_logits(i), ACT.Exp, scale=QSCALE,
                                         bias=small[:, 16 + i:17 + i], accum_out=small[:, 32 + i:33 + i])
                ins.then_inc(exp_ready.sem, 1)
                attend_tail(0, 6, dsa_wT, dsa_swT)

                keys_T(1)
                for h in range(HA):
                    act.wait_ge(z_mm.sem, z_mm.at(l, 5 + h + 1))
                    act.activation(keep[:, h, :], ps[:, 4 + h, 0:N], ACT.Sigmoid, scale=-QSCALE).then_inc(keep_ready.sem, 1)
                act.wait_ge(z_mm.sem, z_mm.at(l, 10))
                act.activation(keep_s[:, 0:3, :], ps[:, 0, 0:3 * NK].rearrange("p (i k) -> p i k", k=NK), ACT.Sigmoid, scale=-QSCALE)
                act.activation(keep_s[:, 3, :], ps[:, 1, 0:NK], ACT.Sigmoid, scale=-QSCALE).then_inc(keep_ready.sem, 1)
                act.wait_ge(weights_ready.sem, weights_ready.at(l, 10))
                attend_tail(1, 0, sb_wT, sb_swT)

                act.wait_ge(gate_mm.sem, gate_mm.at(l, 1))
                act.wait_ge(gate_split.sem, gate_split.at(l, 1))
                for c in range(2):
                    act.activation(tmp_a[:, c, :], ps[:, c, 0:N], ACT.Abs, bias=params_t[:, 124 + c:125 + c])
                act.drain()
                act.activation(tmp_a[:], tmp_a[:], ACT.Exp, scale=-1.0)
                act.drain()
                act.activation(tmp_a[:], tmp_a[:], ACT.Ln, bias=1.0).then_inc(softplus_ready.sem, 1)
                act.wait_ge(decay_ready.sem, decay_ready.at(l, 1))
                act.activation(q_in[:], tmp_a[:], ACT.Exp, scale=1.0 / GATE_TAU)
                act.activation(k_in[:], tmp_a[:], ACT.Exp, scale=-1.0 / GATE_TAU)
                act.activation(k_out[:], tmp_b[:], ACT.Exp, scale=1.0 / GATE_TAU)
                act.activation(logdecay[:], logdecay[:], ACT.Exp, scale=1.0 / GATE_TAU).then_inc(decay_exp.sem, 1)
                act.activation(U[:, RB:RB + 4, :], U[:, RB:RB + 4, :], ACT.Silu).then_inc(silu_r_ready.sem, 1)
                act.wait_ge(krow_tr.sem, krow_tr.at(l, 1))
                act.activation(k_rows[:, 0:2, :], ps[:, 2, :].rearrange("p (t n) -> p t n", n=256), ACT.Copy)
                act.activation(k_rows[:, 2, :], ps[:, 3, 0:256], ACT.Identity, scale=parity[:, 0:1])
                act.activation(k_rows[:, 3, :], ps[:, 3, 0:256], ACT.Identity, scale=parity[:, 1:2]).then_inc(krow_ready.sem, 1)
                for h in range(HB):
                    act.wait_ge(gla_mm.sem, gla_mm.at(l, h + 1))
                    act.activation(gla_sqs[h], ps[:, 4 + h, 0:N], ACT.Square).then_inc(gla_sq.sem, 1)
                    act.activation(gla_out[:, h, :], ps[:, 4 + h, 0:N], ACT.Identity,
                                   scale=params_t[:, 120 + h:121 + h]).then_inc(gla_copied.sem, 1)
                split_hi(U_WOUT + 1, (U_WOUT + 1) % 2)
                for h in range(HB):
                    act.wait_ge(gla_mean_mm.sem, gla_mean_mm.at(l, h + 1))
                    act.activation(gla_stds[h], ps[:, h, 0:N], ACT.Sqrt, bias=eps_col).then_inc(gla_std.sem, 1)
                for h in range(HB):
                    act.wait_ge(gla_f32.sem, gla_f32.at(l, h + 1))
                    act.activation(act_hi[:, 2 + h, :], gla_out[:, h, :], ACT.Copy).then_inc(gla_hi.sem, 1)

                for u in range(U_WOUT + 1, U_WOUT + KD // 2):
                    split_hi(u + 1, (u + 1) % 2)
                act.wait_ge(rows_stored.sem, rows_stored.at(l, 10))
                act.wait_ge(states_stored.sem, states_stored.at(l, 4))
                post_norm(1)
                pre_norm(2)
                four_hidden(U_F2IN, KF, 0, ADA_F2)
                with act.Fori(0, 2) as i:
                    four_hidden(U_F2IN, KF, i * 4 + 4, i + (ADA_F2 + 1))
                with act.Fori(0, (KF - 12) // 2) as i:
                    for s in range(2):
                        hidden(U_F2IN, KF, i * 2 + 12, s)
                proj_out(U_F2OUT, KF // 2, ahead=False)
                post_norm(2)

            for t in range(TT):
                act.wait_ge(yT_mm, 2 * t + 1)
                act.activation(tok_out[:, t, 0:512], ps[:, 2 * t, :], ACT.Copy).then_inc(y_left, 1)

        @block.vector
        def _(dve):
            for free_slots in (lo_ready, hidden_ready, u_odd, idx_summed, mod_ready):
                free_slots.credit(dve)
            dve.memset(c_rows[:], 0.0).then_inc(c_zeroed, 1)
            dve.memset(small[:], EPS)
            dve.wait_ge(cT_mm, 1)
            dve.tensor_copy(silu_cT[:], ps[:, 4, 0:KD * 32].rearrange("p (f n) -> p f n", n=32)).then_inc(cT_ready, 1)
            dve.wait_ge(head_tr.sem, head_tr.at(0, 0))
            dve.tensor_copy(params_t[:, P:P + 24], ps[:, 5, 64:88]).then_inc(head_ready, 1)
            for f in range(4):
                dve.wait_ge(xT_mm, f + 1)
                dve.tensor_copy(x[:, f, :], ps[:, f, 0:N]).then_inc(x_ready.sem, 1)
            dve.drain()

            def ada(l, nth, component, bias_at):
                dve.wait_ge(ada_tr.sem, ada_tr.at(l, nth + 1))
                dst = mod[:, bass.ds(component, 1), :, :].rearrange("p a (q j) s -> p (a q) j s", j=2)
                bias = params_t[:, bass.ds(bias_at, 8)].rearrange("p (q j) -> p q j", j=2)
                for j in range(2):
                    ins = dve.tensor_tensor(dst[:, :, j, :],
                                            ps[:, 5, j * P:(j + 1) * P].rearrange("p (q s) -> p q s", q=4)[:, :, 0:NSEQ],
                                            bias[:, :, j].unsqueeze(2).broadcast_to([P, 4, NSEQ]), ALU.add)
                ins.then_inc(mod_ready.sem, 1)

            def fold_gain(component, gain_at):
                norm, role = component // 3, component % 3
                m = mod[:, component, :, :]
                gain = params_t[:, gain_at:gain_at + KD].unsqueeze(2).broadcast_to([P, KD, NSEQ])
                if role == 1:
                    dve.scalar_tensor_tensor(out=m, in0=m, scalar=1.0, in1=gain, op0=ALU.add, op1=ALU.mult)
                else:
                    dve.scalar_tensor_tensor(out=m, in0=m, scalar=1.0 if norm == 1 else MACARON_W, in1=gain,
                                             op0=ALU.mult, op1=ALU.mult)

            ada(0, -2, 0, P)
            ada(0, -1, 1, P + 8)
            dve.drain()
            fold_gain(1, P + 16)
            dve.wait_ge(const_mm, 1)
            dve.tensor_copy(sb_mask[:], ps[:, 7, 384:416])
            dve.tensor_copy(own_step[:], ps[:, 7, 416:448]).then_inc(masks_ready, 1)
            dve.drain()

            with dve.Fori(0, DEPTH) as l:
                def split_lo(g, slot):
                    dve.wait_ge(hi_ready.sem, hi_ready.at(l, 1) + g)
                    dve.tensor_tensor(w_lo[slot][:], w_raw[slot][:], w_hi[slot][:].bitcast(F32), ALU.subtract).then_inc(lo_ready.sem, 1)

                def inverse_std(norm):
                    dve.wait_ge(std_ready.sem, std_ready.at(l, norm + 1))
                    dve.reciprocal(rstd[:], rstd[:])
                    dve.drain()

                def pre_norm(nth):
                    dve.wait_ge(x_sq_ready.sem, x_sq_ready.at(l, (nth + 1) * KD))
                    dve.tensor_tensor(sumsq[:], sq[:, 0, :], sq[:, 1, :], ALU.add).then_inc(x_sq_last.sem, 1)
                    inverse_std(2 * nth)

                    def low(f):
                        dve.wait_ge(act_hi_ready.sem, act_hi_ready.at(l, nth * KD + f + 1))
                        dve.tensor_tensor(act_lo[:, f, :], y[:, f, :], act_hi[:, f, :].bitcast(F32),
                                          ALU.subtract).then_inc(act_ready.sem, 1)

                    for f in range(KD):
                        dve.tensor_tensor(y[:, f, :], x[:, f, :], rstd[:], ALU.mult).then_inc(x_scaled.sem, 1)
                        if f >= 2:
                            low(f - 2)
                    low(KD - 2)
                    low(KD - 1)

                def post_norm(nth):
                    for f in range(KD):
                        dve.wait_ge(y_sq_ready.sem, y_sq_ready.at(l, nth * KD + f + 1))
                        if f >= 1:
                            dve.tensor_tensor(sumsq[:], sq[:, 0, :] if f == 1 else sumsq[:], sq[:, f % 2, :],
                                              ALU.add).then_inc(y_sq_summed.sem, 1)
                        dve.tensor_tensor(samples(y[:, f, :]), samples(ps[:, f, :]), per_seq(nth, 2, f), ALU.mult)
                        dve.drain()
                    inverse_std(2 * nth + 1)
                    for f in range(0, KD, 2):
                        two = slice(f, f + 2)
                        dve.tensor_tensor(y[:, two, :], y[:, two, :], rstd[:].unsqueeze(1).broadcast_to([P, 2, N]), ALU.mult)
                        dve.drain()
                        dve.tensor_tensor(x[:, two, :], x[:, two, :], y[:, two, :], ALU.add).then_inc(x_ready.sem, 2)

                def hidden(u0, h0, j, s):
                    split_lo(j + (u0 + s + 1), (u0 + s + 1) % 2)
                    dve.wait_ge(silu_ready.sem, silu_ready.at(l, h0 + s + 1) + j)
                    dve.tensor_tensor(hid_f32[:], silu_g[:, s % 2, :], ps[:, 2 * (s % 2) + 1, 0:N], ALU.mult)
                    dve.drain()
                    chunk = bass.ds(j + s, 1)
                    one = hid_f32[:].rearrange("p (a n) -> p a n", a=1)
                    dve.tensor_copy(hid_hi[:, chunk, :], one)
                    dve.drain()
                    dve.tensor_tensor(hid_lo[:, chunk, :], one, hid_hi[:, chunk, :].bitcast(F32), ALU.subtract).then_inc(hidden_ready.sem, 1)
                    dve.drain()

                def four_hidden(u0, h0, j, nth, component, bias_at):
                    for s in range(4):
                        hidden(u0, h0, j, s)
                    ada(l, nth, component, bias_at)

                def proj_out(u0, units, ahead=True):
                    with dve.Fori(0, (units - 1) // 2) as i:
                        for s in range(2):
                            split_lo(i * 2 + (u0 + s + 1), (u0 + s + 1) % 2)
                    for u in range(u0 + (units - 1) // 2 * 2, u0 + units):
                        if ahead or u < u0 + units - 1:
                            split_lo(u + 1, (u + 1) % 2)

                dve.wait_ge(params_tr.sem, params_tr.at(l, 1))
                dve.tensor_copy(params_t[:, 0:P], ps[:, 6, 0:P]).then_inc(params_ready.sem, 1)
                dve.drain()
                pre_norm(0)
                split_lo(0, 0)
                with dve.Fori(0, ADA_WIN) as i:
                    four_hidden(U_F1IN, 0, i * 4, i, i + 2, i * 8 + 16)
                for component in (2, 4, 5):
                    fold_gain(component, 72 + KD * (component // 3 * 2 + (component % 3 == 2)))
                for s in range(2):
                    hidden(U_F1IN, 0, KF - 2, s)
                proj_out(U_F1OUT, KF // 2)
                post_norm(0)
                pre_norm(1)

                def w_in_unit(j, s):
                    split_lo(j + (U_WIN + s + 1), (U_WIN + s + 1) % 2)
                    dve.wait_ge(unit_used.sem, unit_used.at(l, U_WIN + s + 1) + j)
                    dve.tensor_copy(U[:, bass.ds(j * 2 + (2 * s + 1), 1), :],
                                    ps[:, 2 * (s % 2) + 1, 0:N].rearrange("p (a n) -> p a n", a=1)).then_inc(u_odd.sem, 1)

                for s in range(4):
                    w_in_unit(0, s)
                ada(l, ADA_WIN, 7, 56)
                dve.drain()
                fold_gain(7, 72 + KD * 4)
                with dve.Fori(0, 4) as i:
                    for s in range(2):
                        w_in_unit(i * 2 + 4, s)
                for n in range(1, 9, 2):
                    dve.wait_ge(tm_tr.sem, tm_tr.at(l, n + 1))
                    t, g = n // 3, n % 3
                    width = 512 if g < 2 else 256
                    dve.tensor_copy(TM[:, t, g * 512:g * 512 + width], ps[:, 4 + n % 4, 0:width]).then_inc(tm_dve.sem, 1)

                def block_diagonal(dst, tile):
                    for c in range(2):
                        for h in range(2):
                            rows = slice(64 * h, 64 * h + 64)
                            ins = dve.tensor_copy(dst[rows, c, :, 16 * h:16 * h + 16],
                                                  U[rows, tile + c, NP:N].rearrange("p (b t) -> p b t", t=S))
                    return ins

                def mix_low(phase_no, chunk):
                    for c in range(2):
                        dve.wait_ge(mix_hi.sem, mix_hi.at(l, 3 * phase_no + c + 1))
                        dve.tensor_tensor(act_lo[:, chunk + c, 0:NP], ps[:, c, 0:NP], act_hi[:, chunk + c, 0:NP].bitcast(F32),
                                          ALU.subtract).then_inc(mix_lo.sem, 1)
                    dve.wait_ge(mix_hi.sem, mix_hi.at(l, 3 * phase_no + 3))
                    for h in range(2):
                        rows = slice(64 * h, 64 * h + 64)
                        v = lambda t: t[rows, chunk:chunk + 2, NP:N].rearrange("p c (b t) -> p c b t", t=S)
                        ins = dve.tensor_tensor(v(act_lo), sample_view(rows, h), v(act_hi).bitcast(F32), ALU.subtract)
                    ins.then_inc(mix_lo.sem, 1)

                dve.wait_ge(u_even.sem, u_even.at(l, NU // 2))
                dve.memset(snT, 0.0)
                dve.memset(qc_bd[:], 0.0)
                dve.memset(qi_bd[:], 0.0)
                dve.drain()
                block_diagonal(qc_bd, QC)
                block_diagonal(qi_bd, QI)
                dve.wait_ge(tm_act.sem, tm_act.at(l, 5))
                for half in range(2):
                    ins = dve.tensor_copy(vc_new[:, half, :], TM[:, 2, TM_KV + 64:TM_KV + 128])
                ins.then_inc(bd_ready.sem, 1)
                regions = ((0, P), (P, N))
                for h in range(HA):
                    dve.wait_ge(idx_relu.sem, idx_relu.at(l, h + 1))
                    for t, (a, b) in enumerate(regions):
                        w = TM[:, t, TM_KI + WI_ROW + h:TM_KI + WI_ROW + h + 1]
                        if h == 0:
                            ins = dve.tensor_scalar(score[:, a:b], relu_p[:, 0, a:b], w, None, ALU.mult)
                        else:
                            ins = dve.scalar_tensor_tensor(out=score[:, a:b], in0=relu_p[:, h % 2, a:b], scalar=w,
                                                           in1=score[:, a:b], op0=ALU.mult, op1=ALU.add)
                    ins.then_inc(idx_summed.sem, 1)
                    dve.drain()
                dve.memset(score[0:CH, CH:P], NEG_MASKED)
                dve.memset(score[0:CH, P + 3 * CH:N], NEG_MASKED)
                dve.wait_ge(wsel_mm.sem, wsel_mm.at(l, 1))
                dve.tensor_tensor(w_sel[:].rearrange("p (i k) -> p i k", k=32), ps[:, 2, 0:P].rearrange("p (i k) -> p i k", k=32),
                                  own_step[:].unsqueeze(1).broadcast_to([P, PAIRS, 32]), ALU.mult).then_inc(wsel_ready.sem, 1)
                dve.wait_ge(score_s_mm.sem, score_s_mm.at(l, 1))
                dve.tensor_copy(score[:, N:N + PAST], ps[:, 3, 0:PAST])
                dve.tensor_tensor(score[:, N + PAST:N + NK], ps[:, 3, PAST:NK], other_seq[:], ALU.add)
                dve.drain()
                regions = ((0, P, N_SEL_P), (P, N, N_SEL_P), (N, N + NK, N_SEL_S))
                for r in range((N_SEL_P + 7) // 8):
                    src = score if r == 0 else left
                    live = [(n, a, b, k) for n, (a, b, k) in enumerate(regions) if 8 * r < k]
                    for n, a, b, k in live:
                        dve.max(small[:, 40 + 8 * n:48 + 8 * n], src[:, a:b])
                    dve.drain()
                    for n, a, b, k in live:
                        if k - 8 * r < 8:
                            dve.memset(small[:, 40 + 8 * n + k - 8 * r:48 + 8 * n], NEG_TAKEN)
                            dve.drain()
                    for n, a, b, k in live:
                        dve.match_replace(left[:, a:b], small[:, 40 + 8 * n:48 + 8 * n], src[:, a:b], NEG_TAKEN)
                    dve.drain()
                dve.tensor_scalar(off[:], left[:], TAKEN_BELOW, LOGIT_OFF, ALU.is_gt, ALU.mult).then_inc(off_ready.sem, 1)
                dve.drain()
                for h in range(HA):
                    dve.wait_ge(z_mm.sem, z_mm.at(l, h + 1))
                    dve.tensor_tensor(dsa_w[:, h, :], ps[:, 4 + h, 0:N], off[:, 0:N], ALU.add)
                dve.drain()
                dve.tensor_reduce(small[:, 8:12], dsa_w[:, :, 0:P], AX, ALU.max)
                dve.tensor_reduce(small[:, 12:16], dsa_w[:, :, P:N], AX, ALU.max)
                dve.drain()
                dve.tensor_scalar(small[:, 8:16], small[:, 8:16], -QSCALE, None, ALU.mult).then_inc(neg_max_ready.sem, 1)
                dve.wait_ge(z_mm.sem, z_mm.at(l, 5))
                dve.tensor_reduce(small[:, 16:20], ps[:, 0:PAIRS, 0:NK], AX, ALU.max)
                dve.drain()
                dve.tensor_scalar(small[:, 16:20], small[:, 16:20], -QSCALE, None, ALU.mult).then_inc(neg_max_ready.sem, 1)
                dve.wait_ge(exp_ready.sem, exp_ready.at(l, 1))
                dve.reciprocal(small[:, 24:32], small[:, 24:32])
                dve.drain()
                for t, (a, b) in enumerate(((0, P), (P, N))):
                    ins = dve.tensor_tensor(dsa_w[:, :, a:b], dsa_w[:, :, a:b],
                                            small[:, 24 + 4 * t:28 + 4 * t].unsqueeze(2).broadcast_to([P, HA, b - a]), ALU.mult)
                ins.then_inc(weights_ready.sem, 4)
                dve.wait_ge(exp_ready.sem, exp_ready.at(l, 2))
                dve.reciprocal(small[:, 32:36], small[:, 32:36])
                dve.drain()
                dve.tensor_tensor(dsa_sw[:], dsa_sw[:], small[:, 32:36].unsqueeze(2).broadcast_to([P, PAIRS, NK]),
                                  ALU.mult).then_inc(weights_ready.sem, 1)
                mix_low(0, 6)
                dve.drain()

                dve.memset(qa_bd[:], 0.0)
                dve.memset(rest[:, :, P:P + 1], 1.0)
                dve.memset(rest[:, :, N + 1:N + 2], 1.0)
                dve.memset(rest_s[:, :, NK:NK + 1], 1.0)
                dve.drain()
                block_diagonal(qa_bd, QA).then_inc(bd_ready.sem, 1)
                for h in range(HA):
                    dve.wait_ge(keep_ready.sem, keep_ready.at(l, h + 1))
                    for a in (0, 2 * P):
                        dve.tensor_tensor(keep[:, h, a:a + P], keep[:, h, a:a + P], causal[:], ALU.max)
                    dve.drain()
                    for a, b, at in ((0, P, 0), (P, N, P + 1)):
                        dve.tensor_tensor_scan(rest[:, h, at:at + b - a][:, ::-1], keep[:, h, a:b][:, ::-1], ones_row[:, 0:b - a],
                                               1.0, ALU.mult, ALU.mult)
                    dve.drain()
                    for a, b, at in ((0, P, 0), (P, N, P + 1)):
                        ins = dve.tensor_tensor(keep[:, h, a:b], rest[:, h, at + 1:at + 1 + b - a], rest[:, h, at:at + b - a], ALU.subtract)
                    ins.then_inc(weights_ready.sem, 1)
                dve.wait_ge(keep_ready.sem, keep_ready.at(l, 5))
                dve.tensor_tensor(keep_s[:, :, PAST:NK], keep_s[:, :, PAST:NK], sb_mask[:].unsqueeze(1).broadcast_to([P, PAIRS, 32]), ALU.max)
                dve.drain()
                for i in range(PAIRS):
                    dve.tensor_tensor_scan(rest_s[:, i, 0:NK][:, ::-1], keep_s[:, i, :][:, ::-1], ones_row[:, 0:NK], 1.0, ALU.mult, ALU.mult)
                dve.drain()
                dve.tensor_tensor(keep_s[:], rest_s[:, :, 1:NK + 1], rest_s[:, :, 0:NK], ALU.subtract).then_inc(weights_ready.sem, 1)
                mix_low(1, 0)

                dve.wait_ge(gate_mm.sem, gate_mm.at(l, 1))
                for c in range(2):
                    ins = dve.tensor_scalar(logdecay[:, c, :], ps[:, c, 0:N], params_t[:, 124 + c:125 + c], 0.0, ALU.add, ALU.min)
                ins.then_inc(gate_split.sem, 1)
                dve.wait_ge(softplus_ready.sem, softplus_ready.at(l, 1))
                dve.tensor_tensor(tmp_b[:], logdecay[:], tmp_a[:], ALU.subtract)
                dve.drain()
                for c in range(2):
                    dve.tensor_tensor_scan(logdecay[:, c, :], restart[:], tmp_b[:, c, :], 0.0, ALU.mult, ALU.add)
                dve.drain()
                for a, b, length in ((0, NP, LP), (NP, N, S)):
                    view = lambda t: t[:, :, a:b].rearrange("p c (n l) -> p c n l", l=length)
                    n = (b - a) // length
                    cum = view(logdecay)
                    mid = cum[:, :, :, length // 2 - 1:length // 2].broadcast_to([P, 2, n, length])
                    end = cum[:, :, :, length - 1:length].broadcast_to([P, 2, n, length])
                    dve.tensor_tensor(view(tmp_a), cum, mid, ALU.subtract)
                    ins = dve.tensor_tensor(view(tmp_b), end, cum, ALU.subtract)
                ins.then_inc(decay_ready.sem, 1)
                dve.wait_ge(decay_exp.sem, decay_exp.at(l, 1))
                q, k = U[:, QB:QB + 2, :], U[:, KB:KB + 2, :]
                dve.tensor_tensor(k_out[:], k_out[:], k, ALU.mult)
                dve.tensor_tensor(k_in[:], k_in[:], k, ALU.mult)
                dve.scalar_tensor_tensor(out=q_in[:], in0=q, scalar=QSCALE, in1=q_in[:], op0=ALU.mult, op1=ALU.mult)
                dve.scalar_tensor_tensor(out=q_dec[:], in0=q, scalar=QSCALE, in1=logdecay[:], op0=ALU.mult, op1=ALU.mult).then_inc(qk_ready.sem, 1)
                att_v = att[:].rearrange("p t (c e n) -> p t c e n", c=2, e=2)
                for kind in range(2):
                    dve.wait_ge(att_mm.sem, att_mm.at(l, kind + 1))
                    for e in range(2):
                        if kind == 0:
                            for t in range(2):
                                dve.tensor_tensor(att_v[:, t, :, e, :], ps[:, 4 + e, 256 * t:256 * t + 256].rearrange("p (c n) -> p c n", n=P),
                                                  gla_mask[:, 0, :].unsqueeze(1).broadcast_to([P, 2, P]), ALU.mult)
                        else:
                            ins = dve.tensor_tensor(att_v[:, 2, :, e, :], ps[:, 6 + e, 0:256].rearrange("p (c n) -> p c n", n=P),
                                                    gla_mask[:, 1, :].unsqueeze(1).broadcast_to([P, 2, P]), ALU.mult)
                    if kind == 1:
                        ins.then_inc(att_ready.sem, 1)
                dve.wait_ge(kv_mm.sem, kv_mm.at(l, 1))
                for n in range(NBP):
                    for c in range(2):
                        kv = ps[:, n % 4, (n // 4 * 2 + c) * P:(n // 4 * 2 + c + 1) * P]
                        if n == 0:
                            ins = dve.tensor_copy(states[:, 0, c, :], kv)
                        else:
                            end = LP * n + LP - 1
                            ins = dve.scalar_tensor_tensor(out=states[:, n, c, :], in0=states[:, n - 1, c, :],
                                                           scalar=logdecay[:, c, end:end + 1], in1=kv, op0=ALU.mult, op1=ALU.add)
                    ins.then_inc(states_ready.sem, 1)
                    dve.drain()
                dve.wait_ge(kv_mm.sem, kv_mm.at(l, 2))
                for b in range(B):
                    for c in range(2):
                        end = NP + S * b + S - 1
                        ins = dve.scalar_tensor_tensor(out=gstate_new[:, b, c, :], in0=gstate[:, b, c, :],
                                                       scalar=logdecay[:, c, end:end + 1],
                                                       in1=ps[:, b // 2, (b % 2 * 2 + c) * P:(b % 2 * 2 + c + 1) * P],
                                                       op0=ALU.mult, op1=ALU.add)
                ins.then_inc(states_ready.sem, 1)
                split_lo(U_WOUT + 1, (U_WOUT + 1) % 2)

                def gla_low(h):
                    dve.wait_ge(gla_hi.sem, gla_hi.at(l, h + 1))
                    dve.tensor_tensor(act_lo[:, 2 + h, :], gla_out[:, h, :], act_hi[:, 2 + h, :].bitcast(F32),
                                      ALU.subtract).then_inc(gla_lo.sem, 1)

                for h in range(HB):
                    dve.wait_ge(gla_std.sem, gla_std.at(l, h + 1))
                    dve.reciprocal(gla_stds[h], gla_stds[h])
                    dve.drain()
                    dve.wait_ge(gla_gated.sem, gla_gated.at(l, h + 1))
                    dve.tensor_tensor(gla_out[:, h, :], gla_out[:, h, :], gla_stds[h], ALU.mult).then_inc(gla_f32.sem, 1)
                    if h >= 1:
                        gla_low(h - 1)
                gla_low(HB - 1)

                for u in range(U_WOUT + 1, U_WOUT + KD // 2):
                    split_lo(u + 1, (u + 1) % 2)
                dve.wait_ge(rows_stored.sem, rows_stored.at(l, 10))
                dve.wait_ge(states_stored.sem, states_stored.at(l, 4))
                post_norm(1)
                pre_norm(2)
                dve.wait_ge(head_tr.sem, head_tr.at(l, 1))
                dve.tensor_copy(params_t[:, P:P + 24], ps[:, 6, 0:24])
                four_hidden(U_F2IN, KF, 0, ADA_F2, 8, 64)
                dve.drain()
                fold_gain(8, 72 + KD * 5)
                with dve.Fori(0, 2) as i:
                    four_hidden(U_F2IN, KF, i * 4 + 4, i + (ADA_F2 + 1), i, i * 8 + P)
                dve.drain()
                fold_gain(1, P + 16)
                with dve.Fori(0, (KF - 12) // 2) as i:
                    for s in range(2):
                        hidden(U_F2IN, KF, i * 2 + 12, s)
                proj_out(U_F2OUT, KF // 2, ahead=False)
                post_norm(2)

            for t in range(TT):
                dve.wait_ge(yT_mm, 2 * t + 2)
                dve.tensor_copy(tok_out[:, t, 512:1024], ps[:, 2 * t + 1, :]).then_inc(y_right, 1)

        @block.tensor
        def _(pe):
            for never_zero in (unit_used, ada_used, ada_tr, params_tr, kt_tr, gate_mm):
                never_zero.credit(pe)
            pe.wait_ge(ident_ready, 1)
            pe.wait_ge(silu_c_ready, 1)
            for f in range(KD):
                m = pe.transpose(ps[:, 4, 32 * f:32 * f + 32], c_rows[:, f * P:(f + 1) * P], ident[0:32, 0:32])
            m.then_inc(cT_mm, 1)
            pe.wait_ge(head_landed.sem, head_landed.at(0, 0))
            pe.matmul(ps[:, 5, 64:88], head, ident[0:24, 0:24], start=True, stop=True).then_inc(head_tr.sem, 1)
            pe.wait_ge(x_landed, 32)
            for f in range(KD):
                if f == 4:
                    pe.wait_ge(cT_ready, 1)
                if f == 5:
                    pe.wait_ge(head_ready, 1)
                for t in range(TT):
                    m = pe.transpose(ps[:, f, t * P:(t + 1) * P], tok_in[:, t, f * P:(f + 1) * P], ident[:])
                m.then_inc(xT_mm, 1)

            def ada_quarter(l, nth, q, first=False):
                if first:
                    pe.wait_ge(first_ada_landed[q % 2], 16 * ((nth + 2) * 2 + q // 2 + 1))
                else:
                    pe.wait_ge(ada_landed[q % 2].sem, ada_landed[q % 2].at(l, nth * 2 + (q // 2 + 1)))
                if q == 0:
                    pe.wait_ge(ada_rows_ready.sem, ada_rows_ready.at(l, nth))
                for k in range(2):
                    for g in range(4):
                        m = pe.matmul(ps[32 * g:32 * g + 32, 4, 0:256], silu_cT[:, 2 * q + k, :],
                                      w_ada_sb[q % 2][:, k, 256 * g:256 * g + 256],
                                      start=(q + k == 0), stop=(q == 3 and k == 1))
                m.then_inc(ada_used.sem, 1)

            def ada_transpose(l, nth):
                pe.wait_ge(ada_rows_ready.sem, ada_rows_ready.at(l, nth + 1))
                pe.wait_ge(mod_ready.sem, mod_ready.at(l, nth))
                for j in range(2):
                    m = pe.transpose(ps[:, 5, j * P:(j + 1) * P], ada_rows[:, j * P:(j + 1) * P], ident[:])
                m.then_inc(ada_tr.sem, 1)

            pe.wait_ge(x_ready.sem, x_ready.at(0, KD))
            for nth in (-2, -1):
                for q in range(4):
                    ada_quarter(0, nth, q, first=True)
                ada_transpose(0, nth)
            pe.wait_ge(consts_ready, 1)
            pe.matmul(ps[:, 7, 384:416], spread[0:32, :], sb_mask_c[:], start=True, stop=True)
            pe.matmul(ps[:, 7, 416:448], spread[0:32, :], ident[0:32, 0:32], start=True, stop=True).then_inc(const_mm, 1)

            with pe.Fori(0, DEPTH) as l:
                def split_ready(g):
                    pe.wait_ge(lo_ready.sem, lo_ready.at(l, 1) + g)

                def three_products(out, w, wl, a, al, first, last):
                    pe.matmul(out, w, a, start=first, stop=False)
                    pe.matmul(out, w, al, start=False, stop=False)
                    return pe.matmul(out, wl, a, start=False, stop=last)

                def mean_of_x(nth):
                    pe.wait_ge(x_sq_summed.sem, x_sq_summed.at(l, (nth + 1) * (KD - 3)))
                    pe.matmul(ps[:, 0, 0:N], ones_d[:], sumsq_pool, start=True, stop=False)
                    pe.wait_ge(x_sq_last.sem, x_sq_last.at(l, nth + 1))
                    pe.matmul(ps[:, 0, 0:N], ones_d[:], sumsq[:], start=False, stop=True).then_inc(mean_mm.sem, 1)

                def mean_of_y(nth):
                    pe.wait_ge(y_sq_summed.sem, y_sq_summed.at(l, (nth + 1) * (KD - 1)))
                    pe.matmul(ps[:, 0, 0:N], ones_d[:], sumsq[:], start=True, stop=True).then_inc(mean_mm.sem, 1)

                def column_tiles(bank, slot, ats, stride, nth):
                    for f in range(KD):
                        pe.wait_ge(act_ready.sem, act_ready.at(l, nth * KD + f + 1))
                        for half, at in enumerate(ats):
                            cols = slice(at + f * stride, at + f * stride + P)
                            m = three_products(ps[:, bank + half, 0:N], w_hi[slot][:, cols], w_lo[slot][:, cols],
                                               act_hi[:, f, :], act_lo[:, f, :], f == 0, f == KD - 1)
                    return m

                def hidden(u0, h0, norm, j, s):
                    split_ready(j + (u0 + s))
                    pe.wait_ge(hidden_ready.sem, hidden_ready.at(l, h0 + s - 1) + j)
                    column_tiles(2 * (s % 2), (u0 + s) % 2, (0, 1024), P, norm).then_inc(unit_used.sem, 1)

                def four_hidden(u0, h0, norm, j, nth):
                    for s in range(4):
                        ada_quarter(l, nth, s)
                        hidden(u0, h0, norm, j, s)
                    ada_transpose(l, nth)

                def proj_out(u0, units, src_hi, src_lo, h0=None):
                    def products(slot, chunk, kc, o, first, last):
                        cols = slice(kc * 1024 + o * P, kc * 1024 + o * P + P)
                        return three_products(ps[:, o:o + 1, 0:N], w_hi[slot][:, cols], w_lo[slot][:, cols],
                                              src_hi[:, bass.ds(chunk, 1), :], src_lo[:, bass.ds(chunk, 1), :], first, last)

                    split_ready(u0)
                    order = (4, 5, 6, 7, 0, 1, 2, 3) if h0 is not None else range(KD)
                    for kc in range(2):
                        for n, o in enumerate(order):
                            if kc == 0 and h0 is not None and n in (0, 4):
                                pe.wait_ge(hidden_ready.sem, hidden_ready.at(l, h0 + (KF - 2 if n == 0 else KF)))
                            m = products(u0 % 2, kc, kc, o, kc == 0, False)
                    m.then_inc(unit_used.sem, 1)
                    pairs = (units - 2) // 2
                    with pe.Fori(0, pairs) as i:
                        for s in range(2):
                            split_ready(i * 2 + (u0 + 1 + s))
                            for kc in range(2):
                                for o in range(KD):
                                    m = products((u0 + 1 + s) % 2, i * 4 + (2 + 2 * s + kc), kc, o, False, False)
                            m.then_inc(unit_used.sem, 1)
                    for u in range(1 + 2 * pairs, units - 1):
                        split_ready(u0 + u)
                        for kc in range(2):
                            for o in range(KD):
                                m = products((u0 + u) % 2, 2 * u + kc, kc, o, False, False)
                        m.then_inc(unit_used.sem, 1)
                    u = units - 1
                    split_ready(u0 + u)
                    for o in range(KD):
                        for kc in range(2):
                            m = products((u0 + u) % 2, 2 * u + kc, kc, o, False, kc == 1)
                        if o < KD - 1:
                            m.then_inc(proj_done.sem, 1)
                    m.then_inc(unit_used.sem, 1)

                pe.wait_ge(x_ready.sem, x_ready.at(l, KD))
                pe.wait_ge(params_landed.sem, params_landed.at(l, 1))
                pe.transpose(ps[:, 6, 0:P], params[:], ident[:]).then_inc(params_tr.sem, 1)
                mean_of_x(0)
                with pe.Fori(0, ADA_WIN) as i:
                    four_hidden(U_F1IN, 0, 0, i * 4, i)
                for s in range(2):
                    hidden(U_F1IN, 0, 0, KF - 2, s)
                proj_out(U_F1OUT, KF // 2, hid_hi, hid_lo, 0)
                mean_of_y(0)
                mean_of_x(1)

                def w_in_unit(j, s):
                    split_ready(j + (U_WIN + s))
                    pe.wait_ge(u_even.sem, u_even.at(l, s - 1) + j)
                    pe.wait_ge(u_odd.sem, u_odd.at(l, s - 1) + j)
                    column_tiles(2 * (s % 2), (U_WIN + s) % 2, (0, P), 256, 1).then_inc(unit_used.sem, 1)

                for s in range(4):
                    ada_quarter(l, ADA_WIN, s)
                    w_in_unit(0, s)
                ada_transpose(l, ADA_WIN)
                with pe.Fori(0, 4) as i:
                    for s in range(2):
                        w_in_unit(i * 2 + 4, s)

                pe.wait_ge(u_even.sem, u_even.at(l, NU // 2))
                pe.wait_ge(u_odd.sem, u_odd.at(l, NU // 2))
                for n in range(9):
                    t, g = n // 3, n % 3
                    if n >= 4:
                        if n % 2 == 0:
                            pe.wait_ge(tm_act.sem, tm_act.at(l, (n - 4) // 2 + 1))
                        else:
                            pe.wait_ge(tm_dve.sem, tm_dve.at(l, (n - 4) // 2 + 1))
                    for j, tile in enumerate(TM_TILES[4 * g:4 * g + 4]):
                        m = pe.transpose(ps[:, 4 + n % 4, j * P:(j + 1) * P], U[:, tile, t * P:(t + 1) * P], ident[:])
                    m.then_inc(tm_tr.sem, 1)
                for n, tile in enumerate((KV, KI)):
                    pe.matmul(ps[:, n, 0:N], dup_eye[0:64, :], U[0:64, tile, :], start=True, stop=True).then_inc(dup_mm.sem, 1)

                def keys_T(phase_no):
                    pe.wait_ge(k_cache_landed.sem, k_cache_landed.at(l, 5))
                    for g in range(4):
                        if phase_no == 0:
                            bank = (2, 3, 0, 1)[g]
                            if g >= 2:
                                pe.wait_ge(dup_ready.sem, dup_ready.at(l, g - 1))
                        else:
                            bank = g
                        for j in range(4):
                            b = 4 * (g % 2) + j
                            if phase_no == 0:
                                src = (kc_raw, ki_raw)[g // 2][:, b, :, :].rearrange("p a d -> p (a d)")
                            else:
                                src = k_sb_raw[:, b, P * (g // 2):P * (g // 2) + P]
                            m = pe.transpose(ps[:, bank, j * P:(j + 1) * P], src, ident[:])
                        m.then_inc(kt_tr.sem, 1)
                    pe.wait_ge(kt_ready.sem, kt_ready.at(l, 4 * phase_no + 4))

                def scores_prompt(h, q_tile, key, done):
                    rows = slice(64 * (h % 2), 64 * (h % 2) + 64)
                    c = h // 2
                    pe.matmul(ps[:, 4 + h, 0:P], U[rows, q_tile + c, 0:P], key(c)[rows, 0:P], start=True, stop=True)
                    pe.matmul(ps[:, 4 + h, P:N], U[rows, q_tile + c, P:NP], key(c)[rows, 0:NP], start=True, stop=True).then_inc(done.sem, 1)

                def scores_samples(q_bd, past, new, mask=None):
                    for i in range(PAIRS):
                        bank, at = (i, 0) if mask is not None else ((0, NK * i) if i < 3 else (1, 0))
                        if mask is not None:
                            pe.matmul(ps[:, bank, at:at + NK], spread[32 * i:32 * i + 32, :], mask[32 * i:32 * i + 32, N:N + NK],
                                      start=True, stop=False, skip_group_check=True)
                        first = mask is None
                        for b2 in range(2):
                            b = 2 * i + b2
                            for c in range(2):
                                out = ps[64 * b2 + 32 * c:64 * b2 + 32 * c + 32, bank, at:at + NK]
                                pe.matmul(out[:, 0:PAST], q_bd[:, c, b, :], past(c, b), start=first, stop=True, skip_group_check=True)
                                m = pe.matmul(out[:, PAST:NK], q_bd[:, c, b, :], new(c, i), start=first, stop=True, skip_group_check=True)
                    return m

                def attend_tail(phase_no, w, sw, wT, swT, v_prompt, v_past, v_new, per_pair):
                    for h in range(HA):
                        pe.wait_ge(weights_ready.sem, weights_ready.at(l, 5 * phase_no + h + 1))
                        for j in range(3):
                            m = pe.transpose(ps[:, 4 + h, j * P:(j + 1) * P], w[:, h, j * P:(j + 1) * P], ident[:])
                        m.then_inc(wt_tr.sem, 1)
                    pe.wait_ge(weights_ready.sem, weights_ready.at(l, 5 * phase_no + 5))
                    for i in range(PAIRS):
                        m = pe.transpose(ps[:, 2, i * P:(i + 1) * P], sw[:, i, 0:PAST], ident[:])
                    m.then_inc(wt_tr.sem, 1)
                    for i in range(PAIRS):
                        m = pe.matmul(ps[32 * i:32 * i + 32, 3, 0:P], sw[:, i, PAST:NK], ident[:], start=True, stop=True)
                    m.then_inc(wt_tr.sem, 1)
                    for c in range(2):
                        for h2 in range(2):
                            h = 2 * c + h2
                            pe.wait_ge(wt_ready.sem, wt_ready.at(l, 6 * phase_no + h + 1))
                            out = ps[64 * h2:64 * h2 + 64, c, :]
                            pe.matmul(out[:, 0:P], v_prompt(0, h), wT[:, h, 0:P], start=True, stop=True)
                            pe.matmul(out[:, P:NP], v_prompt(0, h), wT[:, h, P:2 * P], start=True, stop=False)
                            m = pe.matmul(out[:, P:NP], v_prompt(1, h), wT[:, h, 2 * P:N], start=False, stop=True)
                        m.then_inc(pv_mm.sem, 1)
                    pe.wait_ge(wt_ready.sem, wt_ready.at(l, 6 * phase_no + 6))
                    for b in range(B):
                        i, b2 = b // 2, b % 2
                        for c in range(2 if per_pair else 1):
                            width = 32 if per_pair else 64
                            cols = slice(64 * b2 + 32 * c, 64 * b2 + 32 * c + width)
                            out = ps[:, 4, 64 * b + 32 * c:64 * b + 32 * c + width]
                            pe.matmul(out, v_past(c, b), swT[:, i, cols], start=True, stop=False)
                            m = pe.matmul(out, v_new(c), snT[:, i, cols], start=False, stop=True)
                    m.then_inc(pv_mm.sem, 1)

                keys_T(0)
                pe.wait_ge(tm_act.sem, tm_act.at(l, 5))
                pe.wait_ge(tm_dve.sem, tm_dve.at(l, 4))
                for h in range(HA):
                    scores_prompt(h, QI, lambda c: ki_dup, idx_mm)
                pe.wait_ge(bd_ready.sem, bd_ready.at(l, 1))
                scores_samples(qi_bd, lambda c, b: kiT[:, b, :], lambda c, i: ki_dup[:, NP + 32 * i:NP + 32 * i + 32]).then_inc(idx_s_mm.sem, 1)
                pe.matmul(ps[:, 2, 0:P], head_rows[WI_ROW:WI_ROW + 4, :], U[WI_ROW:WI_ROW + 4, KI, NP:N], start=True, stop=True).then_inc(wsel_mm.sem, 1)
                pe.wait_ge(wsel_ready.sem, wsel_ready.at(l, 1))
                pe.wait_ge(idx_s_relu.sem, idx_s_relu.at(l, 1))
                for i in range(PAIRS):
                    m = pe.matmul(ps[32 * i:32 * i + 32, 3, 0:NK], w_sel[:, 32 * i:32 * i + 32], relu_s[:, i, :], start=True, stop=True)
                m.then_inc(score_s_mm.sem, 1)
                pe.wait_ge(idx_relu.sem, idx_relu.at(l, HA))
                for h in range(HA):
                    scores_prompt(h, QC, lambda c: kc_dup, z_mm)
                pe.wait_ge(off_ready.sem, off_ready.at(l, 1))
                scores_samples(qc_bd, lambda c, b: kcT[:, b, :], lambda c, i: kc_dup[:, NP + 32 * i:NP + 32 * i + 32], off).then_inc(z_mm.sem, 1)
                pe.wait_ge(v_cache_landed[0].sem, v_cache_landed[0].at(l, 2))
                attend_tail(0, dsa_w, dsa_sw, dsa_wT, dsa_swT,
                            lambda t, h: TM[:, t, TM_KV + 64:TM_KV + 128],
                            lambda c, b: vc_past[:, b, :, :].rearrange("p a d -> p (a d)"),
                            lambda c: vc_new[:].rearrange("p a d -> p (a d)"), False)

                pe.wait_ge(mix_lo.sem, mix_lo.at(l, 3))
                keys_T(1)
                for h in range(HA):
                    scores_prompt(h, QA, lambda c: U[:, KA + c, :], z_mm)
                pe.wait_ge(bd_ready.sem, bd_ready.at(l, 2))
                scores_samples(qa_bd, lambda c, b: kaT[:, c, b, :], lambda c, i: U[:, KA + c, NP + 32 * i:NP + 32 * i + 32]).then_inc(z_mm.sem, 1)
                pe.wait_ge(v_cache_landed[1].sem, v_cache_landed[1].at(l, 1))
                attend_tail(1, keep, keep_s, sb_wT, sb_swT,
                            lambda t, h: TM[:, t, TM_VA + 64 * h:TM_VA + 64 * h + 64],
                            lambda c, b: va_past[:, b, P * c:P * c + P],
                            lambda c: TM[:, 2, TM_VA + P * c:TM_VA + P * c + P], True)

                pe.wait_ge(mix_lo.sem, mix_lo.at(l, 6))
                for c in range(2):
                    m = pe.matmul(ps[:, c, 0:N], w_gate_sb[GB_ROW:GB_ROW + RANK, c * P:(c + 1) * P], U[GB_ROW:GB_ROW + RANK, KI, :],
                                  start=True, stop=True)
                m.then_inc(gate_mm.sem, 1)
                pe.wait_ge(qk_ready.sem, qk_ready.at(l, 1))
                for t in range(TT):
                    for c in range(2):
                        m = pe.transpose(ps[:, 2 + t // 2, (t % 2 * 2 + c) * P:(t % 2 * 2 + c + 1) * P], k_out[:, c, t * P:(t + 1) * P], ident[:])
                m.then_inc(krow_tr.sem, 1)
                for kind, tiles in enumerate(((0, 1), (2,))):
                    for t in tiles:
                        for h in range(HB):
                            e, c = h % 2, h // 2
                            rows = slice(64 * e, 64 * e + 64)
                            at = (t % 2 * 2 + c) * P
                            m = pe.matmul(ps[:, 4 + 2 * kind + e, at:at + P], k_in[rows, c, t * P:(t + 1) * P], q_in[rows, c, t * P:(t + 1) * P],
                                          start=True, stop=True)
                    m.then_inc(att_mm.sem, 1)
                pe.wait_ge(krow_ready.sem, krow_ready.at(l, 1))
                for half in range(NBP // 4):
                    for c in range(2):
                        for e in range(2):
                            for g in range(4):
                                rows = slice(LP * g, LP * g + LP)
                                at = (half * 2 + c) * P
                                m = pe.matmul(ps[64 * e:64 * e + 64, g, at:at + P], k_rows[rows, half, P * c + 64 * e:P * c + 64 * e + 64],
                                              TM[rows, half, TM_VB + (2 * c + e) * P:TM_VB + (2 * c + e + 1) * P], start=True, stop=True)
                m.then_inc(kv_mm.sem, 1)
                pe.wait_ge(att_ready.sem, att_ready.at(l, 1))
                pe.wait_ge(gstate_landed.sem, gstate_landed.at(l, 2))
                for c in range(2):
                    for t in range(TT):
                        for e in range(2):
                            h = 2 * c + e
                            pe.matmul(ps[:, 4 + h, t * P:(t + 1) * P], TM[:, t, TM_VB + h * P:TM_VB + (h + 1) * P],
                                      att[:, t, h * P:(h + 1) * P], start=(t == 0), stop=False, skip_group_check=True)
                    for b in range(B):
                        cols = slice(NP + S * b, NP + S * b + S)
                        for e in range(2):
                            rows = slice(64 * e, 64 * e + 64)
                            pe.matmul(ps[:, 4 + 2 * c + e, cols], gstate[rows, b, c, :], q_dec[rows, c, cols],
                                      start=False, stop=False, skip_group_check=True)
                pe.wait_ge(states_ready.sem, states_ready.at(l, NBP))
                for b2 in range(2):
                    for c in range(2):
                        for e in range(2):
                            for g in range(PAIRS):
                                rows = slice(32 * g, 32 * g + 32)
                                at = (b2 * 2 + c) * P
                                m = pe.matmul(ps[64 * e:64 * e + 64, g, at:at + P], k_rows[rows, 2 + b2, P * c + 64 * e:P * c + 64 * e + 64],
                                              TM[rows, 2, TM_VB + (2 * c + e) * P:TM_VB + (2 * c + e + 1) * P], start=True, stop=True)
                m.then_inc(kv_mm.sem, 1)
                for c in range(2):
                    for n in range(1, NBP):
                        cols = slice(LP * n, LP * n + LP)
                        for e in range(2):
                            rows = slice(64 * e, 64 * e + 64)
                            m = pe.matmul(ps[:, 4 + 2 * c + e, cols], states[rows, n - 1, c, :], q_dec[rows, c, cols],
                                          start=False, stop=(n == NBP - 1), skip_group_check=True)
                            if n == NBP - 1:
                                m.then_inc(gla_mm.sem, 1)
                pe.wait_ge(states_ready.sem, states_ready.at(l, NBP + 1))
                for h in range(HB):
                    pe.wait_ge(gla_sq.sem, gla_sq.at(l, h + 1))
                    pe.matmul(ps[:, h, 0:N], ones_v[:], gla_sqs[h], start=True, stop=True).then_inc(gla_mean_mm.sem, 1)

                pe.wait_ge(gla_std.sem, gla_std.at(l, HB))
                for u, chunk in enumerate(WOUT_CHUNKS):
                    split_ready(U_WOUT + u)
                    slot = (U_WOUT + u) % 2
                    if chunk in (2, 4):
                        pe.wait_ge(gla_lo.sem, gla_lo.at(l, chunk))
                    last = u == KD // 2 - 1
                    for a, b in ((a, b) for a in range(KD if last else 2) for b in range(2 if last else KD)):
                        kc, o = (b, a) if last else (a, b)
                        cols = slice(kc * 1024 + o * P, kc * 1024 + o * P + P)
                        m = three_products(ps[:, o, 0:N], w_hi[slot][:, cols], w_lo[slot][:, cols],
                                           act_hi[:, chunk + kc, :], act_lo[:, chunk + kc, :], u == 0 and kc == 0, last and kc == 1)
                        if last and kc == 1 and o < KD - 1:
                            m.then_inc(proj_done.sem, 1)
                    m.then_inc(unit_used.sem, 1)
                mean_of_y(1)
                mean_of_x(2)
                pe.wait_ge(head_landed.sem, head_landed.at(l, 1))
                pe.matmul(ps[:, 6, 0:24], head, ident[0:24, 0:24], start=True, stop=True).then_inc(head_tr.sem, 1)
                four_hidden(U_F2IN, KF, 2, 0, ADA_F2)
                with pe.Fori(0, 2) as i:
                    four_hidden(U_F2IN, KF, 2, i * 4 + 4, i + (ADA_F2 + 1))
                with pe.Fori(0, (KF - 12) // 2) as i:
                    for s in range(2):
                        hidden(U_F2IN, KF, 2, i * 2 + 12, s)
                proj_out(U_F2OUT, KF // 2, hid_hi, hid_lo, KF)
                mean_of_y(2)

            for t in range(TT):
                if t == 0:
                    pe.wait_ge(x_ready.sem, x_ready.at(DEPTH, KD))
                for f in range(KD):
                    m = pe.transpose(ps[:, 2 * t + f // 4, (f % 4) * P:(f % 4 + 1) * P], x[:, f, t * P:(t + 1) * P], ident[:])
                    if f % 4 == 3:
                        m.then_inc(yT_mm, 1)


_INS = ['x_prompt', 'x_sample', 'cache_k_sb', 'cache_v_sb', 'cache_k_dsa', 'cache_v_dsa', 'cache_k_idx', 'state_gla',
        'c_prompt', 'c_sample', 'w_ada', 'b_ada', 'norm_gains', 'w_ffn1_in', 'w_ffn1_out', 'w_ffn2_in', 'w_ffn2_out',
        'w_in', 'w_gla_gate', 'b_gla_gate', 'gla_norm', 'w_out']
_OUTS = [('y_prompt', (1, 256, 1024)), ('y_sample', (8, 16, 1024)),
         ('new_k_sb_p', (2, 1, 256, 4, 64)), ('new_v_sb_p', (2, 1, 256, 4, 64)),
         ('new_k_dsa_p', (2, 1, 256, 64)), ('new_v_dsa_p', (2, 1, 256, 64)), ('new_k_idx_p', (2, 1, 256, 64)),
         ('new_gla_p', (2, 1, 4, 64, 128)),
         ('new_k_sb_s', (2, 8, 16, 4, 64)), ('new_v_sb_s', (2, 8, 16, 4, 64)),
         ('new_k_dsa_s', (2, 8, 16, 64)), ('new_v_dsa_s', (2, 8, 16, 64)), ('new_k_idx_s', (2, 8, 16, 64)),
         ('new_gla_s', (2, 8, 4, 64, 128))]


def kernel(**inputs):
    import numpy as _np
    import concourse.bacc as _bacc
    from concourse import mybir as _mybir
    from concourse.bass_utils import run_bass_kernel_spmd as _run

    nc = _bacc.Bacc("TRN2", target_bir_lowering=False, num_devices=1)
    arrays, tensors = {}, {}
    for name in _INS:
        a = _np.ascontiguousarray(inputs[name])
        arrays[f"in_{name}_dram"] = a
        tensors[name] = nc.dram_tensor(f"in_{name}_dram", a.shape, _mybir.dt.from_np(a.dtype), kind="ExternalInput").ap()
    for name, shape in _OUTS:
        tensors[name] = nc.dram_tensor(f"out_{name}_dram", shape, _mybir.dt.float32, kind="ExternalOutput").ap()
    encoder_program(nc, tensors)
    r = _run(nc, [arrays], core_ids=[0])
    return tuple(r.results[0][f"out_{name}_dram"] for name, _ in _OUTS)
```

```python
from contextlib import ExitStack

import concourse.bass as bass
from concourse import mybir

ALU = mybir.AluOpType
ACT = mybir.ActivationFunctionType
F32 = mybir.dt.float32
F32R = mybir.dt.float32r
AX = mybir.AxisListType.X

P = 128
EPS = 1e-6
MACARON_W = 0.5
GATE_TAU = 16.0
NEG_MASKED = -3.0e38
NEG_TAKEN = -3.4e38
TAKEN_BELOW = -3.3e38
LOGIT_OFF = -1.0e30


class Signal:

    def __init__(self, ctx, nc, name, per_layer, step=1, start=0, before=0):
        self.sem = ctx.enter_context(nc.semaphore(name))
        self.per_layer, self.step, self.start, self.before = per_layer, step, start, before

    def credit(self, engine):
        engine.sem_inc(self.sem, self.start)

    def at(self, layer, n):
        return layer * (self.per_layer * self.step) + (n * self.step + (self.start + self.before * self.step))


def encoder_program(nc, T):
    x_prompt, x_sample = T["x_prompt"], T["x_sample"]
    _, SEQ, D = x_prompt.shape
    B, S, _ = x_sample.shape
    DEPTH, _, PAST, HA, DH = T["cache_k_sb"].shape
    HB, DK, DV = T["state_gla"].shape[2:]
    FF = T["w_ffn1_out"].shape[1]
    RANK = T["w_gla_gate"].shape[1]
    NSEQ = 1 + B
    DIN = T["w_in"].shape[2]
    N_SEL_P = SEQ // 4
    N_SEL_S = (PAST + S) // 4
    QSCALE = float(DH) ** -0.5

    NP, NS = SEQ, B * S
    N = NP + NS
    TT = N // P
    KD = D // P
    KF = FF // P
    CH = 64
    LP = 32
    NBP = NP // LP
    NK = PAST + 2 * S
    PAIRS = B // 2
    assert (D, N, NP, NS, PAST, S, B, DH, DV, DK, HA, HB) == (1024, 384, 256, 128, 128, 16, 8, 64, 128, 64, 4, 4)

    C_RB_END = 2304
    C_GB, C_QC, C_KV, C_QI, C_KI = C_RB_END, C_RB_END + RANK, C_RB_END + RANK + 256, C_RB_END + RANK + 384, C_RB_END + RANK + 640
    assert C_KI + 68 == DIN
    QA, KA, VA, QB, KB, VB, RB, QC, QI, KV, KI = 0, 2, 4, 6, 8, 10, 14, 18, 20, 22, 23
    NU = 24
    GB_ROW = 96
    WI_ROW = 64
    WIN_TILES = (KV, QI, QC, QA, KA, VA, QB, KB, VB, VB + 2, RB, RB + 2)
    TM_TILES = [KA, KA + 1, VA, VA + 1, VB, VB + 1, VB + 2, VB + 3, KV, KI]
    TM_KA, TM_VA, TM_VB, TM_KV, TM_KI = 0, 256, 512, 1024, 1152
    TM_W = 128 * len(TM_TILES)

    U_F1IN, U_F1OUT = 0, KF
    U_WIN = U_F1OUT + KF // 2
    U_WOUT = U_WIN + NU // 2
    U_F2IN = U_WOUT + KD // 2
    U_F2OUT = U_F2IN + KF
    UNITS = U_F2OUT + KF // 2
    assert UNITS % 2 == 0
    WOUT_CHUNKS = (0, 6, 2, 4)
    N_ADA = 9
    ADA_LAST1, ADA_F2 = 5, 6
    assert DEPTH == 2
    NEXT = DEPTH - 1

    with ExitStack() as ctx:
        base = (nc.sbuf_base + 63) // 64 * 64
        cursor = [base]

        def place(name, shape, dt=F32, at=None):
            size = 4
            for n in shape[1:]:
                size *= n
            size = (size + 31) // 32 * 32
            if at is None:
                at = cursor[0]
                cursor[0] += size
            return nc.alloc_sbuf_tensor_at(name, shape, dt, offset=at)

        x = place("x", [P, KD, N])
        act_hi = place("act_hi", [P, KD, N], F32R)
        act_lo = place("act_lo", [P, KD, N], F32R)
        w_raw = [place(f"w_raw{i}", [P, 2048]) for i in range(2)]
        w_hi = [place(f"w_hi{i}", [P, 2048], F32R) for i in range(2)]
        w_lo = [place(f"w_lo{i}", [P, 2048], F32R) for i in range(2)]
        stage_at = cursor[0]
        w_ada_sb = [place(f"w_ada_sb{i}", [P, 2, 1024]) for i in range(2)]
        stage_end = cursor[0]
        mod = place("mod", [P, 9, KD, NSEQ])
        silu_cT = place("silu_cT", [P, KD, 32])
        params = place("params", [P, P])
        w_gate_sb = place("w_gate_sb", [P, 256])
        head = w_gate_sb[0:24, 0:P]
        params_t = place("params_t", [P, P + 24])
        ident = place("ident", [P, P])
        ones_d = place("ones_d", [P, P])
        ones_v = place("ones_v", [P, P])
        causal = place("causal", [P, P])
        gla_mask = place("gla_mask", [P, 2, P])
        restart = place("restart", [P, N])
        dup_eye = place("dup_eye", [P, P])
        spread = place("spread", [P, P])
        sb_mask_c = place("sb_mask_c", [32, 32])
        sb_mask = place("sb_mask", [P, 32])
        own_step = place("own_step", [P, 32])
        head_rows = place("head_rows", [P, P])
        other_seq = place("other_seq", [P, 32])
        parity = place("parity", [P, 2])
        ones_row = place("ones_row", [P, 256])
        rstd = place("rstd", [P, N])
        sq = place("sq", [P, 2, N])
        sumsq = place("sumsq", [P, N])
        scaled = place("scaled", [P, N])
        cumdecay = place("cumdecay", [P, 2, N])
        ada_rows = place("ada_rows", [P, 256])
        small = place("small", [P, 64])
        gate_low = [rstd[:], sumsq[:]]
        snT = sq[:].rearrange("p a n -> p (a n)")[:, 0:PAIRS * P].rearrange("p (i r) -> p i r", r=P)
        arena = cursor[0]

        def overlay(offset):
            at = [arena + offset]

            def put(name, shape, dt=F32):
                size = 4
                for n in shape[1:]:
                    size *= n
                t = nc.alloc_sbuf_tensor_at(name, shape, dt, offset=at[0])
                at[0] += (size + 31) // 32 * 32
                assert at[0] <= nc.sbuf_usable_end, (name, at[0] - nc.sbuf_usable_end)
                return t
            return put

        put = overlay(0)
        hid_hi = put("hid_hi", [P, KF, N], F32R)
        hid_lo = put("hid_lo", [P, KF, N], F32R)
        y = put("y", [P, KD, N])
        silu_g = put("silu_g", [P, 2, N])
        hid_f32 = put("hid_f32", [P, N])
        put = overlay(0)
        tok_in = put("tok_in", [P, TT, D])
        c_rows = put("c_rows", [32, D])
        put = overlay(0)
        tok_out = put("tok_out", [P, TT, D])
        put = overlay(0)
        U = put("U", [P, NU, N])
        TM = put("TM", [P, TT, TM_W])
        kc_dup = put("kc_dup", [P, N])
        ki_dup = put("ki_dup", [P, N])
        phase = NU * N * 4 + TT * TM_W * 4 + 2 * N * 4
        tile_at = lambda u: u * N * 4
        k_sb_raw = nc.alloc_sbuf_tensor_at("k_sb_raw", [P, B, 2 * P], F32, offset=stage_at)
        kc_raw = nc.alloc_sbuf_tensor_at("kc_raw", [P, B, 2, DH], F32, offset=stage_at + 8192)
        ki_raw = nc.alloc_sbuf_tensor_at("ki_raw", [P, B, 2, DH], F32, offset=stage_at + 12288)
        assert stage_end - stage_at == 16384
        put = overlay(phase)
        kcT = put("kcT", [P, B, P])
        kiT = put("kiT", [P, B, P])
        vc_past = put("vc_past", [P, B, 2, DH])
        qc_bd = put("qc_bd", [P, 2, B, 32])
        qi_bd = put("qi_bd", [P, 2, B, 32])
        vc_new = put("vc_new", [P, 2, DH])
        score_at = [phase + 4096 * 3 + 2048 * 2 + 512]
        score = put("score", [P, N + NK])
        left = put("left", [P, N + NK])
        off = put("off", [P, N + NK])
        dsa_at = score_at[0] + 3 * (N + NK) * 4
        dsa_w = put("dsa_w", [P, HA, N])
        put = overlay(dsa_at)
        relu_p = put("relu_p", [P, 2, N])
        relu_s = put("relu_s", [P, PAIRS, NK])
        w_sel = scaled[:, 0:P]
        put = overlay(score_at[0])
        dsa_swT = put("dsa_swT", [P, PAIRS, P])
        put = overlay(tile_at(VA))
        dsa_sw = put("dsa_sw", [P, PAIRS, NK])
        put = overlay(tile_at(VB))
        dsa_wT = put("dsa_wT", [P, HA, N])
        put = overlay(phase)
        kaT = put("kaT", [P, 2, B, P])
        va_past = put("va_past", [P, B, 2 * P])
        qa_bd = put("qa_bd", [P, 2, B, 32])
        rest = put("rest", [P, HA, N + 2])
        put_wT = overlay(phase + 8192 * 2 + 2048)
        sb_wT = put_wT("sb_wT", [P, HA, N])
        rest_s = put("rest_s", [P, PAIRS, NK + 1])
        sb_swT = put("sb_swT", [P, PAIRS, P])
        put = overlay(tile_at(VA))
        keep_s = put("keep_s", [P, PAIRS, NK])
        put = overlay(tile_at(VB))
        keep = put("keep", [P, HA, N])
        put = overlay(phase)
        gstate = put("gstate", [P, B, 2, DV])
        gstate_new = put("gstate_new", [P, B, 2, DV])
        gla_out = put("gla_out", [P, HB, N])
        k_rows = put("k_rows", [P, 4, 256])
        gla_sqs = [sq[:, 0, :], sq[:, 1, :], kc_dup[:], ki_dup[:]]
        gla_stds = [rstd[:], sumsq[:], scaled[:], cumdecay[:, 1, :]]
        put = overlay(tile_at(QA))
        att = put("att", [P, TT, HB * P])
        put = overlay(phase - 2 * N * 4)
        k_in = put("k_in", [P, 2, N])
        k_out = U[:, QC:QC + 2, :]
        q_in = U[:, QI:QI + 2, :]
        q_dec = U[:, QB:QB + 4, :].rearrange("p (c e) n -> p c e n", e=2)
        decay = cumdecay
        put = overlay(tile_at(QC))
        states = put("states", [P, NBP, 2, DV])

        ps = ctx.enter_context(nc.psum_tensor("ps", [P, 8, 512], F32))

        def sig(name, per_layer, step=1, start=0, before=0):
            return Signal(ctx, nc, name, per_layer, step, start, before)

        sem = lambda name: ctx.enter_context(nc.semaphore(name))
        x_landed = sem("x_landed")
        c_zeroed = sem("c_zeroed")
        c_landed = sem("c_landed")
        ident_ready = sem("ident_ready")
        consts_ready = sem("consts_ready")
        silu_c_ready = sem("silu_c_ready")
        cT_mm = sem("cT_mm")
        cT_ready = sem("cT_ready")
        const_mm = sem("const_mm")
        masks_ready = sem("masks_ready")
        head_ready = sem("head_ready")
        xT_mm = sem("xT_mm")
        raw_landed = [sig(f"raw_landed{i}", UNITS // 2, 32) for i in range(2)]
        gate_cols_landed = sig("gate_cols_landed", 1, 16)
        params_landed = sig("params_landed", 1, 5 * 16)
        hi_ready = sig("hi_ready", UNITS)
        lo_ready = sig("lo_ready", UNITS, start=2)
        unit_used = sig("unit_used", UNITS, start=2)
        ada_landed = [sig(f"ada_landed{i}", N_ADA * 2, 16) for i in range(2)]
        first_ada_landed = [sem(f"first_ada_landed{i}") for i in range(2)]
        ada_used = sig("ada_used", N_ADA * 4, start=2, before=8)
        head_landed = sig("head_landed", 1, 32, before=1)
        head_tr = sig("head_tr", 1, before=1)
        ada_rows_ready = sig("ada_rows_ready", N_ADA, start=1, before=2)
        ada_tr = sig("ada_tr", N_ADA, start=1, before=2)
        mod_ready = sig("mod_ready", N_ADA, start=1, before=2)
        params_tr = sig("params_tr", 1, start=1)
        params_ready = sig("params_ready", 1)
        silu_ready = sig("silu_ready", 2 * KF)
        hidden_ready = sig("hidden_ready", 2 * KF, start=2)
        proj_done = sig("proj_done", 3 * (KD - 1))
        y_sq_ready = sig("y_sq_ready", 3 * KD)
        y_sq_summed = sig("y_sq_summed", 3 * (KD - 1))
        x_sq_ready = sig("x_sq_ready", 3 * KD)
        x_scaled = sig("x_scaled", 3 * KD)
        samples_ready = sig("samples_ready", 3 * KD)
        mean_mm = sig("mean_mm", 6)
        std_ready = sig("std_ready", 6)
        x_ready = sig("x_ready", 3 * KD)
        act_hi_ready = sig("act_hi_ready", 3 * KD)
        act_ready = sig("act_ready", 3 * KD)
        u_even = sig("u_even", NU // 2, start=2)
        u_odd = sig("u_odd", NU // 2, start=2)
        kvi_tr = sig("kvi_tr", 1)
        kvi_ready = sig("kvi_ready", 1)
        tm_tr = sig("tm_tr", 6)
        tm_act = sig("tm_act", 3)
        tm_dve = sig("tm_dve", 3)
        dup_mm = sig("dup_mm", 2)
        dup_ready = sig("dup_ready", 2)
        k_cache_landed = sig("k_cache_landed", 5, 16)
        v_cache_landed = [sig(f"v_cache_landed{i}", n, 16) for i, n in enumerate((2, 1))]
        gstate_landed = sig("gstate_landed", 2, 16)
        kt_tr = sig("kt_tr", 8, start=1)
        kt_ready = sig("kt_ready", 8)
        bd_ready = sig("bd_ready", 2)
        idx_mm = sig("idx_mm", HA)
        idx_relu = sig("idx_relu", HA)
        idx_summed = sig("idx_summed", HA, start=2)
        idx_s_mm = sig("idx_s_mm", 1)
        idx_s_relu = sig("idx_s_relu", 1)
        wsel_mm = sig("wsel_mm", 1)
        wsel_ready = sig("wsel_ready", 1)
        score_s_mm = sig("score_s_mm", 1)
        score_s_read = sig("score_s_read", 1)
        off_ready = sig("off_ready", 1)
        z_mm = sig("z_mm", 10)
        neg_max_ready = sig("neg_max_ready", 2)
        exp_ready = sig("exp_ready", 2)
        keep_ready = sig("keep_ready", 5)
        weights_ready = sig("weights_ready", 10)
        wt_tr = sig("wt_tr", 12)
        wt_ready = sig("wt_ready", 12)
        pv_mm = sig("pv_mm", 6)
        mix_hi = sig("mix_hi", 6)
        mix_lo = sig("mix_lo", 6)
        gate_mm = sig("gate_mm", 1, start=1)
        gate_split = sig("gate_split", 1)
        softplus_ready = sig("softplus_ready", 1)
        cum_ready = sig("cum_ready", 1)
        decay_ready = sig("decay_ready", 1)
        decay_exp = sig("decay_exp", 1)
        silu_r_ready = sig("silu_r_ready", 1)
        k_out_ready = sig("k_out_ready", 1)
        qk_ready = sig("qk_ready", 1)
        q_dec_ready = sig("q_dec_ready", 1)
        krow_tr = sig("krow_tr", 1)
        krow_ready = sig("krow_ready", 1)
        att_mm = sig("att_mm", 2)
        att_ready = sig("att_ready", 1)
        kv_mm = sig("kv_mm", 2)
        states_ready = sig("states_ready", NBP + 1)
        gla_mm = sig("gla_mm", HB)
        gla_sq = sig("gla_sq", HB)
        gla_mean_mm = sig("gla_mean_mm", HB)
        gla_std = sig("gla_std", HB)
        gla_copied = sig("gla_copied", HB)
        gla_gated = sig("gla_gated", HB)
        gla_f32 = sig("gla_f32", HB)
        gla_hi = sig("gla_hi", HB)
        gla_lo = sig("gla_lo", HB)
        rows_stored = sig("rows_stored", 10, 16)
        states_stored = sig("states_stored", 4, 16)
        pool_gates = sem("pool_gates")
        yT_mm = sem("yT_mm")
        y_left, y_right = sem("y_left"), sem("y_right")
        y_stored = sem("y_stored")

        def sample_view(rows, h):
            return ps[rows, 4, :].rearrange("p (b c h t) -> p c h b t", c=2, h=2, t=S)[:, :, h, :, :]

        def gla_banks(h):
            c, e = h // 2, h % 2
            return ps[:, 4 + 2 * c, e * NP:(e + 1) * NP], ps[:, 5 + 2 * c, e * NS:(e + 1) * NS]

        def sample_logits(i):
            return ps[:, i, 0:NK]

        def per_seq(n, role, f):
            return mod[:, 3 * n + role, f, 1:NSEQ].unsqueeze(2).broadcast_to([P, B, S])

        def samples(t):
            return t[:, NP:N].rearrange("p (b s) -> p b s", s=S)

        def slot_sum(f):
            return max(1, f - 2)

        def wait_chunk(engine, l, nth, f):
            if f < KD - 1:
                engine.wait_ge(proj_done.sem, proj_done.at(l, nth * (KD - 1) + f + 1))
            else:
                engine.wait_ge(unit_used.sem, unit_used.at(l, (U_WIN, U_F2IN, UNITS)[nth]))

        block = ctx.enter_context(nc.Block())

        @block.sync
        def _(sp):
            sp.dma_start(tok_in[:, 0:2, :], x_prompt[0].rearrange("(t p) d -> p t d", p=P)).then_inc(x_landed, 16)
            sp.dma_start(tok_in[:, 2, :], x_sample.rearrange("b s d -> (b s) d")).then_inc(x_landed, 16)
            for nth in (-2, -1):
                for q in range(4):
                    sp.wait_ge(ada_used.sem, ada_used.at(0, 4 * nth + q - 1))
                    sp.dma_start(w_ada_sb[q % 2][:],
                                 T["w_ada"][0, q * 256:(q + 1) * 256, (nth + 2) * 1024:(nth + 3) * 1024]
                                 .rearrange("(k p) n -> p k n", p=P)).then_inc(first_ada_landed[q % 2], 16)

            with sp.Fori(0, DEPTH) as l:
                def slot_free(u):
                    sp.wait_ge(lo_ready.sem, lo_ready.at(l, u - 1))

                def ffn_in(w, u0):
                    with sp.Fori(0, KF // 2) as i:
                        for s in range(2):
                            slot = (u0 + s) % 2
                            slot_free(i * 2 + (u0 + s))
                            for half in range(2):
                                src = w[l, :, bass.ds(i * 256 + (half * FF + s * P), P)]
                                sp.dma_start(w_raw[slot][:, half * 1024:(half + 1) * 1024]
                                             .rearrange("p (k n) -> p k n", n=P),
                                             src.rearrange("(k p) n -> p k n", p=P)
                                             ).then_inc(raw_landed[slot].sem, 16)

                def proj_out(w, u0, chunks):
                    def pair(i, s):
                        slot = (u0 + s) % 2
                        slot_free(i * 2 + (u0 + s))
                        for half in range(2):
                            sp.dma_start(w_raw[slot][:, half * 1024:(half + 1) * 1024],
                                         w[l, bass.ds(i * 512 + (s * 256 + half * P), P), :]
                                         ).then_inc(raw_landed[slot].sem, 16)
                    with sp.Fori(0, chunks // 4) as i:
                        pair(i, 0)
                        pair(i, 1)
                    if chunks % 4:
                        pair(chunks // 4, 0)

                def w_in_regular(u, s, col):
                    slot = (U_WIN + s) % 2
                    slot_free(u)
                    for half in range(2):
                        src = T["w_in"][l, half * 512:(half + 1) * 512, bass.ds(col, 256)]
                        sp.dma_start(w_raw[slot][:, half * 1024:(half + 1) * 1024]
                                     .rearrange("p (k n) -> p k n", n=256),
                                     src.rearrange("(k p) n -> p k n", p=P)).then_inc(raw_landed[slot].sem, 16)

                ffn_in(T["w_ffn1_in"], U_F1IN)
                proj_out(T["w_ffn1_out"], U_F1OUT, KF)
                slot = U_WIN % 2
                slot_free(U_WIN)
                first = w_raw[slot][:].rearrange("p (k n) -> p k n", n=256)
                rows = lambda a, b: T["w_in"][l, :, a:b].rearrange("(k p) n -> p k n", p=P)
                sp.dma_start(first[:, :, 0:128], rows(C_KV, C_KV + 128)).then_inc(raw_landed[slot].sem, 16)
                sp.dma_start(first[:, :, 128:196], rows(C_KI, C_KI + 68)).then_inc(raw_landed[slot].sem, 16)
                sp.dma_start(first[:, :, 196:256], rows(C_GB - 28, C_GB + 32)).then_inc(gate_cols_landed.sem, 16)
                w_in_regular(U_WIN + 1, 1, C_QI)
                w_in_regular(U_WIN + 2, 2, C_QC)
                with sp.Fori(0, 4) as i:
                    for s in range(2):
                        w_in_regular(i * 2 + (U_WIN + 3 + s), 3 + s, i * 512 + s * 256)
                w_in_regular(U_WIN + 11, 11, 8 * 256)
                for u, chunk in enumerate(WOUT_CHUNKS):
                    slot = (U_WOUT + u) % 2
                    slot_free(U_WOUT + u)
                    for half in range(2):
                        row = (chunk + half) * P
                        sp.dma_start(w_raw[slot][:, half * 1024:(half + 1) * 1024],
                                     T["w_out"][l, row:row + P, :]).then_inc(raw_landed[slot].sem, 16)
                ffn_in(T["w_ffn2_in"], U_F2IN)
                proj_out(T["w_ffn2_out"], U_F2OUT, KF)

            for t in range(TT):
                sp.wait_ge(y_left, t + 1)
                sp.wait_ge(y_right, t + 1)
                dst = T["y_prompt"][0, t * P:(t + 1) * P, :] if t < 2 else T["y_sample"].rearrange("b s d -> (b s) d")
                sp.dma_start(dst, tok_out[:, t, :]).then_inc(y_stored, 16)
            sp.wait_ge(y_stored, 16 * TT)

        @block.gpsimd
        def _(pool):
            def keep_where(t, pattern, base, channel, compare, fill):
                pool.affine_select(out=t, in_=t, compare_op=compare, fill=fill, base=base,
                                   pattern=pattern, channel_multiplier=channel)
                pool.drain()

            def load_head(layer):
                pool.dma_start(head[0:16, :], T["b_ada"][layer, 0:2 * D].rearrange("(r p) -> r p", p=P)).then_inc(head_landed.sem, 16)
                pool.dma_start(head[16:24, :], T["norm_gains"][layer, 0].rearrange("(r p) -> r p", p=P)).then_inc(head_landed.sem, 16)

            load_head(0)
            pool.memset(ident[:], 0.0)
            pool.drain()
            keep_where(ident[:], [[-1, P]], 0, 1, ALU.not_equal, 1.0)
            pool.sem_inc(ident_ready, 1)
            pool.memset(params[:], 0.0)
            for t, v in ((ones_d, 1.0 / D), (ones_v, 1.0 / DV), (causal, 0.0), (gla_mask, 1.0),
                         (restart, 1.0), (dup_eye, 0.0), (spread, 0.0), (sb_mask_c, 0.0), (head_rows, 0.0),
                         (other_seq, 0.0), (parity, 1.0), (ones_row, 1.0)):
                pool.memset(t[:], v)
            pool.drain()
            keep_where(causal[:], [[-1, P]], 0, 1, ALU.is_gt, 1.0)
            for kind, length in ((0, LP), (1, S)):
                m = gla_mask[:, kind, :]
                keep_where(m, [[1, P]], 0, -1, ALU.is_ge, 0.0)
            pool.memset(restart[:, 0:NP].rearrange("p (n l) -> p n l", l=LP)[:, :, 0:1], 0.0)
            pool.memset(restart[:, NP:N].rearrange("p (n l) -> p n l", l=S)[:, :, 0:1], 0.0)
            keep_where(dup_eye[0:64, :].rearrange("p (a n) -> p a n", a=2), [[0, 2], [-1, 64]], 0, 1, ALU.not_equal, 1.0)
            for i in range(PAIRS):
                rows = slice(32 * i, 32 * i + 32)
                for c in range(4):
                    keep_where(spread[rows, :].rearrange("p (b c t) -> p b c t", b=2, c=4)[:, :, c, :],
                               [[-16, 2], [-1, 16]], 0, 1, ALU.not_equal, 1.0)
                keep_where(other_seq[rows, 0:16], [[0, 16]], 15, -1, ALU.is_ge, NEG_MASKED)
                keep_where(other_seq[rows, 16:32], [[0, 16]], -16, 1, ALU.is_ge, NEG_MASKED)
                keep_where(parity[rows, 0:1], [[0, 1]], 15, -1, ALU.is_ge, 0.0)
                keep_where(parity[rows, 1:2], [[0, 1]], -16, 1, ALU.is_ge, 0.0)
            keep_where(sb_mask_c[:], [[-1, 32]], 0, 1, ALU.is_gt, 1.0)
            keep_where(head_rows[WI_ROW:WI_ROW + 4, :].rearrange("p (b h t) -> p b h t", b=2, h=4),
                       [[0, 2], [-1, 4], [0, 16]], 0, 1, ALU.not_equal, 1.0)
            pool.drain()
            for kind, length in ((0, LP), (1, S)):
                m = gla_mask[:, kind, :].rearrange("p (n l) -> p n l", l=length)
                keep_where(m, [[-length, P // length], [0, length]], 0, 1, ALU.is_ge, 0.0)
            pool.affine_select(out=sb_mask_c[:, 0:16], in_=sb_mask_c[:, 0:16], compare_op=ALU.is_ge, fill=1.0,
                               base=15, pattern=[[0, 16]], channel_multiplier=-1)
            pool.drain()
            pool.sem_inc(consts_ready, 1)

            with pool.Fori(0, DEPTH) as l:
                def pass_gate():
                    pool.sem_inc(pool_gates, 1)

                pool.wait_ge(params_tr.sem, params_tr.at(l, 0))
                pool.wait_ge(gate_mm.sem, gate_mm.at(l, 0))
                pass_gate()
                for dst, src in (
                    (params[0:72, :], T["b_ada"][l].rearrange("(r p) -> r p", p=P)),
                    (params[72:120, :], T["norm_gains"][l].rearrange("g (r p) -> (g r) p", p=P)),
                    (params[120:124, :], T["gla_norm"][l].rearrange("(r p) -> r p", p=P)),
                    (params[124:126, :], T["b_gla_gate"][l].rearrange("(r p) -> r p", p=P)),
                    (w_gate_sb[GB_ROW:GB_ROW + RANK, :], T["w_gla_gate"][l]),
                ):
                    pool.dma_start(dst, src).then_inc(params_landed.sem, 16)

                pool.wait_ge(head_tr.sem, head_tr.at(l, 0))
                pass_gate()
                load_head(NEXT)

                def ada_component(nth, layer, component, quarters=range(4)):
                    for q in quarters:
                        pool.wait_ge(ada_used.sem, ada_used.at(l, nth * 4 + (q - 1)))
                        pass_gate()
                        pool.dma_start(w_ada_sb[q % 2][:],
                                       T["w_ada"][layer, q * 256:(q + 1) * 256, bass.ds(component * 1024, 1024)]
                                       .rearrange("(k p) n -> p k n", p=P)).then_inc(ada_landed[q % 2].sem, 16)

                def pre_norm(nth):
                    for f in range(KD):
                        pool.wait_ge(x_scaled.sem, x_scaled.at(l, nth * KD + f + 1))
                        pool.tensor_tensor(samples(y[:, f, :]), samples(y[:, f, :]), per_seq(nth, 1, f), ALU.mult)
                        pool.drain()
                        pool.tensor_tensor(samples(y[:, f, :]), samples(y[:, f, :]), per_seq(nth, 0, f), ALU.add).then_inc(samples_ready.sem, 1)

                ada_component(0, l, 2, (0, 1))
                pre_norm(0)
                ada_component(0, l, 2, (2, 3))
                with pool.Fori(1, ADA_LAST1 + 1) as i:
                    ada_component(i, l, i + 2)

                pool.wait_ge(ada_used.sem, ada_used.at(l, 4 * ADA_F2))
                pass_gate()
                pool.dma_start(k_sb_raw[:],
                               T["cache_k_sb"][l].rearrange("b p h d -> p b (h d)")).then_inc(k_cache_landed.sem, 16)
                for half in range(2):
                    pool.dma_start(kc_raw[:, :, half, :],
                                   T["cache_k_dsa"][l].rearrange("b p d -> p b d")).then_inc(k_cache_landed.sem, 16)
                    pool.dma_start(ki_raw[:, :, half, :],
                                   T["cache_k_idx"][l].rearrange("b p d -> p b d")).then_inc(k_cache_landed.sem, 16)
                pre_norm(1)
                pool.wait_ge(act_ready.sem, act_ready.at(l, 2 * KD))
                pass_gate()
                for half in range(2):
                    pool.dma_start(vc_past[:, :, half, :],
                                   T["cache_v_dsa"][l].rearrange("b p d -> p b d")).then_inc(v_cache_landed[0].sem, 16)

                pool.wait_ge(cum_ready.sem, cum_ready.at(l, 1))
                pool.wait_ge(tm_act.sem, tm_act.at(l, 3))
                pool.wait_ge(tm_dve.sem, tm_dve.at(l, 3))
                pool.wait_ge(z_mm.sem, z_mm.at(l, 5))
                for a, b, length in ((0, NP, LP), (NP, N, S)):
                    view = lambda t: t[:, :, a:b].rearrange("p c (n l) -> p c n l", l=length)
                    n = (b - a) // length
                    cum = view(cumdecay)
                    mid = cum[:, :, :, length // 2 - 1:length // 2].broadcast_to([P, 2, n, length])
                    end = cum[:, :, :, length - 1:length].broadcast_to([P, 2, n, length])
                    pool.tensor_tensor(view(k_in), cum, mid, ALU.subtract)
                    ins = pool.tensor_tensor(view(k_out), end, cum, ALU.subtract)
                ins.then_inc(decay_ready.sem, 1)
                q, k = U[:, QB:QB + 2, :], U[:, KB:KB + 2, :]
                pool.tensor_scalar(q, q, QSCALE, None, ALU.mult)
                pool.drain()

                pool.wait_ge(mix_lo.sem, mix_lo.at(l, 3))
                pass_gate()
                pool.dma_start(va_past[:], T["cache_v_sb"][l].rearrange("b p h d -> p b (h d)")).then_inc(v_cache_landed[1].sem, 16)
                pool.wait_ge(decay_exp.sem, decay_exp.at(l, 1))
                pool.tensor_tensor(k_out, k_out, k, ALU.mult).then_inc(k_out_ready.sem, 1)
                pool.tensor_tensor(k_in[:], k_in[:], k, ALU.mult)
                pool.tensor_tensor(q_in, q_in, q, ALU.mult).then_inc(qk_ready.sem, 1)
                pool.drain()
                for c, e in ((1, 1), (1, 0), (0, 1), (0, 0)):
                    own = slice(64 * e, 64 * e + 64)
                    pool.tensor_tensor(q_dec[own, c, e, :], q[own, c, :], decay[own, c, :], ALU.mult)
                    pool.drain()
                for c, e in ((1, 1), (1, 0), (0, 1), (0, 0)):
                    other = slice(64 - 64 * e, 128 - 64 * e)
                    ins = pool.memset(q_dec[other, c, e, :], 0.0)
                ins.then_inc(q_dec_ready.sem, 1)
                pool.wait_ge(mix_lo.sem, mix_lo.at(l, 6))
                pass_gate()
                for c in range(2):
                    pool.dma_start(gstate[:, :, c, :],
                                   T["state_gla"][l, :, 2 * c:2 * c + 2].rearrange("b h k v -> (h k) b v")
                                   ).then_inc(gstate_landed.sem, 16)
                for name, col, width in (("k_sb", TM_KA, 256), ("v_sb", TM_VA, 256), ("k_dsa", TM_KV, 64),
                                         ("v_dsa", TM_KV + 64, 64), ("k_idx", TM_KI, 64)):
                    dst = T[f"new_{name}_p"][l, 0]
                    dst = dst.rearrange("(t p) h d -> p t (h d)", p=P) if width == 256 else dst.rearrange("(t p) d -> p t d", p=P)
                    pool.dma_start(dst, TM[:, 0:2, col:col + width]).then_inc(rows_stored.sem, 16)
                    dst = T[f"new_{name}_s"][l]
                    dst = dst.rearrange("b s h d -> (b s) (h d)") if width == 256 else dst.rearrange("b s d -> (b s) d")
                    pool.dma_start(dst, TM[:, 2, col:col + width]).then_inc(rows_stored.sem, 16)

                pool.wait_ge(states_ready.sem, states_ready.at(l, NBP + 1))
                pass_gate()
                for c in range(2):
                    pool.dma_start(T["new_gla_p"][l, 0, 2 * c:2 * c + 2].rearrange("h k v -> (h k) v"),
                                   states[:, NBP - 1, c, :]).then_inc(states_stored.sem, 16)
                    pool.dma_start(T["new_gla_s"][l, :, 2 * c:2 * c + 2].rearrange("b h k v -> (h k) b v"),
                                   gstate_new[:, :, c, :]).then_inc(states_stored.sem, 16)
                for h in range(HB):
                    if h == 0:
                        pool.wait_ge(silu_r_ready.sem, silu_r_ready.at(l, 1))
                    pool.wait_ge(gla_copied.sem, gla_copied.at(l, h + 1))
                    pool.tensor_tensor(gla_out[:, h, :], gla_out[:, h, :], U[:, RB + h, :], ALU.mult).then_inc(gla_gated.sem, 1)

                pool.wait_ge(kt_tr.sem, kt_tr.at(l, 8))
                ada_component(ADA_F2, l, 8, (0, 1))
                pre_norm(2)
                ada_component(ADA_F2, l, 8, (2, 3))
                with pool.Fori(0, 2) as i:
                    ada_component(i + (ADA_F2 + 1), NEXT, i)
            pool.wait_ge(rows_stored.sem, rows_stored.at(DEPTH, 0))
            pool.wait_ge(states_stored.sem, states_stored.at(DEPTH, 0))

        @block.scalar
        def _(act):
            u_even.credit(act)
            ada_rows_ready.credit(act)
            act.wait_ge(c_zeroed, 1)
            act.dma_start(c_rows[0:1, :], T["c_prompt"]).then_inc(c_landed, 16)
            act.dma_start(c_rows[1:NSEQ, :], T["c_sample"]).then_inc(c_landed, 16)
            act.wait_ge(c_landed, 32)
            act.activation(c_rows[:], c_rows[:], ACT.Silu).then_inc(silu_c_ready, 1)
            for f in range(4, KD):
                act.wait_ge(xT_mm, f + 1)
                act.activation(x[:, f, :], ps[:, f, 0:N], ACT.Copy).then_inc(x_ready.sem, 1)

            def ada(l, nth):
                act.wait_ge(ada_used.sem, ada_used.at(l, nth * 4 + 4))
                act.wait_ge(ada_tr.sem, ada_tr.at(l, nth))
                act.activation(ada_rows[:], ps[:, 4, 0:256], ACT.Copy).then_inc(ada_rows_ready.sem, 1)

            ada(0, -2)
            ada(0, -1)

            with act.Fori(0, DEPTH) as l:
                def split_hi(u, slot):
                    act.wait_ge(raw_landed[slot].sem, raw_landed[slot].at(l, 0) + (u // 2 + 1) * 32)
                    act.wait_ge(unit_used.sem, unit_used.at(l, 0) + (u - 1))
                    act.activation(w_hi[slot][:], w_raw[slot][:], ACT.Copy).then_inc(hi_ready.sem, 1)

                def split_hi_in_loop(j, u):
                    slot = u % 2
                    act.wait_ge(raw_landed[slot].sem, raw_landed[slot].at(l, 0) + (j * 16 + (u // 2 + 1) * 32))
                    act.wait_ge(unit_used.sem, unit_used.at(l, 0) + (j + (u - 1)))
                    act.activation(w_hi[slot][:], w_raw[slot][:], ACT.Copy).then_inc(hi_ready.sem, 1)

                def std(norm):
                    act.wait_ge(mean_mm.sem, mean_mm.at(l, norm + 1))
                    act.activation(rstd[:], ps[:, 0, 0:N], ACT.Sqrt, bias=eps_col).then_inc(std_ready.sem, 1)

                def pre_norm(nth):
                    for f in range(KD):
                        act.wait_ge(x_ready.sem, x_ready.at(l, nth * KD + f + 1))
                        act.activation(y[:, f, :], x[:, f, :], ACT.Square).then_inc(x_sq_ready.sem, 1)
                    std(2 * nth)
                    for f in range(KD):
                        act.wait_ge(x_scaled.sem, x_scaled.at(l, nth * KD + f + 1))
                        scale, shift = mod[:, 3 * nth + 1, f, 0:1], mod[:, 3 * nth, f, 0:1]
                        act.activation(act_hi[:, f, 0:NP], y[:, f, 0:NP], ACT.Identity, scale=scale, bias=shift)
                        act.activation(y[:, f, 0:NP], y[:, f, 0:NP], ACT.Identity, scale=scale, bias=shift)
                        act.wait_ge(samples_ready.sem, samples_ready.at(l, nth * KD + f + 1))
                        act.activation(act_hi[:, f, NP:N], y[:, f, NP:N], ACT.Copy).then_inc(act_hi_ready.sem, 1)

                def post_norm(nth):
                    for f in range(KD):
                        wait_chunk(act, l, nth, f)
                        act.activation(y[:, f, 0:NP], ps[:, f, 0:NP], ACT.Identity, scale=mod[:, 3 * nth + 2, f, 0:1])
                        if f >= 2:
                            act.wait_ge(y_sq_summed.sem, y_sq_summed.at(l, nth * (KD - 1) + slot_sum(f)))
                        act.activation(sq[:, f % 2, :], ps[:, f, 0:N], ACT.Square).then_inc(y_sq_ready.sem, 1)
                    std(2 * nth + 1)

                def hidden(u0, h0, j, s):
                    split_hi_in_loop(j, u0 + s + 1)
                    if s == 3:
                        return
                    finish(u0, h0, j, s)

                def finish(u0, h0, j, s):
                    act.wait_ge(unit_used.sem, unit_used.at(l, u0 + s + 1) + j)
                    act.wait_ge(hidden_ready.sem, hidden_ready.at(l, h0 + s - 1) + j)
                    act.activation(silu_g[:, s % 2, :], ps[:, 2 * (s % 2), 0:N], ACT.Silu).then_inc(silu_ready.sem, 1)

                def four_hidden(u0, h0, j, nth):
                    for s in range(4):
                        hidden(u0, h0, j, s)
                    ada(l, nth)
                    finish(u0, h0, j, 3)

                def proj_out(u0, units, ahead=True):
                    with act.Fori(0, (units - 1) // 2) as i:
                        for s in range(2):
                            split_hi_in_loop(i * 2, u0 + s + 1)
                    for u in range(u0 + (units - 1) // 2 * 2, u0 + units):
                        if ahead or u < u0 + units - 1:
                            split_hi(u + 1, (u + 1) % 2)

                eps_col = small[:, 0:1]
                split_hi(0, 0)
                pre_norm(0)
                with act.Fori(0, ADA_LAST1) as i:
                    four_hidden(U_F1IN, 0, i * 4, i)
                hidden(U_F1IN, 0, KF - 2, 0)
                split_hi(U_F1OUT, U_F1OUT % 2)
                ada(l, ADA_LAST1)
                finish(U_F1IN, 0, KF - 2, 1)
                proj_out(U_F1OUT, KF // 2, ahead=False)
                post_norm(0)
                act.wait_ge(gate_cols_landed.sem, gate_cols_landed.at(l, 1))
                split_hi(U_WIN, U_WIN % 2)
                pre_norm(1)

                def w_in_unit(n):
                    split_hi(U_WIN + n + 1, (U_WIN + n + 1) % 2)
                    act.wait_ge(unit_used.sem, unit_used.at(l, U_WIN + n + 1))
                    act.activation(U[:, WIN_TILES[n], :], ps[:, 2 * (n % 2), 0:N], ACT.Copy).then_inc(u_even.sem, 1)

                def keys_T(phase_no):
                    for g in range(4):
                        act.wait_ge(kt_tr.sem, kt_tr.at(l, 4 * phase_no + g + 1))
                        if phase_no == 0:
                            dst = (kcT, kiT)[g // 2][:, 4 * (g % 2):4 * (g % 2) + 4, :]
                            bank = (6, 7, 4, 5)[g]
                        else:
                            dst = kaT[:, g // 2, 4 * (g % 2):4 * (g % 2) + 4, :]
                            bank = g
                        act.activation(dst, ps[:, bank, :].rearrange("p (b k) -> p b k", k=P), ACT.Copy).then_inc(kt_ready.sem, 1)

                def attend_tail(phase_no, chunk, wT, swT):
                    for h in range(HA):
                        act.wait_ge(wt_tr.sem, wt_tr.at(l, 6 * phase_no + h + 1))
                        act.activation(wT[:, h, :], ps[:, 4 + h, 0:N], ACT.Copy).then_inc(wt_ready.sem, 1)
                    act.wait_ge(wt_tr.sem, wt_tr.at(l, 6 * phase_no + 5))
                    act.activation(swT[:], ps[:, 2, :].rearrange("p (i r) -> p i r", r=P), ACT.Copy).then_inc(wt_ready.sem, 1)
                    act.wait_ge(wt_tr.sem, wt_tr.at(l, 6 * phase_no + 6))
                    for i in range(PAIRS):
                        rows = slice(32 * i, 32 * i + 32)
                        ins = act.activation(snT[rows, i, :], ps[rows, 3, 0:P], ACT.Copy)
                    ins.then_inc(wt_ready.sem, 1)
                    for c in range(2):
                        act.wait_ge(pv_mm.sem, pv_mm.at(l, 3 * phase_no + c + 1))
                        act.activation(act_hi[:, chunk + c, 0:NP], ps[:, c, 0:NP], ACT.Copy).then_inc(mix_hi.sem, 1)
                    act.wait_ge(pv_mm.sem, pv_mm.at(l, 3 * phase_no + 3))
                    for h in range(2):
                        rows = slice(64 * h, 64 * h + 64)
                        ins = act.activation(act_hi[rows, chunk:chunk + 2, NP:N].rearrange("p c (b t) -> p c b t", t=S),
                                             sample_view(rows, h), ACT.Copy)
                    ins.then_inc(mix_hi.sem, 1)

                for n in range(3):
                    w_in_unit(n)
                act.wait_ge(kvi_tr.sem, kvi_tr.at(l, 1))
                act.activation(TM[:, 0:2, TM_KV:TM_W], ps[:, 4, :].rearrange("p (t n) -> p t n", n=256), ACT.Copy)
                act.activation(TM[:, 2, TM_KV:TM_W], ps[:, 5, 0:256], ACT.Copy).then_inc(kvi_ready.sem, 1)
                for n, dst in enumerate((kc_dup, ki_dup)):
                    act.wait_ge(dup_mm.sem, dup_mm.at(l, n + 1))
                    act.activation(dst[:], ps[:, 6 + n, 0:N], ACT.Copy).then_inc(dup_ready.sem, 1)
                w_in_unit(3)
                keys_T(0)
                w_in_unit(4)
                act.wait_ge(idx_s_mm.sem, idx_s_mm.at(l, 1))
                act.activation(relu_s[:, 0:3, :], ps[:, 4, 0:3 * NK].rearrange("p (i k) -> p i k", k=NK), ACT.Relu)
                act.activation(relu_s[:, 3, :], ps[:, 5, 0:NK], ACT.Relu).then_inc(idx_s_relu.sem, 1)
                w_in_unit(5)
                act.wait_ge(gate_split.sem, gate_split.at(l, 1))
                for c in range(2):
                    act.activation(cumdecay[:, c, :], ps[:, 4 + c, 0:N], ACT.Abs, bias=params_t[:, 124 + c:125 + c])
                act.drain()
                act.activation(cumdecay[:], cumdecay[:], ACT.Exp, scale=-1.0)
                act.drain()
                act.activation(cumdecay[:], cumdecay[:], ACT.Ln, bias=1.0).then_inc(softplus_ready.sem, 1)
                w_in_unit(6)
                for h in range(HA):
                    act.wait_ge(idx_mm.sem, idx_mm.at(l, h + 1))
                    act.wait_ge(idx_summed.sem, idx_summed.at(l, h - 1))
                    act.activation(relu_p[:, h % 2, :], ps[:, 4 + h, 0:N], ACT.Relu).then_inc(idx_relu.sem, 1)
                for n in range(7, NU // 2):
                    w_in_unit(n)
                for t in range(TT):
                    act.wait_ge(tm_tr.sem, tm_tr.at(l, 2 * t + 1))
                    act.activation(TM[:, t, 0:512], ps[:, 2 * t % 4, :], ACT.Copy).then_inc(tm_act.sem, 1)
                act.wait_ge(neg_max_ready.sem, neg_max_ready.at(l, 1))
                for h in range(HA):
                    for t, cols in enumerate((slice(0, P), slice(P, N))):
                        ins = act.activation(dsa_w[:, h, cols], dsa_w[:, h, cols], ACT.Exp, scale=QSCALE,
                                             bias=small[:, 8 + 4 * t + h:9 + 4 * t + h],
                                             accum_out=small[:, 24 + 4 * t + h:25 + 4 * t + h])
                ins.then_inc(exp_ready.sem, 1)
                act.wait_ge(neg_max_ready.sem, neg_max_ready.at(l, 2))
                for i in range(PAIRS):
                    ins = act.activation(dsa_sw[:, i, :], sample_logits(i), ACT.Exp, scale=QSCALE,
                                         bias=small[:, 16 + i:17 + i], accum_out=small[:, 32 + i:33 + i])
                ins.then_inc(exp_ready.sem, 1)
                act.wait_ge(decay_ready.sem, decay_ready.at(l, 1))
                act.activation(q_in, k_in[:], ACT.Exp, scale=1.0 / GATE_TAU)
                act.activation(k_in[:], k_in[:], ACT.Exp, scale=-1.0 / GATE_TAU)
                act.activation(k_out, k_out, ACT.Exp, scale=1.0 / GATE_TAU)
                act.activation(decay[:], cumdecay[:], ACT.Exp, scale=1.0 / GATE_TAU).then_inc(decay_exp.sem, 1)
                attend_tail(0, 6, dsa_wT, dsa_swT)

                keys_T(1)
                for h in range(HA):
                    act.wait_ge(z_mm.sem, z_mm.at(l, 5 + h + 1))
                    act.activation(keep[:, h, :], ps[:, 4 + h, 0:N], ACT.Sigmoid, scale=-QSCALE).then_inc(keep_ready.sem, 1)
                act.wait_ge(z_mm.sem, z_mm.at(l, 10))
                act.activation(keep_s[:, 0:3, :], ps[:, 0, 0:3 * NK].rearrange("p (i k) -> p i k", k=NK), ACT.Sigmoid, scale=-QSCALE)
                act.activation(keep_s[:, 3, :], ps[:, 1, 0:NK], ACT.Sigmoid, scale=-QSCALE).then_inc(keep_ready.sem, 1)
                act.wait_ge(weights_ready.sem, weights_ready.at(l, 10))
                attend_tail(1, 0, sb_wT, sb_swT)

                act.activation(U[:, RB:RB + 4, :], U[:, RB:RB + 4, :], ACT.Silu).then_inc(silu_r_ready.sem, 1)
                act.wait_ge(krow_tr.sem, krow_tr.at(l, 1))
                act.activation(k_rows[:, 0:2, :], ps[:, 2, :].rearrange("p (t n) -> p t n", n=256), ACT.Copy)
                act.activation(k_rows[:, 2, :], ps[:, 3, 0:256], ACT.Identity, scale=parity[:, 0:1])
                act.activation(k_rows[:, 3, :], ps[:, 3, 0:256], ACT.Identity, scale=parity[:, 1:2]).then_inc(krow_ready.sem, 1)
                split_hi(U_WOUT + 1, (U_WOUT + 1) % 2)
                for h in range(HB):
                    act.wait_ge(gla_mm.sem, gla_mm.at(l, h + 1))
                    prompt, sample = gla_banks(h)
                    act.activation(gla_sqs[h][:, 0:NP], prompt, ACT.Square)
                    act.activation(gla_sqs[h][:, NP:N], sample, ACT.Square).then_inc(gla_sq.sem, 1)
                    gain = params_t[:, 120 + h:121 + h]
                    act.activation(gla_out[:, h, 0:NP], prompt, ACT.Identity, scale=gain)
                    act.activation(gla_out[:, h, NP:N], sample, ACT.Identity, scale=gain).then_inc(gla_copied.sem, 1)
                for h in range(HB):
                    act.wait_ge(gla_mean_mm.sem, gla_mean_mm.at(l, h + 1))
                    act.activation(gla_stds[h], ps[:, h, 0:N], ACT.Sqrt, bias=eps_col).then_inc(gla_std.sem, 1)
                for h in range(HB):
                    act.wait_ge(gla_f32.sem, gla_f32.at(l, h + 1))
                    act.activation(act_hi[:, 2 + h, :], gla_out[:, h, :], ACT.Copy).then_inc(gla_hi.sem, 1)

                for u in range(U_WOUT + 2, U_F2IN):
                    split_hi(u, u % 2)
                act.wait_ge(rows_stored.sem, rows_stored.at(l, 10))
                act.wait_ge(states_stored.sem, states_stored.at(l, 4))
                post_norm(1)
                split_hi(U_F2IN, U_F2IN % 2)
                pre_norm(2)
                four_hidden(U_F2IN, KF, 0, ADA_F2)
                with act.Fori(0, 2) as i:
                    four_hidden(U_F2IN, KF, i * 4 + 4, i + (ADA_F2 + 1))
                with act.Fori(0, (KF - 12) // 2) as i:
                    for s in range(2):
                        hidden(U_F2IN, KF, i * 2 + 12, s)
                proj_out(U_F2OUT, KF // 2, ahead=False)
                post_norm(2)

            for t in range(TT):
                act.wait_ge(yT_mm, 2 * t + 1)
                act.activation(tok_out[:, t, 0:512], ps[:, 2 * t, :], ACT.Copy).then_inc(y_left, 1)

        @block.vector
        def _(dve):
            for free_slots in (lo_ready, hidden_ready, u_odd, idx_summed, mod_ready):
                free_slots.credit(dve)
            dve.memset(c_rows[:], 0.0).then_inc(c_zeroed, 1)
            dve.memset(small[:], EPS)
            dve.wait_ge(cT_mm, 1)
            dve.tensor_copy(silu_cT[:], ps[:, 4, 0:KD * 32].rearrange("p (f n) -> p f n", n=32)).then_inc(cT_ready, 1)
            dve.wait_ge(head_tr.sem, head_tr.at(0, 0))
            dve.tensor_copy(params_t[:, P:P + 24], ps[:, 5, 64:88]).then_inc(head_ready, 1)
            for f in range(4):
                dve.wait_ge(xT_mm, f + 1)
                dve.tensor_copy(x[:, f, :], ps[:, f, 0:N]).then_inc(x_ready.sem, 1)
            dve.drain()

            def ada(l, nth, component, bias_at):
                dve.wait_ge(ada_tr.sem, ada_tr.at(l, nth + 1))
                dst = mod[:, bass.ds(component, 1), :, :].rearrange("p a (q j) s -> p (a q) j s", j=2)
                bias = params_t[:, bass.ds(bias_at, 8)].rearrange("p (q j) -> p q j", j=2)
                for j in range(2):
                    ins = dve.tensor_tensor(dst[:, :, j, :],
                                            ps[:, 5, j * P:(j + 1) * P].rearrange("p (q s) -> p q s", q=4)[:, :, 0:NSEQ],
                                            bias[:, :, j].unsqueeze(2).broadcast_to([P, 4, NSEQ]), ALU.add)
                ins.then_inc(mod_ready.sem, 1)

            def fold_gain(component, gain_at):
                norm, role = component // 3, component % 3
                m = mod[:, component, :, :]
                gain = params_t[:, gain_at:gain_at + KD].unsqueeze(2).broadcast_to([P, KD, NSEQ])
                if role == 1:
                    dve.scalar_tensor_tensor(out=m, in0=m, scalar=1.0, in1=gain, op0=ALU.add, op1=ALU.mult)
                else:
                    dve.scalar_tensor_tensor(out=m, in0=m, scalar=1.0 if norm == 1 else MACARON_W, in1=gain,
                                             op0=ALU.mult, op1=ALU.mult)

            ada(0, -2, 0, P)
            ada(0, -1, 1, P + 8)
            dve.drain()
            fold_gain(1, P + 16)
            dve.wait_ge(const_mm, 1)
            dve.tensor_copy(sb_mask[:], ps[:, 7, 384:416])
            dve.tensor_copy(own_step[:], ps[:, 7, 416:448]).then_inc(masks_ready, 1)
            dve.drain()

            with dve.Fori(0, DEPTH) as l:
                def split_lo(g, slot):
                    dve.wait_ge(hi_ready.sem, hi_ready.at(l, 1) + g)
                    dve.tensor_tensor(w_lo[slot][:], w_raw[slot][:], w_hi[slot][:].bitcast(F32), ALU.subtract).then_inc(lo_ready.sem, 1)

                def inverse_std(norm):
                    dve.wait_ge(std_ready.sem, std_ready.at(l, norm + 1))
                    dve.reciprocal(rstd[:], rstd[:])
                    dve.drain()

                def pre_norm(nth):
                    inverse_std(2 * nth)

                    def low(f):
                        dve.wait_ge(act_hi_ready.sem, act_hi_ready.at(l, nth * KD + f + 1))
                        dve.tensor_tensor(act_lo[:, f, :], y[:, f, :], act_hi[:, f, :].bitcast(F32),
                                          ALU.subtract).then_inc(act_ready.sem, 1)

                    for f in range(KD):
                        dve.tensor_tensor(y[:, f, :], x[:, f, :], rstd[:], ALU.mult).then_inc(x_scaled.sem, 1)
                        if f >= 2:
                            low(f - 2)
                    low(KD - 2)
                    low(KD - 1)

                def post_norm(nth):
                    for f in range(KD):
                        dve.wait_ge(y_sq_ready.sem, y_sq_ready.at(l, nth * KD + f + 1))
                        if f >= 1:
                            dve.tensor_tensor(sumsq[:], sq[:, 0, :] if f == 1 else sumsq[:], sq[:, f % 2, :],
                                              ALU.add).then_inc(y_sq_summed.sem, 1)
                        dve.tensor_tensor(samples(y[:, f, :]), samples(ps[:, f, :]), per_seq(nth, 2, f), ALU.mult)
                        dve.drain()
                    inverse_std(2 * nth + 1)
                    for f in range(0, KD, 2):
                        two = slice(f, f + 2)
                        dve.tensor_tensor(y[:, two, :], y[:, two, :], rstd[:].unsqueeze(1).broadcast_to([P, 2, N]), ALU.mult)
                        dve.drain()
                        dve.tensor_tensor(x[:, two, :], x[:, two, :], y[:, two, :], ALU.add).then_inc(x_ready.sem, 2)

                def hidden(u0, h0, j, s):
                    split_lo(j + (u0 + s + 1), (u0 + s + 1) % 2)
                    dve.wait_ge(silu_ready.sem, silu_ready.at(l, h0 + s + 1) + j)
                    dve.tensor_tensor(hid_f32[:], silu_g[:, s % 2, :], ps[:, 2 * (s % 2) + 1, 0:N], ALU.mult)
                    dve.drain()
                    chunk = bass.ds(j + s, 1)
                    one = hid_f32[:].rearrange("p (a n) -> p a n", a=1)
                    dve.tensor_copy(hid_hi[:, chunk, :], one)
                    dve.drain()
                    dve.tensor_tensor(hid_lo[:, chunk, :], one, hid_hi[:, chunk, :].bitcast(F32), ALU.subtract).then_inc(hidden_ready.sem, 1)
                    dve.drain()

                def four_hidden(u0, h0, j, nth, component, bias_at):
                    for s in range(4):
                        hidden(u0, h0, j, s)
                    ada(l, nth, component, bias_at)

                def proj_out(u0, units, ahead=True):
                    with dve.Fori(0, (units - 1) // 2) as i:
                        for s in range(2):
                            split_lo(i * 2 + (u0 + s + 1), (u0 + s + 1) % 2)
                    for u in range(u0 + (units - 1) // 2 * 2, u0 + units):
                        if ahead or u < u0 + units - 1:
                            split_lo(u + 1, (u + 1) % 2)

                dve.wait_ge(params_tr.sem, params_tr.at(l, 1))
                dve.tensor_copy(params_t[:, 0:P], ps[:, 6, 0:P]).then_inc(params_ready.sem, 1)
                dve.drain()
                split_lo(0, 0)
                pre_norm(0)
                with dve.Fori(0, ADA_LAST1) as i:
                    four_hidden(U_F1IN, 0, i * 4, i, i + 2, i * 8 + 16)
                for component in (2, 4, 5):
                    fold_gain(component, 72 + KD * (component // 3 * 2 + (component % 3 == 2)))
                for s in range(2):
                    hidden(U_F1IN, 0, KF - 2, s)
                ada(l, ADA_LAST1, 7, 56)
                dve.drain()
                fold_gain(7, 72 + KD * 4)
                proj_out(U_F1OUT, KF // 2, ahead=False)
                post_norm(0)
                split_lo(U_WIN, U_WIN % 2)
                pre_norm(1)

                def w_in_unit(n):
                    split_lo(U_WIN + n + 1, (U_WIN + n + 1) % 2)
                    dve.wait_ge(unit_used.sem, unit_used.at(l, U_WIN + n + 1))
                    dve.tensor_copy(U[:, WIN_TILES[n] + 1, :], ps[:, 2 * (n % 2) + 1, 0:N]).then_inc(u_odd.sem, 1)

                def block_diagonal(dst, tile):
                    for c in range(2):
                        for h in range(2):
                            rows = slice(64 * h, 64 * h + 64)
                            ins = dve.tensor_copy(dst[rows, c, :, 16 * h:16 * h + 16],
                                                  U[rows, tile + c, NP:N].rearrange("p (b t) -> p b t", t=S))
                    return ins

                def mix_low(phase_no, chunk):
                    for c in range(2):
                        dve.wait_ge(mix_hi.sem, mix_hi.at(l, 3 * phase_no + c + 1))
                        dve.tensor_tensor(act_lo[:, chunk + c, 0:NP], ps[:, c, 0:NP], act_hi[:, chunk + c, 0:NP].bitcast(F32),
                                          ALU.subtract).then_inc(mix_lo.sem, 1)
                    dve.wait_ge(mix_hi.sem, mix_hi.at(l, 3 * phase_no + 3))
                    for h in range(2):
                        rows = slice(64 * h, 64 * h + 64)
                        v = lambda t: t[rows, chunk:chunk + 2, NP:N].rearrange("p c (b t) -> p c b t", t=S)
                        ins = dve.tensor_tensor(v(act_lo), sample_view(rows, h), v(act_hi).bitcast(F32), ALU.subtract)
                    ins.then_inc(mix_lo.sem, 1)

                for n in range(3):
                    w_in_unit(n)
                dve.wait_ge(u_even.sem, u_even.at(l, 3))
                dve.memset(snT, 0.0)
                dve.memset(qc_bd[:], 0.0)
                dve.memset(qi_bd[:], 0.0)
                dve.drain()
                block_diagonal(qc_bd, QC)
                block_diagonal(qi_bd, QI)
                dve.wait_ge(kvi_ready.sem, kvi_ready.at(l, 1))
                for half in range(2):
                    ins = dve.tensor_copy(vc_new[:, half, :], TM[:, 2, TM_KV + 64:TM_KV + 128])
                ins.then_inc(bd_ready.sem, 1)
                w_in_unit(3)
                w_in_unit(4)
                dve.wait_ge(wsel_mm.sem, wsel_mm.at(l, 1))
                dve.tensor_tensor(w_sel[:].rearrange("p (i k) -> p i k", k=32), ps[:, 6, 0:P].rearrange("p (i k) -> p i k", k=32),
                                  own_step[:].unsqueeze(1).broadcast_to([P, PAIRS, 32]), ALU.mult).then_inc(wsel_ready.sem, 1)
                w_in_unit(5)
                dve.wait_ge(score_s_mm.sem, score_s_mm.at(l, 1))
                dve.tensor_copy(score[:, N:N + PAST], ps[:, 7, 0:PAST])
                dve.tensor_tensor(score[:, N + PAST:N + NK], ps[:, 7, PAST:NK], other_seq[:], ALU.add).then_inc(score_s_read.sem, 1)
                dve.wait_ge(gate_mm.sem, gate_mm.at(l, 1))
                for c in range(2):
                    ins = dve.tensor_scalar(gate_low[c], ps[:, 4 + c, 0:N], params_t[:, 124 + c:125 + c], 0.0, ALU.add, ALU.min)
                ins.then_inc(gate_split.sem, 1)
                w_in_unit(6)
                for h in range(HA):
                    dve.wait_ge(idx_relu.sem, idx_relu.at(l, h + 1))
                    for t, (a, b) in enumerate(((0, P), (P, N))):
                        w = TM[:, t, TM_KI + WI_ROW + h:TM_KI + WI_ROW + h + 1]
                        if h == 0:
                            ins = dve.tensor_scalar(score[:, a:b], relu_p[:, 0, a:b], w, None, ALU.mult)
                        else:
                            ins = dve.scalar_tensor_tensor(out=score[:, a:b], in0=relu_p[:, h % 2, a:b], scalar=w,
                                                           in1=score[:, a:b], op0=ALU.mult, op1=ALU.add)
                    ins.then_inc(idx_summed.sem, 1)
                    dve.drain()
                dve.memset(score[0:CH, CH:P], NEG_MASKED)
                dve.memset(score[0:CH, P + 3 * CH:N], NEG_MASKED)
                dve.drain()

                def select_eight(r):
                    regions = ((0, P, N_SEL_P), (P, N, N_SEL_P), (N, N + NK, N_SEL_S))
                    src = score if r == 0 else left
                    live = [(n, a, b, k) for n, (a, b, k) in enumerate(regions) if 8 * r < k]
                    for n, a, b, k in live:
                        dve.max(small[:, 40 + 8 * n:48 + 8 * n], src[:, a:b])
                    dve.drain()
                    for n, a, b, k in live:
                        if k - 8 * r < 8:
                            dve.memset(small[:, 40 + 8 * n + k - 8 * r:48 + 8 * n], NEG_TAKEN)
                            dve.drain()
                    for n, a, b, k in live:
                        dve.match_replace(left[:, a:b], small[:, 40 + 8 * n:48 + 8 * n], src[:, a:b], NEG_TAKEN)
                    dve.drain()

                rounds = (N_SEL_P + 7) // 8
                for n in range(7, NU // 2):
                    w_in_unit(n)
                    if n == 7:
                        dve.wait_ge(softplus_ready.sem, softplus_ready.at(l, 1))
                        for c in range(2):
                            dve.tensor_tensor(gate_low[c], gate_low[c], cumdecay[:, c, :], ALU.subtract)
                        dve.drain()
                        for c in range(2):
                            ins = dve.tensor_tensor_scan(cumdecay[:, c, :], restart[:], gate_low[c], 0.0, ALU.mult, ALU.add)
                        ins.then_inc(cum_ready.sem, 1)
                    for r in range(2 * (n - 7), rounds if n == NU // 2 - 1 else min(rounds, 2 * (n - 6))):
                        select_eight(r)
                dve.tensor_scalar(off[:], left[:], TAKEN_BELOW, LOGIT_OFF, ALU.is_gt, ALU.mult).then_inc(off_ready.sem, 1)
                dve.drain()
                for t in range(TT):
                    dve.wait_ge(tm_tr.sem, tm_tr.at(l, 2 * t + 2))
                    dve.tensor_copy(TM[:, t, 512:1024], ps[:, (2 * t + 1) % 4, :]).then_inc(tm_dve.sem, 1)
                for h in range(HA):
                    dve.wait_ge(z_mm.sem, z_mm.at(l, h + 1))
                    dve.tensor_tensor(dsa_w[:, h, :], ps[:, 4 + h, 0:N], off[:, 0:N], ALU.add)
                dve.drain()
                dve.tensor_reduce(small[:, 8:12], dsa_w[:, :, 0:P], AX, ALU.max)
                dve.tensor_reduce(small[:, 12:16], dsa_w[:, :, P:N], AX, ALU.max)
                dve.drain()
                dve.tensor_scalar(small[:, 8:16], small[:, 8:16], -QSCALE, None, ALU.mult).then_inc(neg_max_ready.sem, 1)
                dve.wait_ge(z_mm.sem, z_mm.at(l, 5))
                dve.tensor_reduce(small[:, 16:20], ps[:, 0:PAIRS, 0:NK], AX, ALU.max)
                dve.drain()
                dve.tensor_scalar(small[:, 16:20], small[:, 16:20], -QSCALE, None, ALU.mult).then_inc(neg_max_ready.sem, 1)
                dve.wait_ge(exp_ready.sem, exp_ready.at(l, 1))
                dve.reciprocal(small[:, 24:32], small[:, 24:32])
                dve.drain()
                for t, (a, b) in enumerate(((0, P), (P, N))):
                    ins = dve.tensor_tensor(dsa_w[:, :, a:b], dsa_w[:, :, a:b],
                                            small[:, 24 + 4 * t:28 + 4 * t].unsqueeze(2).broadcast_to([P, HA, b - a]), ALU.mult)
                ins.then_inc(weights_ready.sem, 4)
                dve.wait_ge(exp_ready.sem, exp_ready.at(l, 2))
                dve.reciprocal(small[:, 32:36], small[:, 32:36])
                dve.drain()
                dve.tensor_tensor(dsa_sw[:], dsa_sw[:], small[:, 32:36].unsqueeze(2).broadcast_to([P, PAIRS, NK]),
                                  ALU.mult).then_inc(weights_ready.sem, 1)
                mix_low(0, 6)
                dve.drain()

                dve.memset(qa_bd[:], 0.0)
                dve.memset(rest[:, :, P:P + 1], 1.0)
                dve.memset(rest[:, :, N + 1:N + 2], 1.0)
                dve.memset(rest_s[:, :, NK:NK + 1], 1.0)
                dve.drain()
                block_diagonal(qa_bd, QA).then_inc(bd_ready.sem, 1)
                for h in range(HA):
                    dve.wait_ge(keep_ready.sem, keep_ready.at(l, h + 1))
                    for a in (0, 2 * P):
                        dve.tensor_tensor(keep[:, h, a:a + P], keep[:, h, a:a + P], causal[:], ALU.max)
                    dve.drain()
                    for a, b, at in ((0, P, 0), (P, N, P + 1)):
                        dve.tensor_tensor_scan(rest[:, h, at:at + b - a][:, ::-1], keep[:, h, a:b][:, ::-1], ones_row[:, 0:b - a],
                                               1.0, ALU.mult, ALU.mult)
                    dve.drain()
                    for a, b, at in ((0, P, 0), (P, N, P + 1)):
                        ins = dve.tensor_tensor(keep[:, h, a:b], rest[:, h, at + 1:at + 1 + b - a], rest[:, h, at:at + b - a], ALU.subtract)
                    ins.then_inc(weights_ready.sem, 1)
                dve.wait_ge(keep_ready.sem, keep_ready.at(l, 5))
                dve.tensor_tensor(keep_s[:, :, PAST:NK], keep_s[:, :, PAST:NK], sb_mask[:].unsqueeze(1).broadcast_to([P, PAIRS, 32]), ALU.max)
                dve.drain()
                for i in range(PAIRS):
                    dve.tensor_tensor_scan(rest_s[:, i, 0:NK][:, ::-1], keep_s[:, i, :][:, ::-1], ones_row[:, 0:NK], 1.0, ALU.mult, ALU.mult)
                dve.drain()
                dve.tensor_tensor(keep_s[:], rest_s[:, :, 1:NK + 1], rest_s[:, :, 0:NK], ALU.subtract).then_inc(weights_ready.sem, 1)
                mix_low(1, 0)

                att_v = att[:].rearrange("p t (c e n) -> p t c e n", c=2, e=2)
                for kind in range(2):
                    dve.wait_ge(att_mm.sem, att_mm.at(l, kind + 1))
                    for e in range(2):
                        if kind == 0:
                            for t in range(2):
                                dve.tensor_tensor(att_v[:, t, :, e, :], ps[:, 4 + e, 256 * t:256 * t + 256].rearrange("p (c n) -> p c n", n=P),
                                                  gla_mask[:, 0, :].unsqueeze(1).broadcast_to([P, 2, P]), ALU.mult)
                        else:
                            ins = dve.tensor_tensor(att_v[:, 2, :, e, :], ps[:, 6 + e, 0:256].rearrange("p (c n) -> p c n", n=P),
                                                    gla_mask[:, 1, :].unsqueeze(1).broadcast_to([P, 2, P]), ALU.mult)
                    if kind == 1:
                        ins.then_inc(att_ready.sem, 1)
                dve.wait_ge(kv_mm.sem, kv_mm.at(l, 1))
                for n in range(NBP):
                    for c in range(2):
                        kv = ps[:, n % 4, (n // 4 * 2 + c) * P:(n // 4 * 2 + c + 1) * P]
                        if n == 0:
                            ins = dve.tensor_copy(states[:, 0, c, :], kv)
                        else:
                            end = LP * n + LP - 1
                            ins = dve.scalar_tensor_tensor(out=states[:, n, c, :], in0=states[:, n - 1, c, :],
                                                           scalar=decay[:, c, end:end + 1], in1=kv, op0=ALU.mult, op1=ALU.add)
                    ins.then_inc(states_ready.sem, 1)
                    dve.drain()
                dve.wait_ge(kv_mm.sem, kv_mm.at(l, 2))
                for b in range(B):
                    for c in range(2):
                        end = NP + S * b + S - 1
                        ins = dve.scalar_tensor_tensor(out=gstate_new[:, b, c, :], in0=gstate[:, b, c, :],
                                                       scalar=decay[:, c, end:end + 1],
                                                       in1=ps[:, b // 2, (b % 2 * 2 + c) * P:(b % 2 * 2 + c + 1) * P],
                                                       op0=ALU.mult, op1=ALU.add)
                ins.then_inc(states_ready.sem, 1)
                split_lo(U_WOUT + 1, (U_WOUT + 1) % 2)

                def gla_low(h):
                    dve.wait_ge(gla_hi.sem, gla_hi.at(l, h + 1))
                    dve.tensor_tensor(act_lo[:, 2 + h, :], gla_out[:, h, :], act_hi[:, 2 + h, :].bitcast(F32),
                                      ALU.subtract).then_inc(gla_lo.sem, 1)

                for h in range(HB):
                    dve.wait_ge(gla_std.sem, gla_std.at(l, h + 1))
                    dve.reciprocal(gla_stds[h], gla_stds[h])
                    dve.drain()
                    dve.wait_ge(gla_gated.sem, gla_gated.at(l, h + 1))
                    dve.tensor_tensor(gla_out[:, h, :], gla_out[:, h, :], gla_stds[h], ALU.mult).then_inc(gla_f32.sem, 1)
                    if h >= 1:
                        gla_low(h - 1)
                gla_low(HB - 1)

                for u in range(U_WOUT + 2, U_F2IN):
                    split_lo(u, u % 2)
                dve.wait_ge(rows_stored.sem, rows_stored.at(l, 10))
                dve.wait_ge(states_stored.sem, states_stored.at(l, 4))
                post_norm(1)
                split_lo(U_F2IN, U_F2IN % 2)
                pre_norm(2)
                dve.wait_ge(head_tr.sem, head_tr.at(l, 1))
                dve.tensor_copy(params_t[:, P:P + 24], ps[:, 6, 0:24])
                four_hidden(U_F2IN, KF, 0, ADA_F2, 8, 64)
                dve.drain()
                fold_gain(8, 72 + KD * 5)
                with dve.Fori(0, 2) as i:
                    four_hidden(U_F2IN, KF, i * 4 + 4, i + (ADA_F2 + 1), i, i * 8 + P)
                dve.drain()
                fold_gain(1, P + 16)
                with dve.Fori(0, (KF - 12) // 2) as i:
                    for s in range(2):
                        hidden(U_F2IN, KF, i * 2 + 12, s)
                proj_out(U_F2OUT, KF // 2, ahead=False)
                post_norm(2)

            for t in range(TT):
                dve.wait_ge(yT_mm, 2 * t + 2)
                dve.tensor_copy(tok_out[:, t, 512:1024], ps[:, 2 * t + 1, :]).then_inc(y_right, 1)

        @block.tensor
        def _(pe):
            for never_zero in (unit_used, ada_used, ada_tr, params_tr, kt_tr, gate_mm):
                never_zero.credit(pe)
            pe.wait_ge(ident_ready, 1)
            pe.wait_ge(silu_c_ready, 1)
            for f in range(KD):
                m = pe.transpose(ps[:, 4, 32 * f:32 * f + 32], c_rows[:, f * P:(f + 1) * P], ident[0:32, 0:32])
            m.then_inc(cT_mm, 1)
            pe.wait_ge(head_landed.sem, head_landed.at(0, 0))
            pe.matmul(ps[:, 5, 64:88], head, ident[0:24, 0:24], start=True, stop=True).then_inc(head_tr.sem, 1)
            pe.wait_ge(x_landed, 32)
            for f in range(KD):
                if f == 4:
                    pe.wait_ge(cT_ready, 1)
                if f == 5:
                    pe.wait_ge(head_ready, 1)
                for t in range(TT):
                    m = pe.transpose(ps[:, f, t * P:(t + 1) * P], tok_in[:, t, f * P:(f + 1) * P], ident[:])
                m.then_inc(xT_mm, 1)

            def ada_quarter(l, nth, q, first=False):
                if first:
                    pe.wait_ge(first_ada_landed[q % 2], 16 * ((nth + 2) * 2 + q // 2 + 1))
                else:
                    pe.wait_ge(ada_landed[q % 2].sem, ada_landed[q % 2].at(l, nth * 2 + (q // 2 + 1)))
                if q == 0:
                    pe.wait_ge(ada_rows_ready.sem, ada_rows_ready.at(l, nth))
                for k in range(2):
                    for g in range(4):
                        m = pe.matmul(ps[32 * g:32 * g + 32, 4, 0:256], silu_cT[:, 2 * q + k, :],
                                      w_ada_sb[q % 2][:, k, 256 * g:256 * g + 256],
                                      start=(q + k == 0), stop=(q == 3 and k == 1))
                m.then_inc(ada_used.sem, 1)

            def ada_transpose(l, nth):
                pe.wait_ge(ada_rows_ready.sem, ada_rows_ready.at(l, nth + 1))
                pe.wait_ge(mod_ready.sem, mod_ready.at(l, nth))
                for j in range(2):
                    m = pe.transpose(ps[:, 5, j * P:(j + 1) * P], ada_rows[:, j * P:(j + 1) * P], ident[:])
                m.then_inc(ada_tr.sem, 1)

            pe.wait_ge(x_ready.sem, x_ready.at(0, KD))
            for nth in (-2, -1):
                for q in range(4):
                    ada_quarter(0, nth, q, first=True)
                ada_transpose(0, nth)
            pe.wait_ge(consts_ready, 1)
            pe.matmul(ps[:, 7, 384:416], spread[0:32, :], sb_mask_c[:], start=True, stop=True)
            pe.matmul(ps[:, 7, 416:448], spread[0:32, :], ident[0:32, 0:32], start=True, stop=True).then_inc(const_mm, 1)

            with pe.Fori(0, DEPTH) as l:
                def split_ready(g):
                    pe.wait_ge(lo_ready.sem, lo_ready.at(l, 1) + g)

                def three_products(out, w, wl, a, al, first, last):
                    pe.matmul(out, w, a, start=first, stop=False)
                    pe.matmul(out, w, al, start=False, stop=False)
                    return pe.matmul(out, wl, a, start=False, stop=last)

                def mean_of_x(nth):
                    for f in range(KD):
                        pe.wait_ge(x_sq_ready.sem, x_sq_ready.at(l, nth * KD + f + 1))
                        m = pe.matmul(ps[:, 0, 0:N], ones_d[:], y[:, f, :], start=(f == 0), stop=(f == KD - 1))
                    m.then_inc(mean_mm.sem, 1)

                def mean_of_y(nth):
                    pe.wait_ge(y_sq_summed.sem, y_sq_summed.at(l, (nth + 1) * (KD - 1)))
                    pe.matmul(ps[:, 0, 0:N], ones_d[:], sumsq[:], start=True, stop=True).then_inc(mean_mm.sem, 1)

                def column_tiles(bank, slot, ats, stride, nth):
                    for f in range(KD):
                        pe.wait_ge(act_ready.sem, act_ready.at(l, nth * KD + f + 1))
                        for half, at in enumerate(ats):
                            cols = slice(at + f * stride, at + f * stride + P)
                            m = three_products(ps[:, bank + half, 0:N], w_hi[slot][:, cols], w_lo[slot][:, cols],
                                               act_hi[:, f, :], act_lo[:, f, :], f == 0, f == KD - 1)
                    return m

                def hidden(u0, h0, norm, j, s):
                    split_ready(j + (u0 + s))
                    pe.wait_ge(hidden_ready.sem, hidden_ready.at(l, h0 + s - 1) + j)
                    column_tiles(2 * (s % 2), (u0 + s) % 2, (0, 1024), P, norm).then_inc(unit_used.sem, 1)

                def four_hidden(u0, h0, norm, j, nth):
                    for s in range(4):
                        ada_quarter(l, nth, s)
                        hidden(u0, h0, norm, j, s)
                    ada_transpose(l, nth)

                def proj_out(u0, units, src_hi, src_lo, h0=None):
                    def products(slot, chunk, kc, o, first, last):
                        cols = slice(kc * 1024 + o * P, kc * 1024 + o * P + P)
                        return three_products(ps[:, o:o + 1, 0:N], w_hi[slot][:, cols], w_lo[slot][:, cols],
                                              src_hi[:, bass.ds(chunk, 1), :], src_lo[:, bass.ds(chunk, 1), :], first, last)

                    split_ready(u0)
                    order = (4, 6, 7, 5, 0, 1, 2, 3) if h0 is not None else range(KD)
                    for kc in range(2):
                        for n, o in enumerate(order):
                            if kc == 0 and h0 is not None and n in (0, 4):
                                pe.wait_ge(hidden_ready.sem, hidden_ready.at(l, h0 + (KF - 2 if n == 0 else KF)))
                            if kc == 0 and h0 == 0 and o == 5:
                                pe.wait_ge(mod_ready.sem, mod_ready.at(l, ADA_LAST1 + 1))
                            m = products(u0 % 2, kc, kc, o, kc == 0, False)
                    m.then_inc(unit_used.sem, 1)
                    pairs = (units - 2) // 2
                    with pe.Fori(0, pairs) as i:
                        for s in range(2):
                            split_ready(i * 2 + (u0 + 1 + s))
                            for kc in range(2):
                                for o in range(KD):
                                    m = products((u0 + 1 + s) % 2, i * 4 + (2 + 2 * s + kc), kc, o, False, False)
                            m.then_inc(unit_used.sem, 1)
                    for u in range(1 + 2 * pairs, units - 1):
                        split_ready(u0 + u)
                        for kc in range(2):
                            for o in range(KD):
                                m = products((u0 + u) % 2, 2 * u + kc, kc, o, False, False)
                        m.then_inc(unit_used.sem, 1)
                    u = units - 1
                    split_ready(u0 + u)
                    for o in range(KD):
                        for kc in range(2):
                            m = products((u0 + u) % 2, 2 * u + kc, kc, o, False, kc == 1)
                        if o < KD - 1:
                            m.then_inc(proj_done.sem, 1)
                    m.then_inc(unit_used.sem, 1)

                pe.wait_ge(x_ready.sem, x_ready.at(l, KD))
                pe.wait_ge(params_landed.sem, params_landed.at(l, 1))
                pe.transpose(ps[:, 6, 0:P], params[:], ident[:]).then_inc(params_tr.sem, 1)
                mean_of_x(0)
                with pe.Fori(0, ADA_LAST1) as i:
                    four_hidden(U_F1IN, 0, 0, i * 4, i)
                for s in range(2):
                    ada_quarter(l, ADA_LAST1, 2 * s)
                    ada_quarter(l, ADA_LAST1, 2 * s + 1)
                    hidden(U_F1IN, 0, 0, KF - 2, s)
                ada_transpose(l, ADA_LAST1)
                proj_out(U_F1OUT, KF // 2, hid_hi, hid_lo, 0)
                mean_of_y(0)
                mean_of_x(1)

                def w_in_unit(n):
                    split_ready(U_WIN + n)
                    pe.wait_ge(u_even.sem, u_even.at(l, n - 1))
                    pe.wait_ge(u_odd.sem, u_odd.at(l, n - 1))
                    column_tiles(2 * (n % 2), (U_WIN + n) % 2, (0, P), 256, 1).then_inc(unit_used.sem, 1)

                def keys_T(phase_no):
                    pe.wait_ge(k_cache_landed.sem, k_cache_landed.at(l, 5))
                    for g in range(4):
                        if phase_no == 0:
                            bank = (6, 7, 4, 5)[g]
                        else:
                            bank = g
                        for j in range(4):
                            b = 4 * (g % 2) + j
                            if phase_no == 0:
                                src = (kc_raw, ki_raw)[g // 2][:, b, :, :].rearrange("p a d -> p (a d)")
                            else:
                                src = k_sb_raw[:, b, P * (g // 2):P * (g // 2) + P]
                            m = pe.transpose(ps[:, bank, j * P:(j + 1) * P], src, ident[:])
                        m.then_inc(kt_tr.sem, 1)

                def scores_prompt(h, q_tile, key, done):
                    rows = slice(64 * (h % 2), 64 * (h % 2) + 64)
                    c = h // 2
                    pe.matmul(ps[:, 4 + h, 0:P], U[rows, q_tile + c, 0:P], key(c)[rows, 0:P], start=True, stop=True)
                    pe.matmul(ps[:, 4 + h, P:N], U[rows, q_tile + c, P:NP], key(c)[rows, 0:NP], start=True, stop=True).then_inc(done.sem, 1)

                def scores_samples(q_bd, past, new, mask=None, first_bank=0):
                    for i in range(PAIRS):
                        bank, at = (i, 0) if mask is not None else ((first_bank, NK * i) if i < 3 else (first_bank + 1, 0))
                        if mask is not None:
                            pe.matmul(ps[:, bank, at:at + NK], spread[32 * i:32 * i + 32, :], mask[32 * i:32 * i + 32, N:N + NK],
                                      start=True, stop=False, skip_group_check=True)
                        first = mask is None
                        for b2 in range(2):
                            b = 2 * i + b2
                            for c in range(2):
                                out = ps[64 * b2 + 32 * c:64 * b2 + 32 * c + 32, bank, at:at + NK]
                                pe.matmul(out[:, 0:PAST], q_bd[:, c, b, :], past(c, b), start=first, stop=True, skip_group_check=True)
                                m = pe.matmul(out[:, PAST:NK], q_bd[:, c, b, :], new(c, i), start=first, stop=True, skip_group_check=True)
                    return m

                def attend_tail(phase_no, w, sw, wT, swT, v_prompt, v_past, v_new, per_pair):
                    for h in range(HA):
                        pe.wait_ge(weights_ready.sem, weights_ready.at(l, 5 * phase_no + h + 1))
                        for j in range(3):
                            m = pe.transpose(ps[:, 4 + h, j * P:(j + 1) * P], w[:, h, j * P:(j + 1) * P], ident[:])
                        m.then_inc(wt_tr.sem, 1)
                    pe.wait_ge(weights_ready.sem, weights_ready.at(l, 5 * phase_no + 5))
                    for i in range(PAIRS):
                        m = pe.transpose(ps[:, 2, i * P:(i + 1) * P], sw[:, i, 0:PAST], ident[:])
                    m.then_inc(wt_tr.sem, 1)
                    for i in range(PAIRS):
                        m = pe.matmul(ps[32 * i:32 * i + 32, 3, 0:P], sw[:, i, PAST:NK], ident[:], start=True, stop=True)
                    m.then_inc(wt_tr.sem, 1)
                    for c in range(2):
                        for h2 in range(2):
                            h = 2 * c + h2
                            pe.wait_ge(wt_ready.sem, wt_ready.at(l, 6 * phase_no + h + 1))
                            out = ps[64 * h2:64 * h2 + 64, c, :]
                            pe.matmul(out[:, 0:P], v_prompt(0, h), wT[:, h, 0:P], start=True, stop=True)
                            pe.matmul(out[:, P:NP], v_prompt(0, h), wT[:, h, P:2 * P], start=True, stop=False)
                            m = pe.matmul(out[:, P:NP], v_prompt(1, h), wT[:, h, 2 * P:N], start=False, stop=True)
                        m.then_inc(pv_mm.sem, 1)
                    pe.wait_ge(wt_ready.sem, wt_ready.at(l, 6 * phase_no + 6))
                    width = 32 if per_pair else 64
                    for c in range(2 if per_pair else 1):
                        new_w = snT.rearrange("p i (b2 r) -> p (i b2) r", b2=2)[:, :, width * c:width * c + width]
                        out = ps[:, 4, :].rearrange("p (b r) -> p b r", b=B)[:, :, width * c:width * c + width]
                        pe.matmul(out, v_new(c), new_w, start=(c == 0), stop=False, skip_group_check=True)
                    for b in range(B):
                        i, b2 = b // 2, b % 2
                        for c in range(2 if per_pair else 1):
                            cols = slice(64 * b2 + 32 * c, 64 * b2 + 32 * c + width)
                            out = ps[:, 4, 64 * b + 32 * c:64 * b + 32 * c + width]
                            m = pe.matmul(out, v_past(c, b), swT[:, i, cols], start=False, stop=(b == B - 1), skip_group_check=True)
                    m.then_inc(pv_mm.sem, 1)

                for n in range(3):
                    w_in_unit(n)
                pe.wait_ge(u_even.sem, u_even.at(l, 3))
                pe.wait_ge(u_odd.sem, u_odd.at(l, 3))
                for t in range(TT):
                    for j, tile in enumerate((KV, KI)):
                        at = (t % 2) * 256 + j * P
                        m = pe.transpose(ps[:, 4 + t // 2, at:at + P], U[:, tile, t * P:(t + 1) * P], ident[:])
                m.then_inc(kvi_tr.sem, 1)
                for n, tile in enumerate((KV, KI)):
                    pe.matmul(ps[:, 6 + n, 0:N], dup_eye[0:64, :], U[0:64, tile, :], start=True, stop=True).then_inc(dup_mm.sem, 1)
                w_in_unit(3)
                pe.wait_ge(kvi_ready.sem, kvi_ready.at(l, 1))
                pe.wait_ge(dup_ready.sem, dup_ready.at(l, 2))
                keys_T(0)
                w_in_unit(4)
                pe.wait_ge(kt_ready.sem, kt_ready.at(l, 4))
                pe.wait_ge(bd_ready.sem, bd_ready.at(l, 1))
                scores_samples(qi_bd, lambda c, b: kiT[:, b, :], lambda c, i: ki_dup[:, NP + 32 * i:NP + 32 * i + 32],
                               first_bank=4).then_inc(idx_s_mm.sem, 1)
                pe.matmul(ps[:, 6, 0:P], head_rows[WI_ROW:WI_ROW + 4, :], U[WI_ROW:WI_ROW + 4, KI, NP:N], start=True, stop=True).then_inc(wsel_mm.sem, 1)
                w_in_unit(5)
                pe.wait_ge(wsel_ready.sem, wsel_ready.at(l, 1))
                pe.wait_ge(idx_s_relu.sem, idx_s_relu.at(l, 1))
                for i in range(PAIRS):
                    m = pe.matmul(ps[32 * i:32 * i + 32, 7, 0:NK], w_sel[:, 32 * i:32 * i + 32], relu_s[:, i, :], start=True, stop=True)
                m.then_inc(score_s_mm.sem, 1)
                for c in range(2):
                    m = pe.matmul(ps[:, 4 + c, 0:N], w_gate_sb[GB_ROW:GB_ROW + RANK, c * P:(c + 1) * P], U[GB_ROW:GB_ROW + RANK, KI, :],
                                  start=True, stop=True)
                m.then_inc(gate_mm.sem, 1)
                w_in_unit(6)
                pe.wait_ge(softplus_ready.sem, softplus_ready.at(l, 1))
                pe.wait_ge(score_s_read.sem, score_s_read.at(l, 1))
                for h in range(HA):
                    scores_prompt(h, QI, lambda c: ki_dup, idx_mm)
                for n in range(7, NU // 2 - 1):
                    w_in_unit(n)
                pe.wait_ge(idx_relu.sem, idx_relu.at(l, HA))
                for h in range(HA):
                    scores_prompt(h, QC, lambda c: kc_dup, z_mm)
                w_in_unit(NU // 2 - 1)

                pe.wait_ge(u_even.sem, u_even.at(l, NU // 2))
                pe.wait_ge(u_odd.sem, u_odd.at(l, NU // 2))
                for n in range(2 * TT):
                    t, g = n // 2, n % 2
                    if n >= 4:
                        copied = (tm_act, tm_dve)[n % 2]
                        pe.wait_ge(copied.sem, copied.at(l, 1))
                    for j, tile in enumerate(TM_TILES[4 * g:4 * g + 4]):
                        m = pe.transpose(ps[:, n % 4, j * P:(j + 1) * P], U[:, tile, t * P:(t + 1) * P], ident[:])
                    m.then_inc(tm_tr.sem, 1)

                pe.wait_ge(tm_act.sem, tm_act.at(l, TT))
                pe.wait_ge(tm_dve.sem, tm_dve.at(l, TT))
                pe.wait_ge(off_ready.sem, off_ready.at(l, 1))
                scores_samples(qc_bd, lambda c, b: kcT[:, b, :], lambda c, i: kc_dup[:, NP + 32 * i:NP + 32 * i + 32], off).then_inc(z_mm.sem, 1)
                pe.wait_ge(v_cache_landed[0].sem, v_cache_landed[0].at(l, 2))
                attend_tail(0, dsa_w, dsa_sw, dsa_wT, dsa_swT,
                            lambda t, h: TM[:, t, TM_KV + 64:TM_KV + 128],
                            lambda c, b: vc_past[:, b, :, :].rearrange("p a d -> p (a d)"),
                            lambda c: vc_new[:].rearrange("p a d -> p (a d)"), False)

                pe.wait_ge(mix_lo.sem, mix_lo.at(l, 3))
                keys_T(1)
                pe.wait_ge(kt_ready.sem, kt_ready.at(l, 8))
                for h in range(HA):
                    scores_prompt(h, QA, lambda c: U[:, KA + c, :], z_mm)
                pe.wait_ge(bd_ready.sem, bd_ready.at(l, 2))
                scores_samples(qa_bd, lambda c, b: kaT[:, c, b, :], lambda c, i: U[:, KA + c, NP + 32 * i:NP + 32 * i + 32]).then_inc(z_mm.sem, 1)
                pe.wait_ge(v_cache_landed[1].sem, v_cache_landed[1].at(l, 1))
                attend_tail(1, keep, keep_s, sb_wT, sb_swT,
                            lambda t, h: TM[:, t, TM_VA + 64 * h:TM_VA + 64 * h + 64],
                            lambda c, b: va_past[:, b, P * c:P * c + P],
                            lambda c: TM[:, 2, TM_VA + P * c:TM_VA + P * c + P], True)

                pe.wait_ge(mix_lo.sem, mix_lo.at(l, 6))
                pe.wait_ge(k_out_ready.sem, k_out_ready.at(l, 1))
                for t in range(TT):
                    for c in range(2):
                        m = pe.transpose(ps[:, 2 + t // 2, (t % 2 * 2 + c) * P:(t % 2 * 2 + c + 1) * P], k_out[:, c, t * P:(t + 1) * P], ident[:])
                m.then_inc(krow_tr.sem, 1)
                pe.wait_ge(qk_ready.sem, qk_ready.at(l, 1))
                for kind, tiles in enumerate(((0, 1), (2,))):
                    for t in tiles:
                        for h in range(HB):
                            e, c = h % 2, h // 2
                            rows = slice(64 * e, 64 * e + 64)
                            at = (t % 2 * 2 + c) * P
                            m = pe.matmul(ps[:, 4 + 2 * kind + e, at:at + P], k_in[rows, c, t * P:(t + 1) * P], q_in[rows, c, t * P:(t + 1) * P],
                                          start=True, stop=True)
                    m.then_inc(att_mm.sem, 1)
                pe.wait_ge(krow_ready.sem, krow_ready.at(l, 1))
                for half in range(NBP // 4):
                    for c in range(2):
                        for e in range(2):
                            for g in range(4):
                                rows = slice(LP * g, LP * g + LP)
                                at = (half * 2 + c) * P
                                m = pe.matmul(ps[64 * e:64 * e + 64, g, at:at + P], k_rows[rows, half, P * c + 64 * e:P * c + 64 * e + 64],
                                              TM[rows, half, TM_VB + (2 * c + e) * P:TM_VB + (2 * c + e + 1) * P], start=True, stop=True)
                m.then_inc(kv_mm.sem, 1)
                pe.wait_ge(att_ready.sem, att_ready.at(l, 1))
                pe.wait_ge(gstate_landed.sem, gstate_landed.at(l, 2))
                pe.wait_ge(q_dec_ready.sem, q_dec_ready.at(l, 1))
                for c in range(2):
                    for t in range(TT):
                        for e in range(2):
                            h = 2 * c + e
                            prompt, sample = gla_banks(h)
                            out = prompt[:, t * P:(t + 1) * P] if t < 2 else sample
                            pe.matmul(out, TM[:, t, TM_VB + h * P:TM_VB + (h + 1) * P],
                                      att[:, t, h * P:(h + 1) * P], start=(t != 1 and e == 0), stop=False, skip_group_check=True)
                    for b in range(B):
                        out = ps[:, 5 + 2 * c, 0:2 * NS].rearrange("p (e n) -> p e n", e=2)[:, :, S * b:S * b + S]
                        pe.matmul(out, gstate[:, b, c, :], q_dec[:, c, :, NP + S * b:NP + S * b + S],
                                  start=False, stop=(b == B - 1), skip_group_check=True)
                pe.wait_ge(states_ready.sem, states_ready.at(l, NBP))
                for b2 in range(2):
                    for c in range(2):
                        for e in range(2):
                            for g in range(PAIRS):
                                rows = slice(32 * g, 32 * g + 32)
                                at = (b2 * 2 + c) * P
                                m = pe.matmul(ps[64 * e:64 * e + 64, g, at:at + P], k_rows[rows, 2 + b2, P * c + 64 * e:P * c + 64 * e + 64],
                                              TM[rows, 2, TM_VB + (2 * c + e) * P:TM_VB + (2 * c + e + 1) * P], start=True, stop=True)
                m.then_inc(kv_mm.sem, 1)
                for c in range(2):
                    for n in range(1, NBP):
                        out = ps[:, 4 + 2 * c, :].rearrange("p (e n) -> p e n", e=2)[:, :, LP * n:LP * n + LP]
                        m = pe.matmul(out, states[:, n - 1, c, :], q_dec[:, c, :, LP * n:LP * n + LP],
                                      start=False, stop=(n == NBP - 1), skip_group_check=True)
                    m.then_inc(gla_mm.sem, 2)
                pe.wait_ge(states_ready.sem, states_ready.at(l, NBP + 1))
                for h in range(HB):
                    pe.wait_ge(gla_sq.sem, gla_sq.at(l, h + 1))
                    pe.matmul(ps[:, h, 0:N], ones_v[:], gla_sqs[h], start=True, stop=True).then_inc(gla_mean_mm.sem, 1)

                pe.wait_ge(gla_std.sem, gla_std.at(l, HB))
                for u, chunk in enumerate(WOUT_CHUNKS):
                    split_ready(U_WOUT + u)
                    slot = (U_WOUT + u) % 2
                    if chunk in (2, 4):
                        pe.wait_ge(gla_lo.sem, gla_lo.at(l, chunk))
                    last = u == KD // 2 - 1
                    for a, b in ((a, b) for a in range(KD if last else 2) for b in range(2 if last else KD)):
                        kc, o = (b, a) if last else (a, b)
                        cols = slice(kc * 1024 + o * P, kc * 1024 + o * P + P)
                        m = three_products(ps[:, o, 0:N], w_hi[slot][:, cols], w_lo[slot][:, cols],
                                           act_hi[:, chunk + kc, :], act_lo[:, chunk + kc, :], u == 0 and kc == 0, last and kc == 1)
                        if last and kc == 1 and o < KD - 1:
                            m.then_inc(proj_done.sem, 1)
                    m.then_inc(unit_used.sem, 1)
                mean_of_y(1)
                mean_of_x(2)
                pe.wait_ge(head_landed.sem, head_landed.at(l, 1))
                pe.matmul(ps[:, 6, 0:24], head, ident[0:24, 0:24], start=True, stop=True).then_inc(head_tr.sem, 1)
                four_hidden(U_F2IN, KF, 2, 0, ADA_F2)
                with pe.Fori(0, 2) as i:
                    four_hidden(U_F2IN, KF, 2, i * 4 + 4, i + (ADA_F2 + 1))
                with pe.Fori(0, (KF - 12) // 2) as i:
                    for s in range(2):
                        hidden(U_F2IN, KF, 2, i * 2 + 12, s)
                proj_out(U_F2OUT, KF // 2, hid_hi, hid_lo, KF)
                mean_of_y(2)

            for t in range(TT):
                if t == 0:
                    pe.wait_ge(x_ready.sem, x_ready.at(DEPTH, KD))
                for f in range(KD):
                    m = pe.transpose(ps[:, 2 * t + f // 4, (f % 4) * P:(f % 4 + 1) * P], x[:, f, t * P:(t + 1) * P], ident[:])
                    if f % 4 == 3:
                        m.then_inc(yT_mm, 1)


_INS = ['x_prompt', 'x_sample', 'cache_k_sb', 'cache_v_sb', 'cache_k_dsa', 'cache_v_dsa', 'cache_k_idx', 'state_gla',
        'c_prompt', 'c_sample', 'w_ada', 'b_ada', 'norm_gains', 'w_ffn1_in', 'w_ffn1_out', 'w_ffn2_in', 'w_ffn2_out',
        'w_in', 'w_gla_gate', 'b_gla_gate', 'gla_norm', 'w_out']
_OUTS = [('y_prompt', (1, 256, 1024)), ('y_sample', (8, 16, 1024)),
         ('new_k_sb_p', (2, 1, 256, 4, 64)), ('new_v_sb_p', (2, 1, 256, 4, 64)),
         ('new_k_dsa_p', (2, 1, 256, 64)), ('new_v_dsa_p', (2, 1, 256, 64)), ('new_k_idx_p', (2, 1, 256, 64)),
         ('new_gla_p', (2, 1, 4, 64, 128)),
         ('new_k_sb_s', (2, 8, 16, 4, 64)), ('new_v_sb_s', (2, 8, 16, 4, 64)),
         ('new_k_dsa_s', (2, 8, 16, 64)), ('new_v_dsa_s', (2, 8, 16, 64)), ('new_k_idx_s', (2, 8, 16, 64)),
         ('new_gla_s', (2, 8, 4, 64, 128))]


def kernel(**inputs):
    import numpy as _np
    import concourse.bacc as _bacc
    from concourse import mybir as _mybir
    from concourse.bass_utils import run_bass_kernel_spmd as _run

    nc = _bacc.Bacc("TRN2", target_bir_lowering=False, num_devices=1)
    arrays, tensors = {}, {}
    for name in _INS:
        a = _np.ascontiguousarray(inputs[name])
        arrays[f"in_{name}_dram"] = a
        tensors[name] = nc.dram_tensor(f"in_{name}_dram", a.shape, _mybir.dt.from_np(a.dtype), kind="ExternalInput").ap()
    for name, shape in _OUTS:
        tensors[name] = nc.dram_tensor(f"out_{name}_dram", shape, _mybir.dt.float32, kind="ExternalOutput").ap()
    encoder_program(nc, tensors)
    r = _run(nc, [arrays], core_ids=[0])
    return tuple(r.results[0][f"out_{name}_dram"] for name, _ in _OUTS)
```
